# Optimizing a Trainium2 kernel written in Bass

```python
import jax, jax.numpy as jnp
from jax import lax
import numpy as np

D_MODEL = 1024
BATCH = 1
SEQ = 512
DEPTH = 1

CHUNK = 64
HEAD_DIM = 64
N_HEADS_SB = 4
N_HEADS_CH = 8
CONV_CH = 256
CONV_WIDTH = 3
N_PREV_CHUNKS = 8
BAND = (N_PREV_CHUNKS + 1) * CHUNK
REL_CLIP = 128
Q_BLOCK = 128
D_SB = N_HEADS_SB * HEAD_DIM
D_CH = N_HEADS_CH * HEAD_DIM
D_MIX = D_SB + D_CH + CONV_CH
D_IN = 3 * D_SB + 3 * D_CH + 3 * CONV_CH
N_OUT_GROUPS = D_MIX // HEAD_DIM
D_FF = ((8 * D_MODEL // 3 + 255) // 256) * 256
EPS = 1e-6


def rmsnorm(x, w):
    xf = x.astype(jnp.float32)
    y = xf * lax.rsqrt(jnp.mean(xf * xf, axis=-1, keepdims=True) + EPS)
    return (y * w.astype(jnp.float32)).astype(x.dtype)

def group_rmsnorm(y, w):
    b, s, _ = y.shape
    yg = y.astype(jnp.float32).reshape(b, s, N_OUT_GROUPS, HEAD_DIM)
    yg = yg * lax.rsqrt(jnp.mean(yg * yg, axis=-1, keepdims=True) + EPS)
    return (yg.reshape(b, s, D_MIX) * w.astype(jnp.float32)).astype(y.dtype)

def to_heads(t):
    b, s, _ = t.shape
    return t.reshape(b, s, -1, HEAD_DIM).transpose(0, 2, 1, 3)

def from_heads(t):
    b, h, s, d = t.shape
    return t.transpose(0, 2, 1, 3).reshape(b, s, h * d)

def stick_breaking_attention(q, k, v):
    b, h, s, d = q.shape
    n = s // Q_BLOCK
    qb = (q.astype(jnp.float32) * (d ** -0.5)).reshape(b, h, n, Q_BLOCK, d)
    kb = k.astype(jnp.float32).reshape(b, h, n, Q_BLOCK, d)
    vb = v.astype(jnp.float32).reshape(b, h, n, Q_BLOCK, d)
    idx = jnp.arange(Q_BLOCK)
    after_mat = (idx[:, None] > idx[None, :]).astype(jnp.float32)
    diag_mask = idx[None, :] < idx[:, None]
    out = jnp.zeros((b, h, n, Q_BLOCK, d), jnp.float32)
    carry = jnp.zeros((b, h, n, Q_BLOCK), jnp.float32)
    for o in range(n):
        z = jnp.einsum('bhnqd,bhnkd->bhnqk', qb[:, :, o:], kb[:, :, :n - o])
        log_rest = jax.nn.log_sigmoid(-z)
        if o == 0:
            log_rest = jnp.where(diag_mask, log_rest, 0.0)
        after = jnp.einsum('bhnqj,js->bhnqs', log_rest, after_mat) + carry[:, :, o:, :, None]
        w = jnp.exp(jax.nn.log_sigmoid(z) + after)
        if o == 0:
            w = jnp.where(diag_mask, w, 0.0)
        out = out.at[:, :, o:].add(jnp.einsum('bhnqk,bhnkd->bhnqd', w, vb[:, :, :n - o]))
        carry = carry.at[:, :, o:].add(jnp.sum(log_rest, axis=-1))
    return out.reshape(b, h, s, d).astype(v.dtype)

def chunked_relpos_attention(q, k, v, rel_bias):
    b, h, s, d = q.shape
    nc = s // CHUNK
    pad = N_PREV_CHUNKS * CHUNK
    qc = (q.astype(jnp.float32) * (d ** -0.5)).reshape(b, h, nc, CHUNK, d)
    kpad = jnp.pad(k, ((0, 0), (0, 0), (pad, 0), (0, 0))).reshape(b, h, nc + N_PREV_CHUNKS, CHUNK, d)
    vpad = jnp.pad(v, ((0, 0), (0, 0), (pad, 0), (0, 0))).reshape(b, h, nc + N_PREV_CHUNKS, CHUNK, d)
    band_idx = jnp.arange(nc)[:, None] + jnp.arange(N_PREV_CHUNKS + 1)[None, :]
    kb = kpad[:, :, band_idx].reshape(b, h, nc, BAND, d).astype(jnp.float32)
    vb = vpad[:, :, band_idx].reshape(b, h, nc, BAND, d).astype(jnp.float32)
    scores = jnp.einsum('bhcqd,bhckd->bhcqk', qc, kb)
    p = jnp.arange(CHUNK)[:, None]
    m = jnp.arange(BAND)[None, :]
    rel = jnp.clip(N_PREV_CHUNKS * CHUNK + p - m, -REL_CLIP, REL_CLIP) + REL_CLIP
    bias = rel_bias.astype(jnp.float32)[:, rel]
    valid = jnp.repeat(band_idx >= N_PREV_CHUNKS, CHUNK, axis=1)
    scores = jnp.where(valid[None, None, :, None, :], scores + bias[None, :, None], -jnp.inf)
    probs = jax.nn.softmax(scores, axis=-1)
    out = jnp.einsum('bhcqk,bhckd->bhcqd', probs, vb)
    return out.reshape(b, h, s, d).astype(v.dtype)

def short_conv_mixer(gate_b, gate_c, xc, conv_w):
    hc = gate_c * xc
    y = lax.conv_general_dilated(
        hc, conv_w[:, None, :].astype(hc.dtype), window_strides=(1,),
        padding=[(CONV_WIDTH - 1, 0)], dimension_numbers=('NWC', 'WIO', 'NWC'),
        feature_group_count=CONV_CH)
    return gate_b * y

def swiglu(x, w_gate, w_up, w_down):
    return (jax.nn.silu(x @ w_gate) * (x @ w_up)) @ w_down

def first_inputs(seed: int = 0) -> dict:
    key = jax.random.key(seed)
    ks = jax.random.split(key, 14)
    f32 = jnp.float32

    def gain(k, n):
        return 1.0 + 0.02 * jax.random.normal(k, (DEPTH, n), f32)

    return {
        "x": jax.random.normal(ks[0], (BATCH, SEQ, D_MODEL), f32),
        "attn_norm_w": gain(ks[1], D_MODEL),
        "w_in": jax.random.normal(ks[2], (DEPTH, D_MODEL, D_IN), f32) * D_MODEL ** -0.5,
        "q_norm_w": gain(ks[3], HEAD_DIM),
        "k_norm_w": gain(ks[4], HEAD_DIM),
        "rel_bias": 0.1 * jax.random.normal(ks[5], (DEPTH, N_HEADS_CH, 2 * REL_CLIP + 1), f32),
        "conv_w": jax.random.normal(ks[6], (DEPTH, CONV_WIDTH, CONV_CH), f32) * CONV_WIDTH ** -0.5,
        "out_norm_w": gain(ks[7], D_MIX),
        "w_out": jax.random.normal(ks[8], (DEPTH, D_MIX, D_MODEL), f32) * D_MIX ** -0.5,
        "ffn_norm_w": gain(ks[9], D_MODEL),
        "w_gate": jax.random.normal(ks[10], (DEPTH, D_MODEL, D_FF), f32) * D_MODEL ** -0.5,
        "w_up": jax.random.normal(ks[11], (DEPTH, D_MODEL, D_FF), f32) * D_MODEL ** -0.5,
        "w_down": jax.random.normal(ks[12], (DEPTH, D_FF, D_MODEL), f32) * D_FF ** -0.5,
    }

def first_block(x, attn_norm_w, w_in, q_norm_w, k_norm_w, rel_bias, conv_w, out_norm_w,
              w_out, ffn_norm_w, w_gate, w_up, w_down):
    widths = [D_SB] * 3 + [D_CH] * 3 + [CONV_CH] * 3
    split_points = [int(v) for v in np.cumsum(widths)[:-1]]
    for l in range(DEPTH):
        h = rmsnorm(x, attn_norm_w[l])
        proj = h @ w_in[l]
        (q_a, k_a, v_a, q_b, k_b, v_b, g_b, g_c, x_c) = jnp.split(proj, split_points, axis=-1)
        y_sb = from_heads(stick_breaking_attention(to_heads(q_a), to_heads(k_a), to_heads(v_a)))
        qh = rmsnorm(to_heads(q_b), q_norm_w[l])
        kh = rmsnorm(to_heads(k_b), k_norm_w[l])
        y_ch = from_heads(chunked_relpos_attention(qh, kh, to_heads(v_b), rel_bias[l]))
        y_cv = short_conv_mixer(g_b, g_c, x_c, conv_w[l])
        y = group_rmsnorm(jnp.concatenate([y_sb, y_ch, y_cv], axis=-1), out_norm_w[l])
        x = x + y @ w_out[l]
        x = x + swiglu(rmsnorm(x, ffn_norm_w[l]), w_gate[l], w_up[l], w_down[l])
    return x


CONV_CH_2 = D_MODEL
CONV_WIDTH_2 = 31
N_Q_HEADS = 16
N_KV_HEADS = 2
GROUP = N_Q_HEADS // N_KV_HEADS
ATTN_W = N_Q_HEADS * HEAD_DIM
KV_W = N_KV_HEADS * HEAD_DIM
WINDOW = 128
BLOCK = 128
ROPE_THETA = 10000.0
PEER_HEADS = 8
N_KEYS = 128
N_EXPERTS = N_KEYS * N_KEYS
PEER_DKEY = 256
PEER_DHALF = PEER_DKEY // 2
PEER_TOPK = 16
PEER_CHUNK = 128
IN_COLS = 2 * CONV_CH_2 + ATTN_W + 2 * KV_W + 2 * D_MODEL
NEG = -1e30


def rmsnorm_2(x, g):
    xf = x.astype(jnp.float32)
    y = xf * lax.rsqrt(jnp.mean(xf * xf, axis=-1, keepdims=True) + EPS)
    return (y * g.astype(jnp.float32)).astype(x.dtype)

def layernorm(x, g, b):
    xf = x.astype(jnp.float32)
    mu = jnp.mean(xf, axis=-1, keepdims=True)
    xc = xf - mu
    y = xc * lax.rsqrt(jnp.mean(xc * xc, axis=-1, keepdims=True) + EPS)
    return (y * g.astype(jnp.float32) + b.astype(jnp.float32)).astype(x.dtype)

def rope(t, positions):
    half = HEAD_DIM // 2
    inv = ROPE_THETA ** (-(jnp.arange(half, dtype=jnp.float32) * 2.0 / HEAD_DIM))
    ang = positions.astype(jnp.float32)[..., None] * inv
    cos = jnp.cos(ang)[:, :, None, :]
    sin = jnp.sin(ang)[:, :, None, :]
    tf = t.astype(jnp.float32)
    t1, t2 = tf[..., :half], tf[..., half:]
    out = jnp.concatenate([t1 * cos - t2 * sin, t2 * cos + t1 * sin], axis=-1)
    return out.astype(t.dtype)

def conformer_conv(val, gate, conv_w, conv_b, ln_g, ln_b, w_conv_out):
    u = val * jax.nn.sigmoid(gate)
    up = jnp.pad(u, ((0, 0), (CONV_WIDTH_2 - 1, 0), (0, 0)))
    y = lax.conv_general_dilated(
        up, conv_w[:, None, :], window_strides=(1,), padding="VALID",
        dimension_numbers=("NWC", "WIO", "NWC"), feature_group_count=CONV_CH_2) + conv_b
    y = jax.nn.silu(layernorm(y, ln_g, ln_b))
    return y @ w_conv_out

def swa_sink_attention(q, k, v, sinks):
    B, S = q.shape[0], q.shape[1]
    nb = S // BLOCK
    qb = q.reshape(B, nb, BLOCK, N_KV_HEADS, GROUP, HEAD_DIM)

    def band(t):
        tp = jnp.pad(t, ((0, 0), (BLOCK, 0), (0, 0), (0, 0)))
        tb = tp.reshape(B, nb + 1, BLOCK, N_KV_HEADS, HEAD_DIM)
        return jnp.concatenate([tb[:, :-1], tb[:, 1:]], axis=2)

    kb, vb = band(k), band(v)
    s = jnp.einsum("bnqhgd,bnkhd->bnhgqk", qb, kb,
                   preferred_element_type=jnp.float32) * (HEAD_DIM ** -0.5)
    qi = jnp.arange(BLOCK)[:, None]
    kj = jnp.arange(2 * BLOCK)[None, :]
    rel = qi + BLOCK - kj
    in_window = (rel >= 0) & (rel < WINDOW)
    not_pad = (kj >= BLOCK)[None] | (jnp.arange(nb)[:, None, None] > 0)
    mask = in_window[None] & not_pad
    s = jnp.where(mask[None, :, None, None], s, NEG)
    sk = sinks.astype(jnp.float32).reshape(N_KV_HEADS, GROUP)[:, :, None, None]
    m = jnp.maximum(jnp.max(s, axis=-1, keepdims=True), sk)
    e = jnp.exp(s - m)
    p = e / (jnp.sum(e, axis=-1, keepdims=True) + jnp.exp(sk - m))
    o = jnp.einsum("bnhgqk,bnkhd->bnqhgd", p.astype(v.dtype), vb)
    return o.reshape(B, S, ATTN_W)

def peer(h, w_pq, sub_keys, u_emb, v_emb):
    B, S, D = h.shape
    q = (h @ w_pq).reshape(B, S, PEER_HEADS, 2, PEER_DHALF)
    sc = jnp.einsum("bshcd,hcnd->bshcn", q, sub_keys,
                    preferred_element_type=jnp.float32)
    s_top, i_top = lax.top_k(sc, PEER_TOPK)
    cand = s_top[..., 0, :, None] + s_top[..., 1, None, :]
    cand_idx = i_top[..., 0, :, None] * N_KEYS + i_top[..., 1, None, :]
    cand = cand.reshape(B, S, PEER_HEADS, PEER_TOPK * PEER_TOPK)
    cand_idx = cand_idx.reshape(B, S, PEER_HEADS, PEER_TOPK * PEER_TOPK)
    best, pos = lax.top_k(cand, PEER_TOPK)
    expert_idx = jnp.take_along_axis(cand_idx, pos, axis=-1)
    gate = jax.nn.softmax(best, axis=-1).astype(h.dtype)

    n_chunks = (B * S) // PEER_CHUNK
    hc = h.reshape(n_chunks, PEER_CHUNK, D)
    ic = expert_idx.reshape(n_chunks, PEER_CHUNK, PEER_HEADS * PEER_TOPK)
    gc = gate.reshape(n_chunks, PEER_CHUNK, PEER_HEADS * PEER_TOPK)

    def chunk(args):
        hx, idx, g = args
        a = jax.nn.gelu(jnp.einsum("ced,cd->ce", u_emb[idx], hx), approximate=False)
        return jnp.einsum("ce,ced->cd", g * a, v_emb[idx])

    out = lax.map(chunk, (hc, ic, gc))
    return out.reshape(B, S, D)

def second_inputs(seed: int = 0) -> dict:
    key = jax.random.key(seed)
    ks = jax.random.split(key, 20)
    f32 = jnp.float32
    nrm = lambda k, shape, scale: jax.random.normal(k, shape, f32) * scale
    L = DEPTH
    return {
        "x": nrm(ks[0], (BATCH, SEQ, D_MODEL), 1.0),
        "positions": jnp.broadcast_to(jnp.arange(SEQ, dtype=jnp.int32)[None, :], (BATCH, SEQ)),
        "norm1_g": 1.0 + nrm(ks[1], (L, D_MODEL), 0.02),
        "w_in": nrm(ks[2], (L, D_MODEL, IN_COLS), D_MODEL ** -0.5),
        "b_in": nrm(ks[3], (L, IN_COLS), 0.01),
        "conv_w": nrm(ks[4], (L, CONV_WIDTH_2, CONV_CH_2), CONV_WIDTH_2 ** -0.5),
        "conv_b": nrm(ks[5], (L, CONV_CH_2), 0.01),
        "conv_ln_g": 1.0 + nrm(ks[6], (L, CONV_CH_2), 0.02),
        "conv_ln_b": nrm(ks[7], (L, CONV_CH_2), 0.01),
        "w_conv_out": nrm(ks[8], (L, CONV_CH_2, D_MODEL), CONV_CH_2 ** -0.5),
        "attn_sinks": nrm(ks[9], (L, N_Q_HEADS), 0.5),
        "w_attn_o": nrm(ks[10], (L, ATTN_W, D_MODEL), ATTN_W ** -0.5),
        "w_out": nrm(ks[11], (L, D_MODEL, D_MODEL), D_MODEL ** -0.5),
        "norm2_g": 1.0 + nrm(ks[12], (L, D_MODEL), 0.02),
        "w_peer_q": nrm(ks[13], (L, D_MODEL, PEER_HEADS * PEER_DKEY), D_MODEL ** -0.5),
        "peer_sub_keys": nrm(ks[14], (L, PEER_HEADS, 2, N_KEYS, PEER_DHALF), PEER_DHALF ** -0.5),
        "peer_u": nrm(ks[15], (L, N_EXPERTS, D_MODEL), D_MODEL ** -0.5),
        "peer_v": nrm(ks[16], (L, N_EXPERTS, D_MODEL), (PEER_HEADS * PEER_TOPK) ** -0.5),
        "final_g": 1.0 + nrm(ks[17], (D_MODEL,), 0.02),
    }

def second_block(x, positions, norm1_g, w_in, b_in, conv_w, conv_b, conv_ln_g, conv_ln_b,
              w_conv_out, attn_sinks, w_attn_o, w_out, norm2_g, w_peer_q, peer_sub_keys,
              peer_u, peer_v, final_g):
    B, S, _ = x.shape
    c0 = CONV_CH_2
    c1 = c0 + CONV_CH_2
    c2 = c1 + ATTN_W
    c3 = c2 + KV_W
    c4 = c3 + KV_W
    c5 = c4 + D_MODEL
    for l in range(DEPTH):
        h = rmsnorm_2(x, norm1_g[l])
        z = h @ w_in[l] + b_in[l]
        glu_val, glu_gate, q, k, v, g_conv, g_attn = jnp.split(z, [c0, c1, c2, c3, c4, c5], axis=-1)

        conv_out = conformer_conv(glu_val, glu_gate, conv_w[l], conv_b[l],
                                  conv_ln_g[l], conv_ln_b[l], w_conv_out[l])

        q = rope(q.reshape(B, S, N_Q_HEADS, HEAD_DIM), positions)
        k = rope(k.reshape(B, S, N_KV_HEADS, HEAD_DIM), positions)
        v = v.reshape(B, S, N_KV_HEADS, HEAD_DIM)
        attn_out = swa_sink_attention(q, k, v, attn_sinks[l]) @ w_attn_o[l]

        merged = jax.nn.sigmoid(g_conv) * conv_out + jax.nn.sigmoid(g_attn) * attn_out
        x = x + merged @ w_out[l]

        h2 = rmsnorm_2(x, norm2_g[l])
        x = x + peer(h2, w_peer_q[l], peer_sub_keys[l], peer_u[l], peer_v[l])
    return rmsnorm_2(x, final_g)


def setup_inputs(seed=0):
    out = dict(first_inputs(seed))
    for name, value in second_inputs(seed + 1).items():
        if name != "x":
            out[name + "_2"] = value
    return out


def reference(
    x, attn_norm_w, w_in, q_norm_w, k_norm_w, rel_bias, conv_w, out_norm_w, w_out, ffn_norm_w,
    w_gate, w_up, w_down, positions_2, norm1_g_2, w_in_2, b_in_2, conv_w_2, conv_b_2,
    conv_ln_g_2, conv_ln_b_2, w_conv_out_2, attn_sinks_2, w_attn_o_2, w_out_2, norm2_g_2,
    w_peer_q_2, peer_sub_keys_2, peer_u_2, peer_v_2, final_g_2,
):
    x = first_block(
        x, attn_norm_w, w_in, q_norm_w, k_norm_w, rel_bias, conv_w, out_norm_w, w_out,
        ffn_norm_w, w_gate, w_up, w_down,
    )
    return second_block(
        x, positions_2, norm1_g_2, w_in_2, b_in_2, conv_w_2, conv_b_2, conv_ln_g_2, conv_ln_b_2,
        w_conv_out_2, attn_sinks_2, w_attn_o_2, w_out_2, norm2_g_2, w_peer_q_2, peer_sub_keys_2,
        peer_u_2, peer_v_2, final_g_2,
    )


_drawn_inputs = setup_inputs


def setup_inputs(seed=0):
    import zlib

    import numpy as np

    out = dict(_drawn_inputs(seed))
    spreads = {}
    factors = {'q_norm_w': 4.404,
     'k_norm_w': 5.506,
     'out_norm_w': 3.567,
     'ffn_norm_w': 4.873,
     'norm1_g_2': 8.0,
     'b_in_2': 8.0,
     'conv_b_2': 64.0,
     'conv_ln_g_2': 64.0,
     'conv_ln_b_2': 64.0,
     'attn_sinks_2': 200.0,
     'norm2_g_2': 64.0,
     'final_g_2': 23.037}
    for name, (base, spread) in spreads.items():
        noise = np.random.default_rng([zlib.crc32(name.encode()), seed]).standard_normal(out[name].shape)
        drawn = base * np.exp(spread * noise) if base else spread * noise
        out[name] = __import__('jax').numpy.asarray(drawn.astype(out[name].dtype))
    for name, factor in factors.items():
        out[name] = (out[name] * factor).astype(out[name].dtype)
    return out
```

```python
from contextlib import ExitStack

import concourse.bass as bass
import numpy as np
from concourse import mybir

F32 = mybir.dt.float32
F32R = mybir.dt.float32r
I32 = mybir.dt.int32
U32 = mybir.dt.uint32
ALU = mybir.AluOpType
ACT = mybir.ActivationFunctionType
AX_X = mybir.AxisListType.X

P = 128
S = 512
D = 1024
KD = D // P
NT = S // P
EPS = 1e-6
HD = 64
SCALE = HD ** -0.5
NEG = -1e30

SB_PAIRS, CH_PAIRS, CV_TILES = 2, 4, 2
QA, KA, VA = 0, 2, 4
QB, KB, VB = 6, 10, 14
GB, GC, XC = 18, 20, 22
Z1_TILES = 24
FF_TILES = 22

VAL, GATE, Q2, K2, V2, GCONV, GATTN = 0, 8, 16, 24, 25, 26, 34
Z2_TILES = 42
TAPS = 31
SWA_PAIRS = 8
PAIRS_PER_KV = 4

PH = 8
HC = 2 * PH
NKEYS = 128
TOPK = 16
GROUPS = 2
EG = NKEYS // GROUPS
TB = 8

SLOTS = [("in1", Z1_TILES // 2), ("out1", 4), ("ffn", FF_TILES), ("down", FF_TILES // 2),
         ("in2", Z2_TILES // 2), ("co", 4), ("ao", 4), ("out2", 4), ("pq", 8)]
FIRST = {}
_at = 0
for _n, _c in SLOTS:
    FIRST[_n] = _at
    _at += _c
N_SLOTS = _at
COUNT = dict(SLOTS)

CST = ["ident", "blk64", "mean", "negtri", "negone", "rot", "iota"]
VECS = [("attn_norm", 8), ("ffn_norm", 8), ("norm1", 8), ("norm2", 8), ("final", 8), ("out_norm", 8),
        ("qn", 1), ("kn", 1), ("conv", 6), ("b_in", Z2_TILES), ("conv2", TAPS * 8), ("conv2_b", 8),
        ("ln_g", 8), ("ln_b", 8), ("sinks", 16), ("inv", 1), ("eps", 1), ("one", 1)]
VAT = {}
_at = 0
for _n, _c in VECS:
    VAT[_n] = _at
    _at += _c
NVEC = _at

SPLITS = ["n0", "gn", "n1", "n2", "ln", "at", "mg", "n3"]


def rolled(eng, n, unroll, body):
    full = n // unroll
    if full > 1:
        with eng.Fori(0, full) as i:
            for r in range(unroll):
                body(i * unroll + r, r)
    elif full == 1:
        for r in range(unroll):
            body(r, r)
    for r in range(n - full * unroll):
        body(full * unroll + r, r)


def build(nc, ins, out):
    with ExitStack() as ctx:
        def sb(name, shape, dt=F32):
            return ctx.enter_context(nc.sbuf_tensor(name, shape, dt))

        sems = {}

        def sem(name):
            if name not in sems:
                sems[name] = ctx.enter_context(nc.semaphore(name))
            return sems[name]

        cst = sb("cst", [P, len(CST), P])
        vec = sb("vec", [P, NVEC])
        ident, blk64, mean, negtri, negone, rot, iota = (cst[:, i, :] for i in range(len(CST)))

        def v(name, i=0, n=1):
            return vec[:, VAT[name] + i:VAT[name] + i + n]

        def vd(name, i, n=1):
            return vec[:, VAT[name]:VAT[name] + dict(VECS)[name]][:, bass.ds(i, n)]

        ps = ctx.enter_context(nc.psum_tensor("ps", [P, 8, S], F32))
        hh = sb("hh", [P, KD, S], F32R)
        hl = sb("hl", [P, KD, S], F32R)

        early = ExitStack()

        def esb(name, shape, dt=F32, stack=None):
            return (stack or early).enter_context(nc.sbuf_tensor(name, shape, dt))

        xT = esb("xT", [P, KD, S])
        raw = esb("raw", [P, 2, 2048])
        wh = esb("wh", [P, 2, 2048], F32R)
        wl = esb("wl", [P, 2, 2048], F32R)
        tmp = esb("tmp", [P, 2, S])
        sqb = esb("sqb", [P, 2, S])
        lnb = esb("lnb", [P, 2, S])

        one = ExitStack()
        z1 = esb("z1", [P, Z1_TILES, S], stack=one)
        yT = esb("yT", [P, KD, S], stack=one)
        bt = esb("bt", [P, 8, S], stack=one)
        xin = z1[:, 0:KD, :].rearrange("p (t a) n -> p t (a n)", t=NT)
        kst, qst = tmp[:, 0, :], tmp[:, 1, :]
        spl = yT[:, SB_PAIRS:SB_PAIRS + NT, :]
        sb_in = ExitStack()
        vts = esb("vts", [P, S], stack=sb_in)
        vst = esb("vst", [P, NT, P], stack=sb_in)
        ab = esb("ab", [P, NT, S], stack=sb_in)
        sb_in.close()
        csc, cpr, cpt = (z1[:, 2 * i:2 * i + 2, :] for i in range(3))
        ch_in = ExitStack()
        ckst = esb("ckst", [P, S], stack=ch_in)
        cqst = esb("cqst", [P, S], stack=ch_in)
        cvts = esb("cvts", [P, S], stack=ch_in)
        cvst = esb("cvst", [P, NT, P], stack=ch_in)
        cstat = esb("cstat", [P, 2, 4], stack=ch_in)
        ch_in.close()
        one.close()

        ffn = ExitStack()
        hidh = esb("hidh", [P, FF_TILES, S], F32R, stack=ffn)
        hidl = esb("hidl", [P, FF_TILES, S], F32R, stack=ffn)
        sg, hid = sqb, tmp
        ffn.close()

        two = ExitStack()
        z2 = esb("z2", [P, Z2_TILES, S], stack=two)
        csin = esb("csin", [P, 2, S], stack=two)
        msk = esb("msk", [P, 2 * P], stack=two)
        sstat = esb("sstat", [P, 2, 8], stack=two)
        pos_in = ExitStack()
        pos_i = esb("pos_i", [P, S], I32, stack=pos_in)
        pos_in.close()
        kdup = esb("kdup", [P, 2, S], stack=two)
        rq, rt = sqb[:, 0, :], sqb[:, 1, :]
        ssc, spr = lnb[:, :, 0:2 * P], lnb[:, :, 2 * P:4 * P]
        spt, vn_pairs = tmp[:, :, 0:2 * P], tmp[:, :, 2 * P:4 * P]
        two.close()

        rout = ExitStack()
        qT = esb("qT", [P, HC, S], stack=rout)
        skr = esb("skr", [P, HC, P], stack=rout)
        skT = esb("skT", [P, HC, P], stack=rout)
        scev = esb("scev", [P, 2, 4, P], stack=rout)
        rout.close()
        early.close()

        late = ExitStack()
        ga = esb("ga", [P, EG, S], stack=late)
        er = esb("er", [P, 2, D], stack=late)
        eh = esb("eh", [P, 2, D], F32R, stack=late)
        el = esb("el", [P, 2, D], F32R, stack=late)
        tk = ExitStack()
        sc = esb("sc", [P, 8, NKEYS], stack=tk)
        top = esb("top", [P, 8, TOPK], stack=tk)
        topi = esb("topi", [P, 8, TOPK], U32, stack=tk)
        topf = esb("topf", [P, 8, TOPK], stack=tk)
        best = esb("best", [P, 4, TOPK], stack=tk)
        bpos = esb("bpos", [P, 4, TOPK], U32, stack=tk)
        sel = esb("sel", [P, NT, 3, PH * TOPK], stack=tk)
        bab = esb("bab", [P, 2, 4 * TOPK], U32, stack=tk)
        bfl = esb("bfl", [P, 2, 4 * TOPK], stack=tk)
        den = esb("den", [P, 2, NT * PH], stack=tk)
        tk.close()
        slot_t = esb("slot_t", [P, 3, S], stack=late)
        oh = ExitStack()
        oh1 = esb("oh1", [P, 2, TB, EG], stack=oh)
        oh2 = esb("oh2", [P, 2, TB, NKEYS], stack=oh)
        key2 = esb("key2", [P, 2, TB], stack=oh)
        oh.close()
        gv = ExitStack()
        gah = esb("gah", [P, 2, S], F32R, stack=gv)
        gal = esb("gal", [P, 2, S], F32R, stack=gv)
        gv.close()
        late.close()
        fin = ExitStack()
        xf = esb("xf", [P, KD, S], stack=fin)
        pf = esb("pf", [P, KD, S], stack=fin)
        fsq = esb("fsq", [P, 2, S], stack=fin)
        fln = esb("fln", [P, 2, S], stack=fin)
        xo = esb("xo", [P, NT, D], stack=fin)
        fin.close()

        x_dram = nc.dram_tensor("x_spill", [P, KD, S], F32).ap()
        e_dram = nc.dram_tensor("expert_spill", [P, KD, S], F32).ap()
        sc_dram = nc.dram_tensor("score_spill", [2 * NT, P, PH, NKEYS], F32).ap()

        def by_cols(w):
            return w.rearrange("(k p) n -> p k n", p=P)

        w_in1, w_out1 = by_cols(ins["w_in"]), by_cols(ins["w_out"])
        w_gate, w_up = by_cols(ins["w_gate"]), by_cols(ins["w_up"])
        w_down = ins["w_down"].rearrange("(s j p) n -> p s j n", p=P, j=2)
        w_in2, w_co = by_cols(ins["w_in_2"]), by_cols(ins["w_conv_out_2"])
        w_ao, w_out2 = by_cols(ins["w_attn_o_2"]), by_cols(ins["w_out_2"])
        w_pq = by_cols(ins["w_peer_q_2"])
        u_rows = ins["peer_u_2"].rearrange("(e p) d -> p e d", p=P)
        v_rows = ins["peer_v_2"].rearrange("(e p) d -> p e d", p=P)

        def piece(w, b, k, half):
            return w[:, b, :].rearrange("p (k n) -> p k n", k=KD)[:, k, half * P:half * P + P]

        def piece_down(w, b, j, c):
            return w[:, b, :].rearrange("p (j n) -> p j n", j=2)[:, j, c * P:c * P + P]

        def vn(t):
            return vn_pairs[:, t // 2, (t % 2) * P:(t % 2) * P + P]

        def split_base(name):
            return 8 * SPLITS.index(name)

        block = ctx.enter_context(nc.Block())

        def zt(z, n):
            return z[:, bass.ds(n, 1), :].rearrange("p a n -> p (a n)")

        def tile_done(eng, name, s, half):
            if half:
                eng.wait_ge(sem("w_used"), s + (FIRST[name] + 3))
            else:
                eng.wait_ge(sem("mm_" + name), s + 1)

        def pass_by(eng, signal, count):
            eng.wait_ge(sem(signal), count)
            eng.sem_inc(sem("waits_past"), 1)

        def bank_of(name, n):
            return (2 * FIRST[name] + n) % 4

        @block.sync
        def _(sp):
            sp.dma_start(xin[:, :, :], ins["x"].rearrange("(t p) d -> p t d", p=P)).then_inc(sem("x_loaded"), 16)

            def load(g, b, src, k):
                sp.wait_ge(sem("w_lo"), g + 1)
                sp.dma_start(raw[:, b, :].rearrange("p (k n) -> p k n", k=k), src).then_inc(sem(f"w_raw{b}"), 16)

            def by_col_slots(name, w):
                g0 = FIRST[name]
                rolled(sp, COUNT[name], 2,
                       lambda s, r: load(s + g0, (g0 + r) % 2, w[:, :, bass.ds(s * 256, 256)], KD))

            by_col_slots("in1", w_in1)
            by_col_slots("out1", w_out1)
            g0 = FIRST["ffn"]
            with sp.Fori(0, FF_TILES // 2) as i:
                load(i * 2 + g0, g0 % 2, w_gate[:, :, bass.ds(i * 256, 256)], KD)
                load(i * 2 + (g0 + 1), (g0 + 1) % 2, w_up[:, :, bass.ds(i * 256, 256)], KD)
            g0 = FIRST["down"]
            rolled(sp, COUNT["down"], 2,
                   lambda s, r: load(s + g0, (g0 + r) % 2,
                                     w_down[:, bass.ds(s, 1), :, :].rearrange("p s j n -> p (s j) n"), 2))
            by_col_slots("in2", w_in2)
            by_col_slots("co", w_co)
            by_col_slots("ao", w_ao)
            by_col_slots("out2", w_out2)
            by_col_slots("pq", w_pq)
            sp.wait_ge(sem("x_tile"), 8 * 4)
            sp.dma_start(x_dram, xT[:, :, :]).then_inc(sem("x_spilled"), 16)
            for a in (0, PH):
                sp.dma_start(skr[:, a:a + PH, :], ins["peer_sub_keys_2"][a:a + PH, :, :].rearrange("h n d -> n h d")
                             ).then_inc(sem("sk_loaded"), 16)
            for n in range(NT * 4):
                sp.wait_ge(sem("sc_copied"), n + 1)
                sp.dma_start(sc_dram[n // 2, :, 4 * (n % 2):4 * (n % 2) + 4, :], scev[:, n % 2, :, :]
                             ).then_inc(sem(f"sc_out{n % 2}"), 16)
            sp.wait_ge(sem("sc_out0"), 16 * 2 * NT)
            sp.wait_ge(sem("sc_out1"), 16 * 2 * NT)
            sp.wait_ge(sem("x_spilled"), 16)
            sp.sem_inc(sem("late_free"), 1)
            for grp in range(GROUPS):
                e0 = grp * EG

                def load_u(e, r):
                    sp.wait_ge(sem("u_lo"), e + (e0 + 1))
                    sp.dma_start(er[:, r, :], u_rows[:, bass.ds(e + e0, 1), :].rearrange("p e d -> p (e d)")
                                 ).then_inc(sem(f"u_in{r}"), 16)

                def load_v(e, r):
                    sp.wait_ge(sem("v_lo"), e + (e0 + 1))
                    sp.dma_start(er[:, r, :], v_rows[:, bass.ds(e + e0, 1), :].rearrange("p e d -> p (e d)")
                                 ).then_inc(sem(f"v_in{r}"), 16)

                if grp:
                    sp.wait_ge(sem("v_lo"), e0 + 2)
                    rolled(sp, EG, 2, load_u)
                else:
                    with sp.Fori(0, 2 * NT) as m:
                        sp.wait_ge(sem("tk_unit"), m + 1)
                        sp.dma_start(sc[:, :, :], sc_dram[bass.ds(m, 1), :, :, :].rearrange("m p a n -> p (m a) n")
                                     ).then_inc(sem("sc_in"), 16)
                        for j in range(EG // (2 * NT)):
                            load_u(m * (EG // (2 * NT)) + j, j % 2)
                sp.wait_ge(sem("u_lo"), e0 + EG + 2)
                rolled(sp, EG, 2, load_v)
                if grp == 0:
                    sp.wait_ge(sem("e_part"), KD)
                    sp.dma_start(e_dram, ga[:, 0:KD, :]).then_inc(sem("e_spilled"), 16)
            sp.wait_ge(sem("v_used"), GROUPS * EG + 2)
            sp.dma_start(xf[:, :, :], x_dram).then_inc(sem("x_back"), 16)
            sp.dma_start(pf[:, :, :], e_dram).then_inc(sem("x_back"), 16)
            sp.wait_ge(sem("o_ready"), KD)
            sp.dma_start(out.rearrange("(t p) d -> p t d", p=P), xo[:, :, :]).then_inc(sem("out_done"), 16)
            sp.wait_ge(sem("out_done"), 16)

        @block.gpsimd
        def _(pool):
            for name in ("w_lo", "sp_l", "hid_l", "u_lo"):
                pool.sem_inc(sem(name), 2)
            pool.dma_start(bt[:, :, :], ins["rel_tiles"].rearrange("h p m -> p h m")).then_inc(sem("bt_loaded"), 16)

            def low(g, b):
                pool.wait_ge(sem("w_hi"), g + 1)
                pool.tensor_tensor(wl[:, b, :], raw[:, b, :], wh[:, b, :].bitcast(F32), ALU.subtract
                                   ).then_inc(sem("w_lo"), 1)

            def lows(a, b):
                rolled(pool, b - a, 2, lambda s, r: low(s + a, (a + r) % 2))

            def split_low(name):
                base = split_base(name)
                for k in range(KD):
                    pool.wait_ge(sem("sp_h"), base + k + 1)
                    pool.tensor_tensor(hl[:, k, :], tmp[:, k % 2, :], hh[:, k, :].bitcast(F32), ALU.subtract
                                       ).then_inc(sem("sp_l"), 1)

            lows(0, 2)
            split_low("n0")
            lows(2, FIRST["out1"] + 2)
            pool.wait_ge(sem("bt_loaded"), 16)
            pool.memset(bt[0:64, :, 448:512], NEG).then_inc(sem("bt_ready"), 1)
            with pool.Fori(0, SB_PAIRS) as p:
                for e in range(2):
                    for tile, ready, done in ((spl, "sb_sp0", "sb_sp"), (ab, "sb_w0", "sb_w")):
                        for q, b in enumerate(reversed(range(NT))):
                            pass_by(pool, ready, p * 8 + (4 * e + q + 1))
                            pool.affine_select(out=tile[:, b, 0:P], in_=tile[:, b, 0:P], pattern=[[1, P]],
                                               compare_op=ALU.is_gt, fill=0.0, base=0, channel_multiplier=-1
                                               ).then_inc(sem(done), 1)
            split_low("gn")
            lows(FIRST["out1"] + 2, FIRST["ffn"] + 2)
            split_low("n1")
            with pool.Fori(0, FF_TILES // 2) as i:
                for q in range(2):
                    low(i * 2 + (FIRST["ffn"] + 2 + q), q)
                for q in range(2):
                    pool.wait_ge(sem("hid_h"), i * 2 + (q + 1))
                    pool.tensor_tensor(zt(hidl, i * 2 + q), hid[:, q, :], zt(hidh, i * 2 + q).bitcast(F32),
                                       ALU.subtract).then_inc(sem("hid_l"), 1)
            lows(FIRST["down"] + 2, FIRST["in2"] + 2)
            split_low("n2")
            pool.memset(msk[:, :], 0.0).then_inc(sem("msk"), 1)
            pool.wait_ge(sem("msk"), 1)
            pool.affine_select(out=msk[:, :], in_=msk[:, :], pattern=[[1, 2 * P]], compare_op=ALU.is_gt, fill=NEG,
                               base=0, channel_multiplier=-1).then_inc(sem("msk"), 1)
            pool.wait_ge(sem("msk"), 2)
            pool.affine_select(out=msk[:, :], in_=msk[:, :], pattern=[[-1, 2 * P]], compare_op=ALU.is_ge, fill=NEG,
                               base=P, channel_multiplier=1).then_inc(sem("msk"), 1)
            lows(FIRST["in2"] + 2, FIRST["co"] + 2)
            split_low("ln")
            lows(FIRST["co"] + 2, FIRST["ao"] + 2)
            split_low("at")
            lows(FIRST["ao"] + 2, FIRST["out2"] + 2)
            split_low("mg")
            lows(FIRST["out2"] + 2, FIRST["pq"] + 2)
            split_low("n3")
            lows(FIRST["pq"] + 2, N_SLOTS)

            for grp in range(GROUPS):
                def low_u(e, r):
                    pool.wait_ge(sem("u_hi"), e * 2 + (2 * grp * EG + 2))
                    pool.tensor_tensor(el[:, r, :], er[:, r, :], eh[:, r, :].bitcast(F32), ALU.subtract
                                       ).then_inc(sem("u_lo"), 1)

                def hot2(n, r):
                    pool.wait_ge(sem("g_mm"), n + (grp * (S // TB) + 1))
                    pool.tensor_copy(key2[:, r, :], slot_t[:, 1, bass.ds(n * TB, TB)]).then_inc(sem("key2"), 1)
                    pass_by(pool, "key2", n + (grp * (S // TB) + 1))
                    for t in range(TB):
                        pool.tensor_scalar(oh2[:, r, t, :], iota, key2[:, r, t:t + 1], None, ALU.is_equal
                                           ).then_inc(sem("oh2"), 1)

                rolled(pool, EG, 2, low_u)
                pool.wait_ge(sem("slot_t"), 3)
                rolled(pool, S // TB, 2, hot2)

        @block.scalar
        def _(act):
            act.dma_start(cst[:, :, :], ins["cst"]).then_inc(sem("c_loaded"), 16)
            act.dma_start(vec[:, :], ins["vec"]).then_inc(sem("c_loaded"), 16)

            def high(g, b):
                act.wait_ge(sem(f"w_raw{b}"), g * 8 + (16 - 8 * b))
                act.wait_ge(sem("w_used"), g + 1)
                act.activation(wh[:, b, :], raw[:, b, :], ACT.Copy).then_inc(sem("w_hi"), 1)

            def highs(name):
                g0 = FIRST[name]
                rolled(act, COUNT[name], 2, lambda s, r: high(s + (g0 + 2), (g0 + r) % 2))

            def split_high(name):
                base = split_base(name)
                for k in range(KD):
                    act.wait_ge(sem("sp_t"), base + k + 1)
                    act.activation(hh[:, k, :], tmp[:, k % 2, :], ACT.Copy).then_inc(sem("sp_h"), 1)

            def rstd(ms, scratch, dst, done, count):
                act.activation(scratch, ms, ACT.Ln, bias=v("eps")).then_inc(sem(done + "_ln"), 1)
                act.wait_ge(sem(done + "_ln"), count)
                act.activation(dst, scratch, ACT.Exp, scale=-0.5).then_inc(sem(done + "_rs"), 1)

            def norm(n, x, ready, first, sq, ln):
                for k in range(KD):
                    act.wait_ge(sem(ready), first + k + 1)
                    act.wait_ge(sem("nm_mm"), 8 * n + k + 1)
                    act.activation(sq[:, k % 2, :], x[:, k, :], ACT.Square).then_inc(sem("nm_sq"), 1)
                act.wait_ge(sem("nm_mm"), 8 * n + 8 + 2)
                rstd(ps[:, 4, :], ln[:, 0, :], ln[:, 1, :], "nm", n + 1)

            def evacuate(name, first, last, tile, ahead=True):
                g0 = FIRST[name]

                def slot(s, r):
                    g = g0 + first // 2 + r
                    for half in range(2):
                        tile_done(act, name, s + first // 2, half)
                        tile(s * 2 + (first + half), 2 * (g % 2) + half)
                    if ahead:
                        high(s + (g0 + first // 2 + 2), g % 2)

                rolled(act, (last - first) // 2, 2, slot)

            high(0, 0)
            high(1, 1)
            act.wait_ge(sem("c_loaded"), 32)
            norm(0, xT, "x_tile", 0, sqb, lnb)
            split_high("n0")

            def z1_tile(n, bank):
                act.activation(zt(z1, n), ps[:, bank, :], ACT.Copy).then_inc(sem("ev_in1"), 1)

            evacuate("in1", 0, Z1_TILES, z1_tile)

            with act.Fori(0, SB_PAIRS) as p:
                act.wait_ge(sem("sb_vt"), p + 1)
                act.activation(vst[:, :, :], ps[:, 5, :].rearrange("p (t n) -> p t n", t=NT), ACT.Copy
                               ).then_inc(sem("sb_v"), 1)
                for e in range(2):
                    if e:
                        act.wait_ge(sem("sb_pv"), p * 2 + 1)
                    for q, b in enumerate(reversed(range(NT))):
                        w = S - b * P
                        n = p * 8 + (4 * e + q + 1)
                        act.wait_ge(sem("sb_z"), n)
                        act.activation(ab[:, b, 0:w], ps[:, b, 0:w], ACT.Abs).then_inc(sem("sb_abs"), 1)
                        act.wait_ge(sem("sb_abs"), n)
                        act.activation(ab[:, b, 0:w], ab[:, b, 0:w], ACT.Exp, scale=-1.0).then_inc(sem("sb_e"), 1)
                        act.wait_ge(sem("sb_e"), n)
                        act.activation(ab[:, b, 0:w], ab[:, b, 0:w], ACT.Ln, bias=v("one")).then_inc(sem("sb_l"), 1)
                    for q, b in enumerate(reversed(range(NT))):
                        w = S - b * P
                        n = p * 8 + (4 * e + q + 1)
                        act.wait_ge(sem("sb_cum"), n)
                        act.activation(ab[:, b, 0:w], ps[:, b, 0:w], ACT.Exp).then_inc(sem("sb_w0"), 1)
                act.wait_ge(sem("sb_pv"), p * 2 + 2)
                act.activation(zt(yT, p), ps[:, 4, :], ACT.Copy).then_inc(sem("sb_y"), 1)

            act.wait_ge(sem("sb_y"), SB_PAIRS + 1)
            with act.Fori(0, CH_PAIRS) as p:
                for w, src in enumerate((QB, KB)):
                    act.wait_ge(sem("ch_qk"), p * 2 + 1)
                    act.activation(sqb[:, w, :], zt(z1, p + src), ACT.Square).then_inc(sem("ch_sq"), 1)
                for w in range(2):
                    act.wait_ge(sem("ch_ms"), p * 2 + (w + 1))
                    rstd(ps[:, 6 + w, :], lnb[:, w, :], lnb[:, w, :], "ch", p * 2 + (w + 1))
                act.wait_ge(sem("ch_vt"), p + 1)
                act.activation(cvst[:, :, :], ps[:, 5, :].rearrange("p (t n) -> p t n", t=NT), ACT.Copy
                               ).then_inc(sem("ch_v"), 1)

                def weights(s):
                    w = (s % 4 + 1) * P
                    act.wait_ge(sem("ch_m"), p * 8 + (s + 1))
                    act.activation(cpr[:, s % 2, 0:w], csc[:, s % 2, 0:w], ACT.Exp, bias=cstat[:, s % 2, 0:1],
                                   accum_out=cstat[:, s % 2, 1:2]).then_inc(sem("ch_e"), 1)

                weights(0)
                for s in range(8):
                    if s < 7:
                        weights(s + 1)
                    w = (s % 4 + 1) * P
                    act.wait_ge(sem("ch_t"), p * 8 + (s + 1))
                    act.wait_ge(sem("ch_o"), p * 8 + (s + 1))
                    act.activation(cpt[:, s % 2, 0:w], ps[:, 2 + s % 2, 0:w], ACT.Copy).then_inc(sem("ch_pt"), 1)
                act.wait_ge(sem("ch_o"), p * 8 + (8 + 2))
                act.activation(zt(yT, p + SB_PAIRS), ps[:, 4, :], ACT.Copy).then_inc(sem("ch_y"), 1)

            act.wait_ge(sem("cv_y"), CV_TILES)
            act.wait_ge(sem("ch_y"), CH_PAIRS + 1)
            for j in range(KD):
                act.wait_ge(sem("gn_mm"), j + 1)
                act.activation(sqb[:, j % 2, :], yT[:, j, :], ACT.Square).then_inc(sem("gn_sq"), 1)
                act.wait_ge(sem("gn_mm"), j + 3)
                act.wait_ge(sem("sp_t"), split_base("gn") + j)
                rstd(ps[:, 4 + j % 2, :], lnb[:, 0, :], lnb[:, 1, :], "gn", j + 1)
                act.wait_ge(sem("sp_t"), split_base("gn") + j + 1)
                act.activation(hh[:, j, :], tmp[:, j % 2, :], ACT.Copy).then_inc(sem("sp_h"), 1)
            highs("out1")
            norm(1, xT, "x_tile", 8, sqb, lnb)
            split_high("n1")

            g0 = FIRST["ffn"]
            with act.Fori(0, FF_TILES // 2) as i:
                for q in range(2):
                    if q:
                        act.wait_ge(sem("w_used"), i * 2 + (g0 + 3))
                    else:
                        act.wait_ge(sem("mm_g"), i + 1)
                    act.wait_ge(sem("ffn_u"), i * 2 + (q + 1))
                    act.activation(sg[:, q, :], ps[:, q, :], ACT.Silu).then_inc(sem("ffn_g"), 1)
                for q in range(2):
                    high(i * 2 + (g0 + 2 + q), q)
                for q in range(2):
                    act.wait_ge(sem("ffn_u"), i * 2 + (q + 3))
                    act.activation(zt(hidh, i * 2 + q), hid[:, q, :], ACT.Copy).then_inc(sem("hid_h"), 1)
            highs("down")
            act.wait_ge(sem("w_used"), FIRST["in2"] + 2)
            act.dma_start(pos_i[:, :], ins["positions"]).then_inc(sem("pos_loaded"), 16)
            norm(2, xT, "x_tile", 16, sqb, lnb)
            split_high("n2")

            def z2_tile(func):
                def tile(n, bank):
                    act.activation(zt(z2, n), ps[:, bank, :], func, bias=vd("b_in", n)).then_inc(sem("ev_in2"), 1)
                return tile

            evacuate("in2", VAL, GATE, z2_tile(ACT.Identity))
            evacuate("in2", GATE, Q2, z2_tile(ACT.Sigmoid))
            evacuate("in2", Q2, GCONV, z2_tile(ACT.Identity))
            evacuate("in2", GCONV, Z2_TILES, z2_tile(ACT.Sigmoid))

            act.wait_ge(sem("rp_a"), 1)
            act.activation(csin[:, :, :], csin[:, :, :], ACT.Sin).then_inc(sem("rp_s"), 1)

            for j in range(KD):
                act.wait_ge(sem("ln_x"), j + 1)
                act.wait_ge(sem("ln_v"), j + 1)
                act.activation(sqb[:, j % 2, :], z2[:, GATE + j, :], ACT.Square).then_inc(sem("ln_sq"), 1)
            act.wait_ge(sem("ln_v"), KD + 2)
            rstd(ps[:, 7, :], lnb[:, 0, :], lnb[:, 1, :], "ln", 1)
            base = split_base("ln")
            for j in range(KD):
                act.wait_ge(sem("ln_n"), j + 1)
                act.wait_ge(sem("sp_l"), base + j + 1)
                act.activation(tmp[:, j % 2, :], z2[:, GATE + j, :], ACT.Silu, scale=v("ln_g", j), bias=v("ln_b", j)
                               ).then_inc(sem("sp_t"), 1)
                act.wait_ge(sem("sp_t"), base + j + 1)
                act.activation(hh[:, j, :], tmp[:, j % 2, :], ACT.Copy).then_inc(sem("sp_h"), 1)
            highs("co")

            act.wait_ge(sem("sw_vt"), 1)
            act.activation(vn_pairs, ps[:, 5, :].rearrange("p (a n) -> p a n", a=2), ACT.Copy
                           ).then_inc(sem("sw_v"), 1)
            with act.Fori(0, SWA_PAIRS) as p:
                def weights(s):
                    w = P if s % 4 == 0 else 2 * P
                    st = sstat[:, s % 2, :]
                    act.wait_ge(sem("sw_m"), p * 8 + (s + 1))
                    act.activation(spr[:, s % 2, 0:w], ssc[:, s % 2, 0:w], ACT.Exp, bias=st[:, 0:1],
                                   accum_out=st[:, 1:2]).then_inc(sem("sw_e"), 1)
                    act.activation(st[:, 2:3], st[:, 5:6], ACT.Exp, bias=st[:, 0:1]).then_inc(sem("sw_e"), 1)

                weights(0)
                for s in range(8):
                    if s < 7:
                        weights(s + 1)
                    w = P if s % 4 == 0 else 2 * P
                    act.wait_ge(sem("sw_t"), p * 8 + (s + 1))
                    act.wait_ge(sem("sw_o"), p * 8 + (s + 1))
                    act.activation(spt[:, s % 2, 0:w], ps[:, 2 + s % 2, 0:w], ACT.Copy).then_inc(sem("sw_pt"), 1)
                act.wait_ge(sem("sw_o"), p * 8 + (8 + 2))
                act.activation(zt(z2, p), ps[:, 4, :], ACT.Copy).then_inc(sem("sw_y"), 1)
            base = split_base("at")
            act.wait_ge(sem("sw_y"), SWA_PAIRS + 1)
            act.wait_ge(sem("w_used"), FIRST["ao"] + 2)
            for k in range(KD):
                act.wait_ge(sem("sp_l"), base + k + 1)
                act.activation(tmp[:, k % 2, :], z2[:, k, :], ACT.Copy).then_inc(sem("sp_t"), 1)
                act.activation(hh[:, k, :], z2[:, k, :], ACT.Copy).then_inc(sem("sp_h"), 1)
            highs("ao")
            split_high("mg")
            highs("out2")
            norm(3, xT, "x_tile", 24, sqb, lnb)
            split_high("n3")

            def q_tile(n, bank):
                act.activation(zt(qT, n), ps[:, bank, :], ACT.Copy).then_inc(sem("ev_pq"), 1)

            evacuate("pq", 0, HC - 4, q_tile)
            evacuate("pq", HC - 4, HC, q_tile, ahead=False)
            for n in range(4):
                act.wait_ge(sem("sk_t"), n + 1)
                act.activation(skT[:, 4 * n:4 * n + 4, :], ps[:, 4 + n % 2, :].rearrange("p (a n) -> p a n", a=4),
                               ACT.Copy).then_inc(sem("sk_c"), 1)
            for n in range(NT * 4):
                act.wait_ge(sem("sc_mm"), n + 1)
                if n >= 2:
                    act.wait_ge(sem(f"sc_out{n % 2}"), 16 * (n // 2))
                act.activation(scev[:, n % 2, :, :], ps[:, 6 + n % 2, :].rearrange("p (a n) -> p a n", a=4), ACT.Copy
                               ).then_inc(sem("sc_copied"), 1)
            act.wait_ge(sem("late_free"), 1)

            for grp in range(GROUPS):
                e0 = grp * EG

                def turned(e, r):
                    act.wait_ge(sem("u_turned"), e + (e0 + 1))
                    act.wait_ge(sem("a_mm"), e + (e0 + 1))
                    for dst in (er, eh):
                        act.activation(dst[:, r, :].rearrange("p (b n) -> p b n", b=2), ps[:, 2 * r:2 * r + 2, :],
                                       ACT.Copy).then_inc(sem("u_hi"), 1)

                def gelu(e, r):
                    act.wait_ge(sem("a_mm"), e + (e0 + 1 + 2))
                    act.activation(zt(ga, e), ps[:, 4 + r, :], ACT.Gelu).then_inc(sem("a_ev"), 1)

                def high_v(e, r):
                    act.wait_ge(sem(f"v_in{r}"), e * 8 + (16 - 8 * r + 8 * e0))
                    act.wait_ge(sem("v_used"), e + (e0 + 1))
                    act.activation(eh[:, r, :], er[:, r, :], ACT.Copy).then_inc(sem("v_hi"), 1)
                    act.activation(gah[:, r, :], zt(ga, e), ACT.Copy).then_inc(sem("v_hi"), 1)

                if grp:
                    act.wait_ge(sem("e_spilled"), 16)
                    act.wait_ge(sem("v_used"), e0 + 2)
                turned(0, 0)
                with act.Fori(0, EG // 2 - 1) as i:
                    for r in range(2):
                        turned(i * 2 + (r + 1), (r + 1) % 2)
                        gelu(i * 2 + r, r)
                turned(EG - 1, 1)
                gelu(EG - 2, 0)
                gelu(EG - 1, 1)
                if grp == 0:
                    act.wait_ge(sem("tk_unit"), 2 * NT + 1)
                    act.activation(sel[:, :, 2, :], sel[:, :, 2, :], ACT.Exp).then_inc(sem("gt_e"), 1)
                    for a in range(3):
                        act.wait_ge(sem("slot_mm"), a + 1)
                        act.activation(slot_t[:, a, :], ps[:, 5 + a, :], ACT.Copy).then_inc(sem("slot_t"), 1)
                act.wait_ge(sem("g_mul"), (grp + 1) * (S // TB) + 2)
                rolled(act, EG, 2, high_v)
            norm(4, xf, "y_sum", 0, fsq, fln)

        @block.tensor
        def _(pe):
            for name in ("w_used", "nm_mm", "gn_mm", "ln_v", "ch_o", "sw_o", "a_mm", "g_mm", "v_used"):
                pe.sem_inc(sem(name), 2)

            def three(bank, whi, wlo, xhi, xlo, start, stop):
                nc.tensor.matmul(bank, whi, xhi, start=start, stop=False)
                nc.tensor.matmul(bank, whi, xlo, start=False, stop=False)
                return nc.tensor.matmul(bank, wlo, xhi, start=False, stop=stop)

            def norm(n, sq):
                for k in range(KD):
                    pe.wait_ge(sem("nm_sq"), 8 * n + k + 1)
                    nc.tensor.matmul(ps[:, 4, :], mean, sq[:, k % 2, :], start=(k == 0), stop=(k == KD - 1)
                                     ).then_inc(sem("nm_mm"), 1)

            def slot_tiles(g, b, first_done, bank_free):
                pe.wait_ge(sem("w_lo"), g + 3)
                for half in range(2):
                    bank_free(half)
                    for k in range(KD):
                        last = three(ps[:, 2 * b + half, :], piece(wh, b, k, half), piece(wl, b, k, half),
                                     hh[:, k, :], hl[:, k, :], k == 0, k == KD - 1)
                    last.then_inc(sem("w_used" if half else first_done), 1)

            def gemm(name, split, freed=None, base=0):
                g0 = FIRST[name]
                pe.wait_ge(sem("sp_l"), split_base(split) + 8 + 2)
                rolled(pe, COUNT[name], 2, lambda s, r: slot_tiles(
                    s + g0, (g0 + r) % 2, "mm_" + name,
                    lambda half: pe.wait_ge(sem(freed or "ev_" + name), s * 2 + (half + 1 + base))))

            pe.wait_ge(sem("x_loaded"), 16)
            pe.wait_ge(sem("c_loaded"), 32)
            for k in range(KD):
                if k >= 4:
                    pe.wait_ge(sem("x_tile"), k - 3)
                for t in range(NT):
                    last = nc.tensor.transpose(ps[:, k % 4, t * P:t * P + P], xin[:, t, k * P:k * P + P], ident)
                last.then_inc(sem("x_turned"), 1)
            norm(0, sqb)
            gemm("in1", "n0")

            with pe.Fori(0, SB_PAIRS) as p:
                pe.wait_ge(sem("sb_staged"), p * 3 + 3)
                for t in range(NT):
                    last = nc.tensor.transpose(ps[:, 5, t * P:t * P + P], vts[:, t * P:t * P + P], ident)
                last.then_inc(sem("sb_vt"), 1)
                for e in range(2):
                    n = p * 8 + 4 * e
                    h = slice(HD * e, HD * e + HD)
                    if e:
                        pe.wait_ge(sem("sb_w0"), p * 8 + 4)
                    for b in reversed(range(NT)):
                        nc.tensor.matmul(ps[:, b, 0:S - b * P], kst[h, b * P:b * P + P], qst[h, b * P:S],
                                         start=True, stop=True).then_inc(sem("sb_z"), 1)
                    for q, b in enumerate(reversed(range(NT))):
                        pe.wait_ge(sem("sb_sp"), n + (q + 1))
                        last = nc.tensor.matmul(ps[:, b, 0:S - b * P], negtri, spl[:, b, 0:S - b * P], start=False,
                                                stop=(b == NT - 1), skip_group_check=True)
                        for c in range(b + 1, NT):
                            last = nc.tensor.matmul(ps[:, b, (c - b) * P:S - b * P], negone, spl[:, c, 0:S - c * P],
                                                    start=False, stop=(c == NT - 1), skip_group_check=True)
                        last.then_inc(sem("sb_cum"), 1)
                    pe.wait_ge(sem("sb_v"), p + 1)
                    pe.wait_ge(sem("sb_w"), n + 4)
                    if e == 0:
                        pe.wait_ge(sem("sb_y"), p + 1)
                    for b in range(NT):
                        last = nc.tensor.matmul(ps[h, 4, b * P:S], vst[:, b, h], ab[:, b, 0:S - b * P],
                                                start=(b == 0), stop=(b == NT - 1))
                    last.then_inc(sem("sb_pv"), 1)

            with pe.Fori(0, CH_PAIRS) as p:
                for w in range(2):
                    pe.wait_ge(sem("ch_sq"), p * 2 + (w + 1))
                    nc.tensor.matmul(ps[:, 6 + w, :], blk64, sqb[:, w, :], start=True, stop=True
                                     ).then_inc(sem("ch_ms"), 1)
                pe.wait_ge(sem("ch_vs"), p + 1)
                for t in range(NT):
                    last = nc.tensor.transpose(ps[:, 5, t * P:t * P + P], cvts[:, t * P:t * P + P], ident)
                last.then_inc(sem("ch_vt"), 1)
                pe.wait_ge(sem("ch_qk"), p * 2 + 3)

                def scores(s):
                    e, i = s // 4, s % 4
                    h = slice(HD * e, HD * e + HD)
                    pe.wait_ge(sem("ch_s"), p * 8 + (s + 1))
                    nc.tensor.matmul(ps[:, s % 2, 0:(i + 1) * P], cqst[h, i * P:i * P + P], ckst[h, 0:(i + 1) * P],
                                     start=True, stop=True).then_inc(sem("ch_sc"), 1)

                def turn(s):
                    pe.wait_ge(sem("ch_p"), p * 8 + (s + 1))
                    pe.wait_ge(sem("ch_pt"), p * 8 + (s + 1))
                    for b in range(s % 4 + 1):
                        last = nc.tensor.transpose(ps[:, 2 + s % 2, b * P:b * P + P], cpr[:, s % 2, b * P:b * P + P],
                                                   ident)
                    last.then_inc(sem("ch_t"), 1)

                def values(s):
                    e, i = s // 4, s % 4
                    h = slice(HD * e, HD * e + HD)
                    pe.wait_ge(sem("ch_pt"), p * 8 + (s + 3))
                    if s == 0:
                        pe.wait_ge(sem("ch_v"), p + 1)
                        pe.wait_ge(sem("ch_y"), p + 1)
                    for b in range(i + 1):
                        last = nc.tensor.matmul(ps[h, 4, i * P:i * P + P], cvst[:, b, h],
                                                cpt[:, s % 2, b * P:b * P + P], start=(b == 0), stop=(b == i))
                    last.then_inc(sem("ch_o"), 1)

                scores(0)
                for s in range(8):
                    if s < 7:
                        scores(s + 1)
                    turn(s)
                    if s:
                        values(s - 1)
                values(7)

            for j in range(KD):
                pe.wait_ge(sem("gn_sq"), j + 1)
                if j >= 2:
                    pe.wait_ge(sem("gn_ln"), j - 1)
                nc.tensor.matmul(ps[:, 4 + j % 2, :], blk64, sqb[:, j % 2, :], start=True, stop=True
                                 ).then_inc(sem("gn_mm"), 1)
            gemm("out1", "gn", "x_tile", 8 - 4)
            norm(1, sqb)

            pe.wait_ge(sem("sp_l"), split_base("n1") + 8 + 2)
            g0 = FIRST["ffn"]
            with pe.Fori(0, FF_TILES // 2) as i:
                slot_tiles(i * 2 + g0, 0, "mm_g", lambda half: pe.wait_ge(sem("ffn_g"), i * 2 + (half + 1)))
                slot_tiles(i * 2 + (g0 + 1), 1, "mm_u", lambda half: pe.wait_ge(sem("ffn_u"), i * 2 + (half + 1)))
            g0 = FIRST["down"]
            pe.wait_ge(sem("ffn_u"), FF_TILES + 2)

            def down(s, b, start=False, stop=False):
                pe.wait_ge(sem("w_lo"), s + (g0 + 3))
                pe.wait_ge(sem("hid_l"), s * 2 + 4)
                for j in range(2):
                    for c in range(KD):
                        last = three(ps[:, c, :], piece_down(wh, b, j, c), piece_down(wl, b, j, c),
                                     zt(hidh, s * 2 + j), zt(hidl, s * 2 + j), start and j == 0, stop and j == 1)
                last.then_inc(sem("w_used"), 1)

            down(0, g0 % 2, start=True)
            rolled(pe, COUNT["down"] - 2, 2, lambda s, r: down(s + 1, (g0 + 1 + r) % 2))
            down(COUNT["down"] - 1, (g0 + COUNT["down"] - 1) % 2, stop=True)
            pe.wait_ge(sem("x_tile"), 8 * 2 + 5)
            norm(2, sqb)
            gemm("in2", "n2")

            for j in range(KD):
                pe.wait_ge(sem("cv2_y"), j + 1)
                last = nc.tensor.matmul(ps[:, 6, :], mean, z2[:, GATE + j, :], start=(j == 0), stop=(j == KD - 1))
            last.then_inc(sem("ln_m"), 1)
            for j in range(KD):
                pe.wait_ge(sem("ln_sq"), j + 1)
                nc.tensor.matmul(ps[:, 7, :], mean, sqb[:, j % 2, :], start=(j == 0), stop=(j == KD - 1)
                                 ).then_inc(sem("ln_v"), 1)
            gemm("co", "ln")

            pe.wait_ge(sem("ev_in2"), Z2_TILES + 4)
            nc.tensor.matmul(ps[:, 6, :], rot, z2[:, K2, :], start=True, stop=True).then_inc(sem("rk_mm"), 1)
            for t in range(NT):
                last = nc.tensor.transpose(ps[:, 5, t * P:t * P + P], z2[:, V2, t * P:t * P + P], ident)
            last.then_inc(sem("sw_vt"), 1)
            pe.wait_ge(sem("kd"), 4)
            pe.wait_ge(sem("sw_v"), 1)
            for kv in range(2):
                with pe.Fori(kv * PAIRS_PER_KV, (kv + 1) * PAIRS_PER_KV) as p:
                    pe.wait_ge(sem("rq"), p + 1)
                    nc.tensor.matmul(ps[:, 6, :], rot, zt(z2, p + Q2), start=True, stop=True).then_inc(sem("rq_mm"), 1)
                    pe.wait_ge(sem("rq"), p + 2)

                    def scores(s):
                        e, i = s // 4, s % 4
                        h = slice(HD * e, HD * e + HD)
                        k0 = max(i - 1, 0) * P
                        pe.wait_ge(sem("sw_s"), p * 8 + (s + 1))
                        nc.tensor.matmul(ps[:, s % 2, 0:(i + 1) * P - k0], rq[h, i * P:i * P + P],
                                         kdup[h, kv, k0:(i + 1) * P], start=True, stop=True
                                         ).then_inc(sem("sw_sc"), 1)

                    def turn(s):
                        pe.wait_ge(sem("sw_p"), p * 8 + (s + 1))
                        pe.wait_ge(sem("sw_pt"), p * 8 + (s + 1))
                        for b in range(1 if s % 4 == 0 else 2):
                            last = nc.tensor.transpose(ps[:, 2 + s % 2, b * P:b * P + P],
                                                       spr[:, s % 2, b * P:b * P + P], ident)
                        last.then_inc(sem("sw_t"), 1)

                    def values(s):
                        e, i = s // 4, s % 4
                        h = slice(HD * e, HD * e + HD)
                        n = 1 if i == 0 else 2
                        pe.wait_ge(sem("sw_pt"), p * 8 + (s + 3))
                        if s == 0:
                            pe.wait_ge(sem("sw_y"), p + 1)
                        for b in range(n):
                            last = nc.tensor.matmul(ps[h, 4, i * P:i * P + P],
                                                    vn(i + 1 - n + b)[:, HD * kv:HD * kv + HD],
                                                    spt[:, s % 2, b * P:b * P + P], start=(b == 0), stop=(b == n - 1))
                        last.then_inc(sem("sw_o"), 1)

                    scores(0)
                    for s in range(8):
                        if s < 7:
                            scores(s + 1)
                        turn(s)
                        if s:
                            values(s - 1)
                    values(7)
            gemm("ao", "at")
            gemm("out2", "mg", "x_tile", 24 - 4)
            norm(3, sqb)
            gemm("pq", "n3")

            pe.wait_ge(sem("sk_loaded"), 32)
            for n in range(4):
                if n >= 2:
                    pe.wait_ge(sem("sk_c"), n - 1)
                for a in range(4):
                    last = nc.tensor.transpose(ps[:, 4 + n % 2, a * P:a * P + P], skr[:, 4 * n + a, :], ident)
                last.then_inc(sem("sk_t"), 1)
            pe.wait_ge(sem("sk_c"), 4)
            pe.wait_ge(sem("ev_pq"), HC + 4)
            for n in range(NT * 4):
                t, c = n // 4, n % 4
                if n >= 2:
                    pe.wait_ge(sem("sc_copied"), n - 1)
                for a in range(4):
                    last = nc.tensor.matmul(ps[:, 6 + n % 2, a * P:a * P + P], qT[:, 4 * c + a, t * P:t * P + P],
                                            skT[:, 4 * c + a, :], start=True, stop=True)
                last.then_inc(sem("sc_mm"), 1)

            for grp in range(GROUPS):
                e0, n0 = grp * EG, grp * (S // TB)

                def turn_u(e, r):
                    pe.wait_ge(sem(f"u_in{r}"), e * 8 + (16 - 8 * r + 8 * e0))
                    pe.wait_ge(sem("u_lo"), e + (e0 + 1))
                    for k in range(KD):
                        last = nc.tensor.transpose(ps[:, 2 * r + k // 4, (k % 4) * P:(k % 4) * P + P],
                                                   er[:, r, k * P:k * P + P], ident)
                    last.then_inc(sem("u_turned"), 1)

                def dots(e, r):
                    pe.wait_ge(sem("u_lo"), e + (e0 + 3))
                    pe.wait_ge(sem("a_ev"), e + (e0 + 1))
                    for k in range(KD):
                        last = three(ps[:, 4 + r, :], eh[:, r, k * P:k * P + P], el[:, r, k * P:k * P + P],
                                     hh[:, k, :], hl[:, k, :], k == 0, k == KD - 1)
                    last.then_inc(sem("a_mm"), 1)

                def table(n, r):
                    pe.wait_ge(sem("oh1"), n * 2 + (2 * n0 + 2))
                    pe.wait_ge(sem("oh2"), n * TB + (TB * n0 + TB))
                    pe.wait_ge(sem("g_mul"), n + (n0 + 1))
                    for t in range(TB):
                        last = nc.tensor.matmul(ps[:, r, t * EG:t * EG + EG], oh2[:, r, t, :], oh1[:, r, t, :],
                                                start=True, stop=True)
                    last.then_inc(sem("g_mm"), 1)

                def gather(e, r, start=False, stop=False):
                    pe.wait_ge(sem("v_lo"), e + (e0 + 3))
                    for c in range(KD):
                        last = three(ps[:, c, :], eh[:, r, c * P:c * P + P], el[:, r, c * P:c * P + P], gah[:, r, :],
                                     gal[:, r, :], start, stop)
                    last.then_inc(sem("v_used"), 1)

                if grp:
                    pe.wait_ge(sem("e_part"), KD)
                turn_u(0, 0)
                with pe.Fori(0, EG // 2 - 1) as i:
                    for r in range(2):
                        turn_u(i * 2 + (r + 1), (r + 1) % 2)
                        dots(i * 2 + r, r)
                turn_u(EG - 1, 1)
                dots(EG - 2, 0)
                dots(EG - 1, 1)
                pe.wait_ge(sem("a_ev"), e0 + EG + 2)
                if grp == 0:
                    pe.wait_ge(sem("gt"), 1)
                    for a in range(3):
                        for t in range(NT):
                            last = nc.tensor.transpose(ps[:, 5 + a, t * P:t * P + P], sel[:, t, a, :], ident)
                        last.then_inc(sem("slot_mm"), 1)
                rolled(pe, S // TB, 2, table)
                gather(0, 0, start=True)
                rolled(pe, EG - 2, 2, lambda e, r: gather(e + 1, (1 + r) % 2))
                gather(EG - 1, 1, stop=True)
            norm(4, fsq)
            for k in range(KD):
                pe.wait_ge(sem("y_t"), k + 1)
                if k >= 4:
                    pe.wait_ge(sem("o_ready"), k - 3)
                for t in range(NT):
                    last = nc.tensor.transpose(ps[:, k % 4, t * P:t * P + P], pf[:, k, t * P:t * P + P], ident)
                last.then_inc(sem("y_turned"), 1)

        @block.vector
        def _(dve):
            for name in ("in1", "in2", "co", "ao", "pq"):
                dve.sem_inc(sem("ev_" + name), 4)
            for name in ("ffn_u", "ffn_g", "ch_s", "ch_pt", "sw_s", "sw_pt", "a_ev", "g_mul", "v_lo"):
                dve.sem_inc(sem(name), 2)
            for name in ("sb_y", "ch_qk", "ch_y", "rq", "sw_y", "tk_unit"):
                dve.sem_inc(sem(name), 1)

            chained = {}

            def chain(name, ins):
                chained[name] = chained.get(name, 0) + 1
                ins.then_inc(sem(name), 1)
                dve.wait_ge(sem(name), chained[name])

            def norm(n, gain, split):
                dve.wait_ge(sem("nm_rs"), n + 1)
                for k in range(KD):
                    dve.wait_ge(sem("sp_l"), split_base(split) + k + 1)
                    dve.scalar_tensor_tensor(tmp[:, k % 2, :], xT[:, k, :], v(gain, k), lnb[:, 1, :], ALU.mult, ALU.mult
                                             ).then_inc(sem("sp_t"), 1)

            def add_to_x(name):
                for n in range(KD):
                    tile_done(dve, name, n // 2, n % 2)
                    dve.tensor_tensor(xT[:, n, :], xT[:, n, :], ps[:, bank_of(name, n), :], ALU.add
                                      ).then_inc(sem("x_tile"), 1)

            for k in range(KD):
                dve.wait_ge(sem("x_turned"), k + 1)
                dve.tensor_copy(xT[:, k, :], ps[:, k % 4, :]).then_inc(sem("x_tile"), 1)
            dve.wait_ge(sem("c_loaded"), 32)
            norm(0, "attn_norm", "n0")

            dve.wait_ge(sem("ev_in1"), Z1_TILES + 4)
            for c in range(CV_TILES):
                y, hc = yT[:, SB_PAIRS + CH_PAIRS + c, :], z1[:, GC + c, :]
                chain("cv", dve.tensor_tensor(hc, hc, z1[:, XC + c, :], ALU.mult))
                chain("cv", dve.tensor_scalar(y, hc, v("conv", 3 * c + 2), None, ALU.mult))
                for back in (1, 2):
                    chain("cv", dve.scalar_tensor_tensor(y[:, back:S], hc[:, 0:S - back], v("conv", 3 * c + 2 - back),
                                                         y[:, back:S], ALU.mult, ALU.add))
                dve.tensor_tensor(y, y, z1[:, GB + c, :], ALU.mult).then_inc(sem("cv_y"), 1)

            with dve.Fori(0, SB_PAIRS) as p:
                dve.wait_ge(sem("sb_y"), p + 1)
                dve.tensor_copy(kst, zt(z1, p + KA)).then_inc(sem("sb_staged"), 1)
                dve.tensor_scalar(qst, zt(z1, p + QA), SCALE, None, ALU.mult).then_inc(sem("sb_staged"), 1)
                dve.tensor_copy(vts[:, :], zt(z1, p + VA)).then_inc(sem("sb_staged"), 1)
                for e in range(2):
                    for q, b in enumerate(reversed(range(NT))):
                        dve.wait_ge(sem("sb_l"), p * 8 + (4 * e + q + 1))
                        dve.scalar_tensor_tensor(spl[:, b, 0:S - b * P], ps[:, b, 0:S - b * P], 0.0,
                                                 ab[:, b, 0:S - b * P], ALU.max, ALU.add).then_inc(sem("sb_sp0"), 1)

            dve.wait_ge(sem("sb_y"), SB_PAIRS + 1)
            dve.wait_ge(sem("bt_ready"), 1)
            with dve.Fori(0, CH_PAIRS) as p:
                dve.wait_ge(sem("ch_y"), p + 1)
                dve.tensor_copy(cvts[:, :], zt(z1, p + VB)).then_inc(sem("ch_vs"), 1)
                for w, (src, dst, gain) in enumerate(((QB, cqst, "qn"), (KB, ckst, "kn"))):
                    dve.wait_ge(sem("ch_rs"), p * 2 + (w + 1))
                    dve.scalar_tensor_tensor(dst[:, :], zt(z1, p + src), v(gain), lnb[:, w, :], ALU.mult, ALU.mult
                                             ).then_inc(sem("ch_qk"), 1)

                def shifted(s):
                    e, i = s // 4, s % 4
                    w = (i + 1) * P
                    bias = bt[:, bass.ds(p * 2 + e, 1), (3 - i) * P:S].rearrange("p a n -> p (a n)")
                    dve.wait_ge(sem("ch_sc"), p * 8 + (s + 1))
                    dve.scalar_tensor_tensor(csc[:, s % 2, 0:w], ps[:, s % 2, 0:w], SCALE, bias, ALU.mult, ALU.add
                                             ).then_inc(sem("ch_s"), 1)
                    dve.wait_ge(sem("ch_s"), p * 8 + (s + 3))
                    dve.tensor_reduce(cstat[:, s % 2, 0:1], csc[:, s % 2, 0:w], AX_X, ALU.max, negate=True
                                      ).then_inc(sem("ch_m"), 1)

                def divided(s):
                    w = (s % 4 + 1) * P
                    dve.wait_ge(sem("ch_e"), p * 8 + (s + 1))
                    dve.reciprocal(cstat[:, s % 2, 2:3], cstat[:, s % 2, 1:2]).then_inc(sem("ch_r"), 1)
                    dve.wait_ge(sem("ch_r"), p * 8 + (s + 1))
                    dve.tensor_scalar(cpr[:, s % 2, 0:w], cpr[:, s % 2, 0:w], cstat[:, s % 2, 2:3], None, ALU.mult
                                      ).then_inc(sem("ch_p"), 1)

                shifted(0)
                for s in range(8):
                    if s < 7:
                        shifted(s + 1)
                    divided(s)

            for j in range(KD):
                dve.wait_ge(sem("gn_rs"), j + 1)
                dve.wait_ge(sem("sp_l"), split_base("gn") + j + 1)
                dve.scalar_tensor_tensor(tmp[:, j % 2, :], yT[:, j, :], v("out_norm", j), lnb[:, 1, :], ALU.mult,
                                         ALU.mult).then_inc(sem("sp_t"), 1)
            add_to_x("out1")
            norm(1, "ffn_norm", "n1")
            with dve.Fori(0, FF_TILES // 2) as i:
                for q in range(2):
                    if q:
                        dve.wait_ge(sem("w_used"), i * 2 + (FIRST["ffn"] + 4))
                    else:
                        dve.wait_ge(sem("mm_u"), i + 1)
                    dve.wait_ge(sem("ffn_g"), i * 2 + (q + 3))
                    dve.wait_ge(sem("hid_l"), i * 2 + (q + 1))
                    dve.tensor_tensor(hid[:, q, :], sg[:, q, :], ps[:, 2 + q, :], ALU.mult).then_inc(sem("ffn_u"), 1)
            dve.wait_ge(sem("w_used"), FIRST["in2"] + 2)
            for k in range(KD):
                dve.tensor_tensor(xT[:, k, :], xT[:, k, :], ps[:, k, :], ALU.add).then_inc(sem("x_tile"), 1)
            norm(2, "norm1", "n2")

            dve.wait_ge(sem("pos_loaded"), 16)
            two_pi = 2.0 * np.pi
            part1 = 6.28125
            part2 = float((np.array([two_pi - part1], np.float32).view(np.uint32) & np.uint32(0xFFFFF000))
                          .view(np.float32)[0])
            part3 = float(np.float32(two_pi - part1 - part2))
            to_whole = 1.5 * 2.0 ** 23
            limit = 3.1415925
            chain("rp", dve.tensor_copy(rt, pos_i[:, :]))
            chain("rp", dve.tensor_scalar(rt, rt, v("inv"), None, ALU.mult))
            for q, shift in ((0, np.pi / 2), (1, 0.0)):
                a = csin[:, q, :]
                chain("rp", dve.tensor_scalar(rq, rt, 1.0 / two_pi, shift / two_pi, ALU.mult, ALU.add))
                chain("rp", dve.tensor_scalar(rq, rq, to_whole, None, ALU.add))
                chain("rp", dve.tensor_scalar(rq, rq, -to_whole, None, ALU.add))
                chain("rp", dve.scalar_tensor_tensor(a, rq, -part1, rt, ALU.mult, ALU.add))
                chain("rp", dve.scalar_tensor_tensor(a, rq, -part2, a, ALU.mult, ALU.add))
                chain("rp", dve.scalar_tensor_tensor(a, rq, -part3, a, ALU.mult, ALU.add))
                chain("rp", dve.tensor_scalar(a, a, float(shift), limit, ALU.add, ALU.min))
                chain("rp", dve.tensor_scalar(a, a, -limit, None, ALU.max))
            dve.sem_inc(sem("rp_a"), 1)

            with dve.Fori(0, KD // 2) as i:
                dve.wait_ge(sem("ev_in2"), i * 2 + (GATE + 2 + 4))
                steps = TAPS + 1
                for q in range(2):
                    j = i * 2 + q
                    dve.tensor_tensor(zt(z2, j), zt(z2, j), zt(z2, j + GATE), ALU.mult).then_inc(sem(f"cv2_{q}"), 1)
                for back in range(TAPS):
                    for q in range(2):
                        j = i * 2 + q
                        w = vd("conv2", j * TAPS + (TAPS - 1 - back))
                        acc, u = zt(z2, j + GATE), zt(z2, j)
                        dve.wait_ge(sem(f"cv2_{q}"), i * steps + (back + 1))
                        if back == 0:
                            dve.tensor_scalar(acc, u, w, vd("conv2_b", j), ALU.mult, ALU.add
                                              ).then_inc(sem(f"cv2_{q}"), 1)
                        else:
                            dve.scalar_tensor_tensor(acc[:, back:S], u[:, 0:S - back], w, acc[:, back:S],
                                                     ALU.mult, ALU.add).then_inc(sem(f"cv2_{q}"), 1)
                for q in range(2):
                    dve.wait_ge(sem(f"cv2_{q}"), i * steps + steps)
                    dve.sem_inc(sem("cv2_y"), 1)

            dve.wait_ge(sem("ln_m"), 1)
            for j in range(KD):
                dve.tensor_tensor(z2[:, GATE + j, :], z2[:, GATE + j, :], ps[:, 6, :], ALU.subtract
                                  ).then_inc(sem("ln_x"), 1)
            dve.wait_ge(sem("ln_rs"), 1)
            for j in range(KD):
                dve.wait_ge(sem("ln_sq"), j + 1)
                dve.tensor_tensor(z2[:, GATE + j, :], z2[:, GATE + j, :], lnb[:, 1, :], ALU.mult
                                  ).then_inc(sem("ln_n"), 1)

            for n in range(KD):
                tile_done(dve, "co", n // 2, n % 2)
                dve.tensor_tensor(z2[:, GCONV + n, :], z2[:, GCONV + n, :], ps[:, bank_of("co", n), :], ALU.mult
                                  ).then_inc(sem("ev_co"), 1)

            dve.wait_ge(sem("rp_s"), 1)
            dve.wait_ge(sem("rk_mm"), 1)
            chain("rk", dve.tensor_tensor(rq, z2[:, K2, :], csin[:, 0, :], ALU.mult))
            chain("rk", dve.tensor_tensor(rt, ps[:, 6, :], csin[:, 1, :], ALU.mult))
            chain("rk", dve.tensor_tensor(rq, rq, rt, ALU.add))
            for kv in range(2):
                for e in range(2):
                    dve.tensor_copy(kdup[HD * e:HD * e + HD, kv, :], rq[HD * kv:HD * kv + HD, :]
                                    ).then_inc(sem("kd"), 1)
            dve.wait_ge(sem("kd"), 4)
            dve.wait_ge(sem("msk"), 3)
            with dve.Fori(0, SWA_PAIRS) as p:
                dve.wait_ge(sem("rq_mm"), p + 1)
                dve.wait_ge(sem("sw_y"), p + 1)
                dve.tensor_tensor(rt, ps[:, 6, :], csin[:, 1, :], ALU.mult).then_inc(sem("rq_a"), 1)
                dve.tensor_tensor(rq, zt(z2, p + Q2), csin[:, 0, :], ALU.mult).then_inc(sem("rq_a"), 1)
                dve.wait_ge(sem("rq_a"), p * 2 + 2)
                dve.tensor_tensor(rq, rq, rt, ALU.add).then_inc(sem("rq"), 1)

                def shifted(s):
                    e, i = s // 4, s % 4
                    w = P if i == 0 else 2 * P
                    st = sstat[:, s % 2, :]
                    dve.wait_ge(sem("sw_sc"), p * 8 + (s + 1))
                    dve.scalar_tensor_tensor(ssc[:, s % 2, 0:w], ps[:, s % 2, 0:w], SCALE, msk[:, 2 * P - w:2 * P],
                                             ALU.mult, ALU.add).then_inc(sem("sw_s"), 1)
                    dve.tensor_copy(st[:, 5:6], vd("sinks", p * 2 + e)).then_inc(sem("sw_k"), 1)
                    dve.wait_ge(sem("sw_s"), p * 8 + (s + 3))
                    dve.tensor_reduce(st[:, 3:4], ssc[:, s % 2, 0:w], AX_X, ALU.max).then_inc(sem("sw_x"), 1)
                    dve.wait_ge(sem("sw_x"), p * 8 + (s + 1))
                    dve.wait_ge(sem("sw_k"), p * 8 + (s + 1))
                    dve.tensor_scalar(st[:, 0:1], st[:, 3:4], st[:, 5:6], -1.0, ALU.max, ALU.mult
                                      ).then_inc(sem("sw_m"), 1)

                def divided(s):
                    w = P if s % 4 == 0 else 2 * P
                    st = sstat[:, s % 2, :]
                    dve.wait_ge(sem("sw_e"), p * 16 + (2 * s + 2))
                    dve.tensor_tensor(st[:, 4:5], st[:, 1:2], st[:, 2:3], ALU.add).then_inc(sem("sw_r"), 1)
                    dve.wait_ge(sem("sw_r"), p * 16 + (2 * s + 1))
                    dve.reciprocal(st[:, 6:7], st[:, 4:5]).then_inc(sem("sw_r"), 1)
                    dve.wait_ge(sem("sw_r"), p * 16 + (2 * s + 2))
                    dve.tensor_scalar(spr[:, s % 2, 0:w], spr[:, s % 2, 0:w], st[:, 6:7], None, ALU.mult
                                      ).then_inc(sem("sw_p"), 1)

                shifted(0)
                for s in range(8):
                    if s < 7:
                        shifted(s + 1)
                    divided(s)

            for n in range(KD):
                tile_done(dve, "ao", n // 2, n % 2)
                dve.tensor_tensor(z2[:, GATTN + n, :], z2[:, GATTN + n, :], ps[:, bank_of("ao", n), :], ALU.mult
                                  ).then_inc(sem("ev_ao"), 1)
            dve.wait_ge(sem("w_used"), FIRST["out2"] + 2)
            for n in range(KD):
                dve.wait_ge(sem("ev_ao"), 4 + n + 1)
                dve.wait_ge(sem("sp_l"), split_base("mg") + n + 1)
                dve.tensor_tensor(tmp[:, n % 2, :], z2[:, GATTN + n, :], z2[:, GCONV + n, :], ALU.add
                                  ).then_inc(sem("sp_t"), 1)
            add_to_x("out2")
            norm(3, "norm2", "n3")

            flat = sc[:, :, :].rearrange("p a n -> p (a n)")
            cand = flat.rearrange("p (h c) -> p h c", h=4)
            cand4 = flat.rearrange("p (h i j) -> p h i j", h=4, i=TOPK)
            pairs = top[:, :, :].rearrange("p (h c) k -> p h c k", c=2)
            keys = topf[:, :, :].rearrange("p (h c) k -> p h c k", c=2)
            grid = [P, 4, TOPK, TOPK]

            def unit(t, half, count):
                steps = 0

                def step(ins):
                    nonlocal steps
                    steps += 1
                    ins.then_inc(sem("tk"), 1)

                def settle():
                    pass_by(dve, "tk", count + steps)

                def sixteen(rows, vals, idx, n):
                    for a in range(n):
                        step(dve.max(out=vals[:, a, 0:8], in_=rows[:, a, :]))
                    settle()
                    for a in range(n):
                        step(dve.max_index(idx[:, a, 0:8], vals[:, a, 0:8], rows[:, a, :]))
                    settle()
                    for a in range(n):
                        step(dve.match_replace(out=rows[:, a, :], in_to_replace=vals[:, a, 0:8],
                                               in_values=rows[:, a, :], imm_value=-3.0e38))
                    settle()
                    for a in range(n):
                        step(dve.max(out=vals[:, a, 8:16], in_=rows[:, a, :]))
                    settle()
                    for a in range(n):
                        step(dve.max_index(idx[:, a, 8:16], vals[:, a, 8:16], rows[:, a, :]))
                    settle()

                pass_by(dve, "sc_in", t * 32 + (16 * half + 16))
                sixteen(sc, top, topi, 8)
                step(dve.tensor_copy(topf[:, :, :], topi[:, :, :]))
                step(dve.tensor_tensor(cand4, pairs[:, :, 0, :].unsqueeze(3).to_broadcast(grid),
                                       pairs[:, :, 1, :].unsqueeze(2).to_broadcast(grid), ALU.add))
                settle()
                sixteen(cand, best, bpos, 4)
                where = bpos[:, :, :].rearrange("p h k -> p (h k)")
                step(dve.tensor_scalar(bab[:, 0, :], where, 4, None, ALU.logical_shift_right))
                step(dve.tensor_scalar(bab[:, 1, :], where, TOPK - 1, None, ALU.bitwise_and))
                settle()
                step(dve.tensor_copy(bfl[:, :, :], bab[:, :, :]))
                settle()
                chosen = sel[:, bass.ds(t, 1), :, half * 4 * TOPK:(half + 1) * 4 * TOPK].rearrange(
                    "p t a s -> p (t a) s")
                for c in range(2):
                    at = bfl[:, c, :].rearrange("p (h k) -> p h k", h=4)
                    step(dve.tensor_tensor(cand4, at.unsqueeze(3).to_broadcast(grid),
                                           iota[:, 0:TOPK].unsqueeze(1).unsqueeze(1).to_broadcast(grid),
                                           ALU.is_equal))
                    settle()
                    step(dve.tensor_tensor(cand4, cand4, keys[:, :, c, :].unsqueeze(2).to_broadcast(grid), ALU.mult))
                    settle()
                    step(dve.tensor_reduce(chosen[:, c, :], flat.rearrange("p (s j) -> p s j", j=TOPK), AX_X, ALU.add))
                    settle()
                step(dve.tensor_tensor(chosen[:, 2, :].rearrange("p (h k) -> p h k", h=4), best[:, :, :],
                                       best[:, :, 0:1].to_broadcast([P, 4, TOPK]), ALU.subtract))
                settle()
                dve.sem_inc(sem("tk_unit"), 1)
                return steps

            UNIT_STEPS = 5 * 8 + 2 + 5 * 4 + 3 + 6 + 1
            with dve.Fori(0, NT) as t:
                for half in range(2):
                    n = unit(t, half, t * (2 * UNIT_STEPS) + half * UNIT_STEPS)
                    assert n == UNIT_STEPS
            dve.wait_ge(sem("gt_e"), 1)
            gates = sel[:, :, 2, :].rearrange("p t (h k) -> p t h k", k=TOPK)
            sums = den[:, 0, :].rearrange("p (t h) -> p t h", t=NT)
            rec = den[:, 1, :].rearrange("p (t h) -> p t h", t=NT)
            chain("gt_s", dve.tensor_reduce(sums, gates, AX_X, ALU.add))
            chain("gt_s", dve.reciprocal(rec, sums))
            dve.tensor_tensor(gates, gates, rec.unsqueeze(3).to_broadcast([P, NT, PH, TOPK]), ALU.mult
                              ).then_inc(sem("gt"), 1)

            for grp in range(GROUPS):
                e0, n0 = grp * EG, grp * (S // TB)

                def hot1(n, r):
                    grid1 = [P, TB, EG]
                    dve.wait_ge(sem("g_mm"), n + (n0 + 1))
                    dve.tensor_tensor(oh1[:, r, :, :], iota[:, e0:e0 + EG].unsqueeze(1).to_broadcast(grid1),
                                      slot_t[:, 0, bass.ds(n * TB, TB)].unsqueeze(2).to_broadcast(grid1),
                                      ALU.is_equal).then_inc(sem("oh1"), 1)
                    dve.wait_ge(sem("oh1"), n * 2 + (2 * n0 + 1))
                    dve.tensor_tensor(oh1[:, r, :, :], oh1[:, r, :, :],
                                      slot_t[:, 2, bass.ds(n * TB, TB)].unsqueeze(2).to_broadcast(grid1),
                                      ALU.mult).then_inc(sem("oh1"), 1)

                def weigh(n, r):
                    dve.wait_ge(sem("g_mm"), n + (n0 + 3))
                    at = ga[:, :, bass.ds(n * TB, TB)]
                    dve.tensor_tensor(at, at, ps[:, r, :].rearrange("p (t e) -> p e t", t=TB), ALU.mult
                                      ).then_inc(sem("g_mul"), 1)

                def low_v(e, r):
                    dve.wait_ge(sem("v_hi"), e * 2 + (2 * e0 + 2))
                    dve.tensor_tensor(gal[:, r, :], zt(ga, e), gah[:, r, :].bitcast(F32), ALU.subtract
                                      ).then_inc(sem("ga_lo"), 1)
                    dve.tensor_tensor(el[:, r, :], er[:, r, :], eh[:, r, :].bitcast(F32), ALU.subtract
                                      ).then_inc(sem("v_lo"), 1)

                dve.wait_ge(sem("slot_t"), 3)
                if grp:
                    dve.wait_ge(sem("a_ev"), e0 + EG + 2)
                hot1(0, 0)
                with dve.Fori(0, S // TB // 2 - 1) as i:
                    for r in range(2):
                        hot1(i * 2 + (r + 1), (r + 1) % 2)
                        weigh(i * 2 + r, r)
                hot1(S // TB - 1, 1)
                weigh(S // TB - 2, 0)
                weigh(S // TB - 1, 1)
                rolled(dve, EG, 2, low_v)
                dve.wait_ge(sem("v_used"), e0 + EG + 2)
                if grp == 0:
                    for c in range(KD):
                        dve.tensor_copy(ga[:, c, :], ps[:, c, :]).then_inc(sem("e_part"), 1)
            dve.wait_ge(sem("x_back"), 32)
            for c in range(KD):
                dve.tensor_tensor(pf[:, c, :], pf[:, c, :], ps[:, c, :], ALU.add).then_inc(sem("y_part"), 1)
            for c in range(KD):
                dve.wait_ge(sem("y_part"), c + 1)
                dve.tensor_tensor(xf[:, c, :], xf[:, c, :], pf[:, c, :], ALU.add).then_inc(sem("y_sum"), 1)
            dve.wait_ge(sem("nm_rs"), 5)
            for k in range(KD):
                dve.scalar_tensor_tensor(pf[:, k, :], xf[:, k, :], v("final", k), fln[:, 1, :], ALU.mult, ALU.mult
                                         ).then_inc(sem("y_t"), 1)
            for k in range(KD):
                dve.wait_ge(sem("y_turned"), k + 1)
                dve.tensor_copy(xo[:, :, k * P:k * P + P], ps[:, k % 4, :].rearrange("p (t n) -> p t n", t=NT)
                                ).then_inc(sem("o_ready"), 1)


def constants():
    i = np.arange(P)
    same64 = (i[:, None] // HD == i[None, :] // HD).astype(np.float32)
    half = HD // 2
    turn = np.zeros((P, P), np.float32)
    for m in range(P):
        if m % HD < half:
            turn[m + half, m] = -1.0
        else:
            turn[m - half, m] = 1.0
    tables = {
        "ident": np.eye(P, dtype=np.float32),
        "blk64": same64 / HD,
        "mean": np.full((P, P), 1.0 / D, np.float32),
        "negtri": -(i[:, None] >= i[None, :]).astype(np.float32),
        "negone": np.full((P, P), -1.0, np.float32),
        "rot": turn,
        "iota": np.broadcast_to(i.astype(np.float32)[None, :], (P, P)),
    }
    return np.ascontiguousarray(np.stack([tables[n] for n in CST], axis=1).astype(np.float32))


def kernel(**inputs):
    import concourse.bacc as bacc
    from concourse.bass_utils import run_bass_kernel_spmd

    a = {k: np.asarray(x) for k, x in inputs.items()}

    def cols(x):
        return x.reshape(-1, P).T

    half = HD // 2
    inv = 10000.0 ** (-(np.arange(half, dtype=np.float32) * np.float32(2.0) / np.float32(HD)))
    packed = {
        "attn_norm": cols(a["attn_norm_w"][0]), "ffn_norm": cols(a["ffn_norm_w"][0]), "norm1": cols(a["norm1_g_2"][0]),
        "norm2": cols(a["norm2_g_2"][0]), "final": cols(a["final_g_2"]), "out_norm": cols(a["out_norm_w"][0]),
        "qn": np.tile(a["q_norm_w"][0], 2)[:, None], "kn": np.tile(a["k_norm_w"][0], 2)[:, None],
        "conv": a["conv_w"][0].reshape(3, CV_TILES, P).transpose(2, 1, 0).reshape(P, -1),
        "b_in": cols(a["b_in_2"][0]),
        "conv2": a["conv_w_2"][0].reshape(TAPS, KD, P).transpose(2, 1, 0).reshape(P, -1),
        "conv2_b": cols(a["conv_b_2"][0]), "ln_g": cols(a["conv_ln_g_2"][0]), "ln_b": cols(a["conv_ln_b_2"][0]),
        "sinks": np.tile(a["attn_sinks_2"], (P, 1)),
        "inv": np.tile(inv.astype(np.float32), P // half)[:, None],
        "eps": np.full((P, 1), EPS, np.float32), "one": np.ones((P, 1), np.float32),
    }
    vec = np.concatenate([packed[n] for n, _ in VECS], axis=1)
    assert vec.shape == (P, NVEC)
    far = np.clip(S - P + np.arange(P)[:, None] - np.arange(S)[None, :], -P, P) + P
    arrays = {
        "x": a["x"][0], "cst": constants(), "vec": vec, "rel_tiles": a["rel_bias"][0][:, far],
        "positions": np.tile(a["positions_2"], (P, 1)), "peer_sub_keys_2": a["peer_sub_keys_2"][0].reshape(HC, NKEYS, P),
    }
    for name in ("w_in", "w_out", "w_gate", "w_up", "w_down", "w_in_2", "w_conv_out_2", "w_attn_o_2", "w_out_2",
                 "w_peer_q_2", "peer_u_2", "peer_v_2"):
        arrays[name] = a[name][0]
    arrays = {f"in_{n}": np.ascontiguousarray(x) for n, x in arrays.items()}

    nc = bacc.Bacc("TRN2", target_bir_lowering=False, num_devices=1)
    ins = {n[3:]: nc.dram_tensor(n, x.shape, mybir.dt.from_np(x.dtype), kind="ExternalInput").ap()
           for n, x in arrays.items()}
    out = nc.dram_tensor("out", (S, D), F32, kind="ExternalOutput").ap()
    build(nc, ins, out)
    r = run_bass_kernel_spmd(nc, [arrays], core_ids=[0])
    return r.results[0]["out"].reshape(1, S, D)
```

```python
from contextlib import ExitStack

import concourse.bass as bass
import numpy as np
from concourse import mybir

F32 = mybir.dt.float32
F32R = mybir.dt.float32r
BF16 = mybir.dt.bfloat16
I32 = mybir.dt.int32
U32 = mybir.dt.uint32
ALU = mybir.AluOpType
ACT = mybir.ActivationFunctionType
AX_X = mybir.AxisListType.X

P = 128
S = 512
D = 1024
KD = D // P
NT = S // P
EPS = 1e-6
HD = 64
SCALE = HD ** -0.5
NEG = -1e30

SB_PAIRS, CH_PAIRS, CV_TILES = 2, 4, 2
QA, KA, VA = 0, 2, 4
QB, KB, VB = 6, 10, 14
GB, GC, XC = 18, 20, 22
Z1_TILES = 24
FF_TILES = 22

VAL, GATE, Q2, K2, V2, GCONV, GATTN = 0, 8, 16, 24, 25, 26, 34
Z2_TILES = 42
TAPS = 31
SWA_PAIRS = 8
PAIRS_PER_KV = 4
STEPS = 2 * NT

PH = 8
HC = 2 * PH
NKEYS = 128
TOPK = 16
GROUPS = 2
EG = NKEYS // GROUPS
TB = 8

SLOTS = [("in1", Z1_TILES // 2), ("out1", 4), ("ffn", FF_TILES), ("down", FF_TILES // 2),
         ("in2", Z2_TILES // 2), ("co", 4), ("ao", 4), ("out2", 4), ("pq", 8)]
FIRST = {}
_at = 0
for _n, _c in SLOTS:
    FIRST[_n] = _at
    _at += _c
N_SLOTS = _at
COUNT = dict(SLOTS)

CST = ["ident", "mean", "iota", "blk64", "negtri", "negone", "rot"]
VECS = [("attn_norm", 8), ("ffn_norm", 8), ("norm1", 8), ("norm2", 8), ("final", 8), ("out_norm", 8),
        ("qn", 1), ("kn", 1), ("conv", 6), ("b_in", Z2_TILES), ("conv2", TAPS * 8), ("conv2_b", 8),
        ("ln_g", 8), ("ln_b", 8), ("sinks", 16), ("inv", 1), ("eps", 1), ("one", 1)]
VAT = {}
_at = 0
for _n, _c in VECS:
    VAT[_n] = _at
    _at += _c
NVEC = _at

SPLITS = ["n0", "gn", "n1", "n2", "ln", "at", "mg", "n3"]


def rolled(eng, n, unroll, body):
    full = n // unroll
    if full > 1:
        with eng.Fori(0, full) as i:
            for r in range(unroll):
                body(i * unroll + r, r)
    elif full == 1:
        for r in range(unroll):
            body(r, r)
    for r in range(n - full * unroll):
        body(full * unroll + r, r)


def build(nc, ins, out):
    with ExitStack() as ctx:
        def sb(name, shape, dt=F32):
            return ctx.enter_context(nc.sbuf_tensor(name, shape, dt))

        sems = {}

        def sem(name):
            if name not in sems:
                sems[name] = ctx.enter_context(nc.semaphore(name))
            return sems[name]

        cst = sb("cst", [P, len(CST), P])
        vec = sb("vec", [P, NVEC])
        ident, mean, iota, blk64, negtri, negone, rot = (cst[:, i, :] for i in range(len(CST)))

        def v(name, i=0, n=1):
            return vec[:, VAT[name] + i:VAT[name] + i + n]

        def vd(name, i, n=1):
            return vec[:, VAT[name]:VAT[name] + dict(VECS)[name]][:, bass.ds(i, n)]

        ps = ctx.enter_context(nc.psum_tensor("ps", [P, 8, S], F32))
        hh = sb("hh", [P, KD, S], F32R)
        hl = sb("hl", [P, KD, S], F32R)

        early = ExitStack()

        def esb(name, shape, dt=F32, stack=None):
            return (stack or early).enter_context(nc.sbuf_tensor(name, shape, dt))

        xT = esb("xT", [P, KD, S])
        raw = esb("raw", [P, 2, 2048])
        wh = esb("wh", [P, 2, 2048], F32R)
        wl = esb("wl", [P, 2, 2048], F32R)
        tmp = esb("tmp", [P, 2, S])
        sqb = esb("sqb", [P, 2, S])
        lnb = esb("lnb", [P, 2, S])

        one = ExitStack()
        z1 = esb("z1", [P, Z1_TILES, S], stack=one)
        yT = esb("yT", [P, KD, S], stack=one)
        bt = esb("bt", [P, 8, S], stack=one)
        kst, qst = tmp[:, 0, :], tmp[:, 1, :]
        spl = yT[:, SB_PAIRS:SB_PAIRS + NT, :]
        sb_in = ExitStack()
        vts = esb("vts", [P, S], stack=sb_in)
        vst = esb("vst", [P, NT, P], stack=sb_in)
        ab = esb("ab", [P, NT, S], stack=sb_in)
        sb_in.close()
        csc, cpr, cpt = (z1[:, 2 * i:2 * i + 2, :] for i in range(3))
        ch_in = ExitStack()
        ckst = esb("ckst", [P, S], stack=ch_in)
        cqst = esb("cqst", [P, S], stack=ch_in)
        cvts = esb("cvts", [P, S], stack=ch_in)
        cvst = esb("cvst", [P, NT, P], stack=ch_in)
        cstat = esb("cstat", [P, 2, 4], stack=ch_in)
        ch_in.close()
        one.close()

        ffn = ExitStack()
        hidh = esb("hidh", [P, FF_TILES, S], F32R, stack=ffn)
        hidl = esb("hidl", [P, FF_TILES, S], F32R, stack=ffn)
        sg, hid = sqb, tmp
        ffn.close()

        two = ExitStack()
        z2 = esb("z2", [P, Z2_TILES, S], stack=two)
        csin = esb("csin", [P, 2, S], stack=two)
        msk = esb("msk", [P, 2 * P], stack=two)
        sstat = esb("sstat", [P, 2, 16], stack=two)
        nsink = esb("nsink", [P, 2 * SWA_PAIRS], stack=two)
        pos_in = ExitStack()
        pos_i = esb("pos_i", [P, S], I32, stack=pos_in)
        pos_in.close()
        kdup = esb("kdup", [P, 2, S], stack=two)
        rq = sqb
        rt = z2[:, GATE + 6:GATE + 8, :]
        ssc, spr, spt = (z2[:, GATE + 2 * i:GATE + 2 * i + 2, :].rearrange("p r (e n) -> p r e n", e=2)
                         for i in range(3))
        vn_pairs = tmp[:, :, 2 * P:4 * P]
        two.close()

        rout = ExitStack()
        qT = esb("qT", [P, HC, S], stack=rout)
        skT = esb("skT", [P, HC, P], stack=rout)
        scev = esb("scev", [P, 2, 4, P], stack=rout)
        rout.close()
        early.close()

        late = ExitStack()
        ga = esb("ga", [P, EG, S], stack=late)
        er = esb("er", [P, 2, D], stack=late)
        slot_t = esb("slot_t", [P, 5, S], BF16, stack=late)
        gate_t = cst[:, CST.index("blk64"):, :].rearrange("p a n -> p (a n)")
        uv = ExitStack()
        eh = esb("eh", [P, 2, D], F32R, stack=uv)
        el = esb("el", [P, 2, D], F32R, stack=uv)
        tk = ExitStack()
        sc = esb("sc", [P, 8, NKEYS], stack=tk)
        top = esb("top", [P, 8, TOPK], stack=tk)
        topi = esb("topi", [P, 8, TOPK], U32, stack=tk)
        topf = esb("topf", [P, 8, TOPK], stack=tk)
        best = esb("best", [P, 4, TOPK], stack=tk)
        bpos = esb("bpos", [P, 4, TOPK], U32, stack=tk)
        sel = esb("sel", [P, NT, 3, PH * TOPK], stack=tk)
        bab = esb("bab", [P, 2, 4 * TOPK], U32, stack=tk)
        bfl = esb("bfl", [P, 2, 4 * TOPK], stack=tk)
        den = esb("den", [P, 2, NT * PH], stack=tk)
        tk.close()
        gv = ExitStack()
        gah = esb("gah", [P, 2, S], F32R, stack=gv)
        gal = esb("gal", [P, 2, S], F32R, stack=gv)
        gv.close()
        uv.close()
        oh = ExitStack()
        rest = esb("rest", [P, 2, S], stack=oh)
        oh.close()
        iota_t = esb("iota_t", [P, NKEYS, TB], BF16, stack=oh)
        oh2 = esb("oh2", [P, 4, NKEYS, TB], BF16, stack=oh)
        eq1 = esb("eq1", [P, 4, EG, TB], BF16, stack=oh)
        oh1 = esb("oh1", [P, 4, 3, EG, TB], BF16, stack=oh)
        oh.close()
        late.close()
        xf, pf = ga[:, 0:KD, :], ga[:, KD:2 * KD, :]
        fsq, fln = ga[:, 2 * KD:2 * KD + 2, :], ga[:, 2 * KD + 2:2 * KD + 4, :]

        x_dram = nc.dram_tensor("x_spill", [P, KD, S], F32).ap()
        e_dram = nc.dram_tensor("expert_spill", [P, KD, S], F32).ap()
        sc_dram = nc.dram_tensor("score_spill", [2 * NT, P, PH, NKEYS], F32).ap()

        u_tiles, v_tiles = ins["u_tiles"], ins["v_tiles"]

        def piece(w, b, k, half):
            return w[:, b, :].rearrange("p (k n) -> p k n", k=KD)[:, k, half * P:half * P + P]

        def piece_down(w, b, j, c):
            return w[:, b, :].rearrange("p (j n) -> p j n", j=2)[:, j, c * P:c * P + P]

        def vn(t):
            return vn_pairs[:, t // 2, (t % 2) * P:(t % 2) * P + P]

        def split_base(name):
            return 8 * SPLITS.index(name)

        block = ctx.enter_context(nc.Block())

        def zt(z, n):
            return z[:, bass.ds(n, 1), :].rearrange("p a n -> p (a n)")

        def tile_done(eng, name, s, half):
            if half:
                eng.wait_ge(sem("w_used"), s + (FIRST[name] + 3))
            else:
                eng.wait_ge(sem("mm_" + name), s + 1)

        def pass_by(eng, signal, count):
            eng.wait_ge(sem(signal), count)
            eng.sem_inc(sem("waits_past"), 1)

        def all_steps(eng, rounds, step):
            with eng.Fori(0, rounds - 1) as j:
                for r in range(STEPS):
                    step(j, r, False)
            for r in range(STEPS):
                step(rounds - 1, r, True)

        def ahead(j, r, n):
            return (j + 1, r + n - STEPS) if r + n >= STEPS else (j, r + n)

        def swa_cols(r):
            return P if r % NT == 0 else 0

        def bank_of(name, n):
            return (2 * FIRST[name] + n) % 4

        @block.sync
        def _(sp):
            sp.dma_start(xT[:, :, :], ins["x"]).then_inc(sem("x_loaded"), 16)

            def load(g, b):
                sp.wait_ge(sem("w_lo"), g + 1)
                sp.dma_start(raw[:, b, :], ins["w_slots"][bass.ds(g, 1), :, :].rearrange("g p n -> p (g n)")
                             ).then_inc(sem(f"w_raw{b}"), 16)

            rolled(sp, N_SLOTS, 2, load)
            sp.wait_ge(sem("x_tile"), 8 * 4)
            sp.dma_start(x_dram, xT[:, :, :]).then_inc(sem("x_spilled"), 16)
            sp.dma_start(skT[:, :, :], ins["sub_keys"]).then_inc(sem("sk_loaded"), 16)
            for n in range(NT * 4):
                sp.wait_ge(sem("sc_copied"), n + 1)
                sp.dma_start(sc_dram[n // 2, :, 4 * (n % 2):4 * (n % 2) + 4, :], scev[:, n % 2, :, :]
                             ).then_inc(sem(f"sc_out{n % 2}"), 16)
            sp.wait_ge(sem("sc_out0"), 16 * 2 * NT)
            sp.wait_ge(sem("sc_out1"), 16 * 2 * NT)
            sp.wait_ge(sem("x_spilled"), 16)
            sp.sem_inc(sem("late_free"), 1)
            for grp in range(GROUPS):
                e0 = grp * EG

                def load_u(e, r):
                    sp.wait_ge(sem("u_lo"), e + (e0 + 1))
                    sp.dma_start(er[:, r, :], u_tiles[bass.ds(e + e0, 1), :, :].rearrange("e p n -> p (e n)")
                                 ).then_inc(sem(f"u_in{r}"), 16)

                def load_v(e, r):
                    sp.wait_ge(sem("v_lo"), e + (e0 + 1))
                    sp.dma_start(er[:, r, :], v_tiles[bass.ds(e + e0, 1), :, :].rearrange("e p n -> p (e n)")
                                 ).then_inc(sem(f"v_in{r}"), 16)

                if grp:
                    sp.wait_ge(sem("v_lo"), e0 + 2)
                    rolled(sp, EG, 2, load_u)
                else:
                    with sp.Fori(0, 2 * NT) as m:
                        sp.wait_ge(sem("tk_unit"), m + 1)
                        sp.dma_start(sc[:, :, :], sc_dram[bass.ds(m, 1), :, :, :].rearrange("m p a n -> p (m a) n")
                                     ).then_inc(sem("sc_in"), 16)
                        for j in range(EG // (2 * NT)):
                            load_u(m * (EG // (2 * NT)) + j, j % 2)
                sp.wait_ge(sem("u_lo"), e0 + EG + 2)
                rolled(sp, EG, 2, load_v)
                if grp == 0:
                    sp.wait_ge(sem("e_part"), KD)
                    sp.dma_start(e_dram, ga[:, 0:KD, :]).then_inc(sem("e_spilled"), 16)
            sp.wait_ge(sem("v_used"), (GROUPS - 1) * EG + 2 * KD + 4 + 2)
            sp.dma_start(xf, x_dram).then_inc(sem("x_back"), 16)
            sp.dma_start(pf, e_dram).then_inc(sem("x_back"), 16)
            for k in range(KD):
                sp.wait_ge(sem("y_t"), k + 1)
                sp.dma_start(out[:, k, :], pf[:, k, :]).then_inc(sem("out_done"), 16)
            sp.wait_ge(sem("out_done"), 16 * KD)

        @block.gpsimd
        def _(pool):
            for name in ("w_lo", "sp_l", "hid_l", "u_lo"):
                pool.sem_inc(sem(name), 2)
            pool.dma_start(bt[:, :, :], ins["rel_tiles"].rearrange("h p m -> p h m")).then_inc(sem("bt_loaded"), 16)

            def low(g, b):
                pool.wait_ge(sem("w_hi"), g + 1)
                pool.tensor_tensor(wl[:, b, :], raw[:, b, :], wh[:, b, :].bitcast(F32), ALU.subtract
                                   ).then_inc(sem("w_lo"), 1)

            def lows(a, b):
                rolled(pool, b - a, 2, lambda s, r: low(s + a, (a + r) % 2))

            def split_low(name):
                base = split_base(name)
                for k in range(KD):
                    pool.wait_ge(sem("sp_h"), base + k + 1)
                    pool.tensor_tensor(hl[:, k, :], tmp[:, k % 2, :], hh[:, k, :].bitcast(F32), ALU.subtract
                                       ).then_inc(sem("sp_l"), 1)

            lows(0, 2)
            split_low("n0")
            lows(2, FIRST["out1"] + 2)
            pool.wait_ge(sem("bt_loaded"), 16)
            pool.memset(bt[0:64, :, 448:512], NEG).then_inc(sem("bt_ready"), 1)
            with pool.Fori(0, SB_PAIRS) as p:
                for e in range(2):
                    for tile, ready, done in ((spl, "sb_sp0", "sb_sp"), (ab, "sb_w0", "sb_w")):
                        for q, b in enumerate(reversed(range(NT))):
                            pass_by(pool, ready, p * 8 + (4 * e + q + 1))
                            pool.affine_select(out=tile[:, b, 0:P], in_=tile[:, b, 0:P], pattern=[[1, P]],
                                               compare_op=ALU.is_gt, fill=0.0, base=0, channel_multiplier=-1
                                               ).then_inc(sem(done), 1)
            pool.wait_ge(sem("sb_y"), SB_PAIRS + 1)
            with pool.Fori(0, CH_PAIRS) as p:
                pool.wait_ge(sem("ch_vt"), p + 1)
                pool.tensor_copy(cvts[:, :], zt(z1, p + VB)).then_inc(sem("ch_vs"), 1)
            split_low("gn")
            lows(FIRST["out1"] + 2, FIRST["ffn"] + 2)
            split_low("n1")
            with pool.Fori(0, FF_TILES // 2) as i:
                for q in range(2):
                    low(i * 2 + (FIRST["ffn"] + 2 + q), q)
                for q in range(2):
                    pool.wait_ge(sem("hid_h"), i * 2 + (q + 1))
                    pool.tensor_tensor(zt(hidl, i * 2 + q), hid[:, q, :], zt(hidh, i * 2 + q).bitcast(F32),
                                       ALU.subtract).then_inc(sem("hid_l"), 1)
            lows(FIRST["down"] + 2, FIRST["in2"] + 2)
            split_low("n2")
            pool.memset(msk[:, :], 0.0).then_inc(sem("msk"), 1)
            pool.wait_ge(sem("msk"), 1)
            pool.affine_select(out=msk[:, :], in_=msk[:, :], pattern=[[1, 2 * P]], compare_op=ALU.is_gt, fill=NEG,
                               base=0, channel_multiplier=-1).then_inc(sem("msk"), 1)
            pool.wait_ge(sem("msk"), 2)
            pool.affine_select(out=msk[:, :], in_=msk[:, :], pattern=[[-1, 2 * P]], compare_op=ALU.is_ge, fill=NEG,
                               base=P, channel_multiplier=1).then_inc(sem("msk"), 1)
            lows(FIRST["in2"] + 2, FIRST["co"] + 2)
            split_low("ln")
            lows(FIRST["co"] + 2, FIRST["ao"] + 2)
            pool.wait_ge(sem("kd"), 4)

            def rotary(j, kv):
                n = j * 2 + kv
                if not (isinstance(j, int) and j == 0):
                    pool.wait_ge(sem("sw_sc"), (j - 1) * STEPS + (kv * NT + NT))
                pool.wait_ge(sem("rh"), n + 1)
                pool.tensor_tensor(rt[:, kv, :], rt[:, kv, :], csin[:, 1, :], ALU.mult).then_inc(sem("rq_a"), 1)
                pool.tensor_tensor(rq[:, kv, :], zt(z2, j + (Q2 + kv * PAIRS_PER_KV)), csin[:, 0, :], ALU.mult
                                   ).then_inc(sem("rq_a"), 1)
                pool.wait_ge(sem("rq_a"), n * 2 + 2)
                pool.tensor_tensor(rq[:, kv, :], rq[:, kv, :], rt[:, kv, :], ALU.add).then_inc(sem("rq"), 1)

            for kv in range(2):
                rotary(0, kv)
            with pool.Fori(1, PAIRS_PER_KV) as j:
                for kv in range(2):
                    rotary(j, kv)
            split_low("at")
            lows(FIRST["ao"] + 2, FIRST["out2"] + 2)
            split_low("mg")
            lows(FIRST["out2"] + 2, FIRST["pq"] + 2)
            split_low("n3")
            lows(FIRST["pq"] + 2, N_SLOTS)

            for grp in range(GROUPS):
                def low_u(e, r):
                    pool.wait_ge(sem("u_hi"), e + (grp * EG + 1))
                    pool.tensor_tensor(el[:, r, :], er[:, r, :], eh[:, r, :].bitcast(F32), ALU.subtract
                                       ).then_inc(sem("u_lo"), 1)

                def second_part(n, r):
                    gn = n + (grp * (S // TB) + 1)
                    pool.wait_ge(sem("g_mm"), gn)
                    pass_by(pool, "oh1_eq", gn)
                    pool.tensor_tensor(oh1[:, r, 1, :, :], eq1[:, r, :, :],
                                       slot_t[:, 3, bass.ds(n * TB, TB)].unsqueeze(1).to_broadcast([P, EG, TB]),
                                       ALU.mult).then_inc(sem("oh1_2"), 1)

                rolled(pool, EG, 2, low_u)
                pool.wait_ge(sem("gate_p"), 1)
                rolled(pool, S // TB, 4, second_part)

        @block.scalar
        def _(act):
            act.dma_start(cst[:, :, :], ins["cst"]).then_inc(sem("c_loaded"), 16)
            act.dma_start(vec[:, :], ins["vec"]).then_inc(sem("c_loaded"), 16)

            def high(g, b):
                act.wait_ge(sem(f"w_raw{b}"), g * 8 + (16 - 8 * b))
                act.wait_ge(sem("w_used"), g + 1)
                act.activation(wh[:, b, :], raw[:, b, :], ACT.Copy).then_inc(sem("w_hi"), 1)

            def highs(name):
                g0 = FIRST[name]
                rolled(act, COUNT[name], 2, lambda s, r: high(s + (g0 + 2), (g0 + r) % 2))

            def split_high(name):
                base = split_base(name)
                for k in range(KD):
                    act.wait_ge(sem("sp_t"), base + k + 1)
                    act.activation(hh[:, k, :], tmp[:, k % 2, :], ACT.Copy).then_inc(sem("sp_h"), 1)

            def rstd(ms, scratch, dst, done, count):
                act.activation(scratch, ms, ACT.Ln, bias=v("eps")).then_inc(sem(done + "_ln"), 1)
                act.wait_ge(sem(done + "_ln"), count)
                act.activation(dst, scratch, ACT.Exp, scale=-0.5).then_inc(sem(done + "_rs"), 1)

            def norm(n, x, ready, first, sq, ln, bank=4):
                for k in range(KD):
                    act.wait_ge(sem(ready), first + k + 1)
                    act.wait_ge(sem("nm_mm"), 8 * n + k + 1)
                    act.activation(sq[:, k % 2, :], x[:, k, :], ACT.Square).then_inc(sem("nm_sq"), 1)
                act.wait_ge(sem("nm_mm"), 8 * n + 8 + 2)
                rstd(ps[:, bank, :], ln[:, 0, :], ln[:, 1, :], "nm", n + 1)

            def evacuate(name, first, last, tile, ahead=True):
                g0 = FIRST[name]

                def slot(s, r):
                    g = g0 + first // 2 + r
                    for half in range(2):
                        tile_done(act, name, s + first // 2, half)
                        tile(s * 2 + (first + half), 2 * (g % 2) + half)
                    if ahead:
                        high(s + (g0 + first // 2 + 2), g % 2)

                rolled(act, (last - first) // 2, 2, slot)

            def ln_exp_tables():
                act.preload_act_table_set("natural_log_exp_and_others")

            ln_exp_tables()
            high(0, 0)
            high(1, 1)
            act.wait_ge(sem("c_loaded"), 32)
            norm(0, xT, "x_tile", 0, sqb, lnb)
            split_high("n0")

            def z1_tile(n, bank):
                act.activation(zt(z1, n), ps[:, bank, :], ACT.Copy).then_inc(sem("ev_in1"), 1)

            evacuate("in1", 0, Z1_TILES, z1_tile)

            with act.Fori(0, SB_PAIRS) as p:
                act.wait_ge(sem("sb_vt"), p + 1)
                act.activation(vst[:, :, :], ps[:, 5, :].rearrange("p (t n) -> p t n", t=NT), ACT.Copy
                               ).then_inc(sem("sb_v"), 1)
                for e in range(2):
                    if e:
                        act.wait_ge(sem("sb_pv"), p * 2 + 1)
                    for q, b in enumerate(reversed(range(NT))):
                        w = S - b * P
                        n = p * 8 + (4 * e + q + 1)
                        act.wait_ge(sem("sb_z"), n)
                        act.activation(ab[:, b, 0:w], ps[:, b, 0:w], ACT.Abs).then_inc(sem("sb_abs"), 1)
                        act.wait_ge(sem("sb_abs"), n)
                        act.activation(ab[:, b, 0:w], ab[:, b, 0:w], ACT.Exp, scale=-1.0).then_inc(sem("sb_e"), 1)
                        act.wait_ge(sem("sb_e"), n)
                        act.activation(ab[:, b, 0:w], ab[:, b, 0:w], ACT.Ln, bias=v("one")).then_inc(sem("sb_l"), 1)
                    for q, b in enumerate(reversed(range(NT))):
                        w = S - b * P
                        n = p * 8 + (4 * e + q + 1)
                        act.wait_ge(sem("sb_cum"), n)
                        act.activation(ab[:, b, 0:w], ps[:, b, 0:w], ACT.Exp).then_inc(sem("sb_w0"), 1)
                act.wait_ge(sem("sb_pv"), p * 2 + 2)
                act.activation(zt(yT, p), ps[:, 4, :], ACT.Copy).then_inc(sem("sb_y"), 1)

            act.wait_ge(sem("sb_y"), SB_PAIRS + 1)

            def squares(p):
                for w, src in enumerate((QB, KB)):
                    if not (isinstance(p, int) and p == 0):
                        act.wait_ge(sem("ch_ms"), p * 2 + (w - 1))
                    act.activation(sqb[:, w, :], zt(z1, p + src), ACT.Square).then_inc(sem("ch_sq"), 1)

            def rstds(p):
                act.wait_ge(sem("ch_qk"), p * 2 + 2)
                for w in range(2):
                    act.wait_ge(sem("ch_ms"), p * 2 + (w + 1))
                    rstd(ps[:, 6 + w, :], lnb[:, w, :], lnb[:, w, :], "ch", p * 2 + (w + 1))

            def turned_values(p, e):
                act.wait_ge(sem("ch_vt"), p + 2)
                act.wait_ge(sem("ch_o"), p * STEPS + (NT * e + 2 - NT))
                act.activation(cvst[:, :, HD * e:HD * e + HD],
                               ps[:, 5, :].rearrange("p (t n) -> p t n", t=NT)[:, :, HD * e:HD * e + HD], ACT.Copy
                               ).then_inc(sem("ch_v"), 1)

            def weights(p, r):
                w = (r % NT + 1) * P
                act.wait_ge(sem("ch_m"), p * STEPS + (r + 1))
                act.activation(cpr[:, r % 2, 0:w], csc[:, r % 2, 0:w], ACT.Exp, bias=cstat[:, r % 2, 0:1],
                               accum_out=cstat[:, r % 2, 1:2]).then_inc(sem("ch_e"), 1)

            def turned_weights(p, r):
                w = (r % NT + 1) * P
                act.wait_ge(sem("ch_t"), p * STEPS + (r + 1))
                act.wait_ge(sem("ch_o"), p * STEPS + (r + 1))
                act.activation(cpt[:, r % 2, 0:w], ps[:, 2 + r % 2, 0:w], ACT.Copy).then_inc(sem("ch_pt"), 1)

            def head_out(p, e):
                h = slice(HD * e, HD * e + HD)
                act.wait_ge(sem("ch_o"), p * STEPS + (NT * e + NT + 2))
                act.activation(zt(yT, p + SB_PAIRS)[h, :], ps[h, 4, :], ACT.Copy).then_inc(sem("ch_y"), 1)

            def step(p, r, last):
                if not last and r == 1:
                    squares(p + 1)
                if not last and r == 3:
                    rstds(p + 1)
                if not last or r + 1 < STEPS:
                    weights(*ahead(p, r, 1))
                turned_weights(p, r)
                if r == 1:
                    turned_values(p, 1)
                if r == NT + 1:
                    head_out(p, 0)
                    if not last:
                        turned_values(p + 1, 0)
                if r == STEPS - 1:
                    head_out(p, 1)

            squares(0)
            rstds(0)
            act.wait_ge(sem("ch_vt"), 2)
            act.activation(cvst[:, :, 0:HD], ps[:, 5, :].rearrange("p (t n) -> p t n", t=NT)[:, :, 0:HD], ACT.Copy
                           ).then_inc(sem("ch_v"), 1)
            weights(0, 0)
            all_steps(act, CH_PAIRS, step)

            act.wait_ge(sem("cv_y"), CV_TILES)
            act.wait_ge(sem("ch_y"), 2 * CH_PAIRS + 2)
            for j in range(KD):
                act.wait_ge(sem("gn_mm"), j + 1)
                act.activation(sqb[:, j % 2, :], yT[:, j, :], ACT.Square).then_inc(sem("gn_sq"), 1)
                act.wait_ge(sem("gn_mm"), j + 3)
                act.wait_ge(sem("sp_t"), split_base("gn") + j)
                rstd(ps[:, 4 + j % 2, :], lnb[:, 0, :], lnb[:, 1, :], "gn", j + 1)
                act.wait_ge(sem("sp_t"), split_base("gn") + j + 1)
                act.activation(hh[:, j, :], tmp[:, j % 2, :], ACT.Copy).then_inc(sem("sp_h"), 1)
            highs("out1")
            norm(1, xT, "x_tile", 8, sqb, lnb)
            split_high("n1")

            g0 = FIRST["ffn"]
            act.preload_act_table(ACT.Silu)
            with act.Fori(0, FF_TILES // 2) as i:
                for q in range(2):
                    if q:
                        act.wait_ge(sem("w_used"), i * 2 + (g0 + 3))
                    else:
                        act.wait_ge(sem("mm_g"), i + 1)
                    act.wait_ge(sem("ffn_u"), i * 2 + (q + 1))
                    act.activation(sg[:, q, :], ps[:, q, :], ACT.Silu).then_inc(sem("ffn_g"), 1)
                for q in range(2):
                    high(i * 2 + (g0 + 2 + q), q)
                for q in range(2):
                    act.wait_ge(sem("ffn_u"), i * 2 + (q + 3))
                    act.activation(zt(hidh, i * 2 + q), hid[:, q, :], ACT.Copy).then_inc(sem("hid_h"), 1)
            highs("down")
            act.wait_ge(sem("w_used"), FIRST["in2"] + 2)
            act.dma_start(pos_i[:, :], ins["positions"]).then_inc(sem("pos_loaded"), 16)
            ln_exp_tables()
            norm(2, xT, "x_tile", 16, sqb, lnb, bank=0)
            split_high("n2")

            def z2_tile(func):
                def tile(n, bank):
                    act.activation(zt(z2, n), ps[:, bank, :], func, bias=vd("b_in", n)).then_inc(sem("ev_in2"), 1)
                return tile

            act.preload_act_table(ACT.Sigmoid)
            evacuate("in2", VAL, GATE, z2_tile(ACT.Identity))
            evacuate("in2", GATE, Q2, z2_tile(ACT.Sigmoid))
            evacuate("in2", Q2, GCONV, z2_tile(ACT.Identity))
            evacuate("in2", GCONV, Z2_TILES, z2_tile(ACT.Sigmoid))

            act.wait_ge(sem("rp_a"), 1)
            act.activation(csin[:, :, :], csin[:, :, :], ACT.Sin).then_inc(sem("rp_s"), 1)

            ln_exp_tables()
            for j in range(KD):
                act.wait_ge(sem("ln_x"), j + 1)
                act.wait_ge(sem("ln_v"), j + 1)
                act.activation(sqb[:, j % 2, :], z2[:, GATE + j, :], ACT.Square).then_inc(sem("ln_sq"), 1)
            act.wait_ge(sem("ln_v"), KD + 2)
            rstd(ps[:, 7, :], lnb[:, 0, :], lnb[:, 1, :], "ln", 1)
            act.preload_act_table(ACT.Silu)
            base = split_base("ln")
            for j in range(KD):
                act.wait_ge(sem("ln_n"), j + 1)
                act.wait_ge(sem("sp_l"), base + j + 1)
                act.activation(tmp[:, j % 2, :], z2[:, GATE + j, :], ACT.Silu, scale=v("ln_g", j), bias=v("ln_b", j)
                               ).then_inc(sem("sp_t"), 1)
                act.wait_ge(sem("sp_t"), base + j + 1)
                act.activation(hh[:, j, :], tmp[:, j % 2, :], ACT.Copy).then_inc(sem("sp_h"), 1)
            ln_exp_tables()
            highs("co")

            act.wait_ge(sem("sw_vt"), 1)
            act.activation(vn_pairs, ps[:, 5, :].rearrange("p (a n) -> p a n", a=2), ACT.Copy
                           ).then_inc(sem("sw_v"), 1)

            def weights(j, r):
                c, n, st = swa_cols(r), j * STEPS + r, sstat[:, r % 2, :]
                act.wait_ge(sem("sw_m"), n + 1)
                for e in range(2):
                    act.activation(spr[:, r % 2, e, c:], ssc[:, r % 2, e, c:], ACT.Exp, bias=st[:, 2 + e:3 + e],
                                   accum_out=st[:, 6 + e:7 + e]).then_inc(sem("sw_e"), 1)
                act.wait_ge(sem("sw_d"), n + 1)
                act.activation(st[:, 8:10], st[:, 4:6], ACT.Exp).then_inc(sem("sw_e"), 1)

            def turned_weights(j, r):
                n, b = j * STEPS + r, swa_cols(r) // P
                act.wait_ge(sem("sw_t"), n + 1)
                act.wait_ge(sem("sw_o"), n + 1)
                act.activation(spt[:, r % 2, :, :].rearrange("p e (b n) -> p e b n", b=2)[:, :, b:, :],
                               ps[:, 2 + r % 2, :].rearrange("p (e b n) -> p e b n", e=2, b=2)[:, :, b:, :], ACT.Copy
                               ).then_inc(sem("sw_pt"), 1)

            def heads_out(j, kv):
                act.wait_ge(sem("sw_o"), j * STEPS + (kv * NT + NT + 2))
                act.activation(zt(z2, j + kv * PAIRS_PER_KV), ps[:, 4 + kv, :], ACT.Copy).then_inc(sem("sw_y"), 1)

            def halves_out(j, kv):
                if not (isinstance(j, int) and j == 0):
                    act.wait_ge(sem("rq"), j * 2 + (kv - 1))
                act.wait_ge(sem("rq_mm"), j * 2 + (kv + 1))
                act.activation(rt[:, kv, :], ps[:, 6 + kv, :], ACT.Copy).then_inc(sem("rh"), 1)

            def step(j, r, last):
                if not last and r % NT == 1:
                    halves_out(j + 1, r // NT)
                if not last or r + 1 < STEPS:
                    weights(*ahead(j, r, 1))
                turned_weights(j, r)
                if r == NT:
                    heads_out(j, 0)
                if r == STEPS - 1:
                    heads_out(j, 1)

            for kv in range(2):
                halves_out(0, kv)
            weights(0, 0)
            all_steps(act, PAIRS_PER_KV, step)
            base = split_base("at")
            act.wait_ge(sem("sw_y"), SWA_PAIRS + 2)
            act.wait_ge(sem("w_used"), FIRST["ao"] + 2)
            for k in range(KD):
                act.wait_ge(sem("sp_l"), base + k + 1)
                act.activation(tmp[:, k % 2, :], z2[:, k, :], ACT.Copy).then_inc(sem("sp_t"), 1)
                act.activation(hh[:, k, :], z2[:, k, :], ACT.Copy).then_inc(sem("sp_h"), 1)
            highs("ao")
            split_high("mg")
            highs("out2")
            norm(3, xT, "x_tile", 24, sqb, lnb)
            split_high("n3")

            def q_tile(n, bank):
                act.activation(zt(qT, n), ps[:, bank, :], ACT.Copy).then_inc(sem("ev_pq"), 1)

            evacuate("pq", 0, HC - 4, q_tile)
            evacuate("pq", HC - 4, HC, q_tile, ahead=False)
            for n in range(NT * 4):
                act.wait_ge(sem("sc_mm"), n + 1)
                if n >= 2:
                    act.wait_ge(sem(f"sc_out{n % 2}"), 16 * (n // 2))
                act.activation(scev[:, n % 2, :, :], ps[:, 6 + n % 2, :].rearrange("p (a n) -> p a n", a=4), ACT.Copy
                               ).then_inc(sem("sc_copied"), 1)
            act.wait_ge(sem("late_free"), 1)

            for grp in range(GROUPS):
                e0 = grp * EG

                def high_u(e, r):
                    act.wait_ge(sem(f"u_in{r}"), e * 8 + (16 - 8 * r + 8 * e0))
                    act.wait_ge(sem("a_mm"), e + (e0 + 1))
                    act.activation(eh[:, r, :], er[:, r, :], ACT.Copy).then_inc(sem("u_hi"), 1)

                def gelu(e, r):
                    act.wait_ge(sem("a_mm"), e + (e0 + 1 + 2))
                    act.activation(zt(ga, e), ps[:, 4 + r, :], ACT.Gelu).then_inc(sem("a_ev"), 1)

                def high_v(e, r):
                    act.wait_ge(sem(f"v_in{r}"), e * 8 + (16 - 8 * r + 8 * e0))
                    act.wait_ge(sem("v_used"), e + (e0 + 1))
                    act.activation(eh[:, r, :], er[:, r, :], ACT.Copy).then_inc(sem("v_hi"), 1)
                    act.activation(gah[:, r, :], zt(ga, e), ACT.Copy).then_inc(sem("v_hi"), 1)

                if grp:
                    act.wait_ge(sem("e_spilled"), 16)
                    act.wait_ge(sem("v_used"), e0 + 2)
                act.preload_act_table(ACT.Gelu)
                high_u(0, 0)
                with act.Fori(0, EG // 2 - 1) as i:
                    for r in range(2):
                        high_u(i * 2 + (r + 1), (r + 1) % 2)
                        gelu(i * 2 + r, r)
                high_u(EG - 1, 1)
                gelu(EG - 2, 0)
                gelu(EG - 1, 1)
                ln_exp_tables()
                if grp == 0:
                    act.wait_ge(sem("tk_unit"), 2 * NT + 1)
                    act.activation(sel[:, :, 2, :], sel[:, :, 2, :], ACT.Exp).then_inc(sem("gt_e"), 1)
                    for a, dst in enumerate((slot_t[:, 0, :], slot_t[:, 1, :], gate_t)):
                        act.wait_ge(sem("slot_mm"), a + 1)
                        act.activation(dst, ps[:, 5 + a, :], ACT.Copy).then_inc(sem("slot_t"), 1)
                    act.wait_ge(sem("slot_t"), 3)
                    act.activation(slot_t[:, 2, :], gate_t, ACT.Copy).then_inc(sem("slot_t"), 1)

                def gated(n, r):
                    act.wait_ge(sem("oh1_eq"), n + (grp * (S // TB) + 1))
                    act.wait_ge(sem("g_mm"), n + (grp * (S // TB) + 1))
                    for t in range(TB):
                        act.activation(oh1[:, r, 0, :, t], eq1[:, r, :, t], ACT.Identity,
                                       scale=gate_t[:, bass.ds(n * TB + t, 1)]).then_inc(sem("oh1_1"), 1)

                rolled(act, S // TB, 4, gated)
                act.wait_ge(sem("g_mul"), (grp + 1) * (S // TB) + 4)
                rolled(act, EG, 2, high_v)
            norm(4, xf, "y_sum", 0, fsq, fln, bank=0)

        @block.tensor
        def _(pe):
            for name in ("w_used", "nm_mm", "gn_mm", "ln_v", "ch_o", "sw_o", "a_mm", "v_used"):
                pe.sem_inc(sem(name), 2)
            pe.sem_inc(sem("g_mm"), 4)

            def three(bank, whi, wlo, xhi, xlo, start, stop):
                nc.tensor.matmul(bank, whi, xhi, start=start, stop=False)
                nc.tensor.matmul(bank, whi, xlo, start=False, stop=False)
                return nc.tensor.matmul(bank, wlo, xhi, start=False, stop=stop)

            def norm(n, sq, bank=4):
                for k in range(KD):
                    pe.wait_ge(sem("nm_sq"), 8 * n + k + 1)
                    nc.tensor.matmul(ps[:, bank, :], mean, sq[:, k % 2, :], start=(k == 0), stop=(k == KD - 1)
                                     ).then_inc(sem("nm_mm"), 1)

            def slot_tiles(g, b, first_done, bank_free):
                pe.wait_ge(sem("w_lo"), g + 3)
                for half in range(2):
                    bank_free(half)
                    for k in range(KD):
                        last = three(ps[:, 2 * b + half, :], piece(wh, b, k, half), piece(wl, b, k, half),
                                     hh[:, k, :], hl[:, k, :], k == 0, k == KD - 1)
                    last.then_inc(sem("w_used" if half else first_done), 1)

            def gemm(name, split, freed=None, base=0):
                g0 = FIRST[name]
                pe.wait_ge(sem("sp_l"), split_base(split) + 8 + 2)
                rolled(pe, COUNT[name], 2, lambda s, r: slot_tiles(
                    s + g0, (g0 + r) % 2, "mm_" + name,
                    lambda half: pe.wait_ge(sem(freed or "ev_" + name), s * 2 + (half + 1 + base))))

            pe.wait_ge(sem("c_loaded"), 32)
            norm(0, sqb)
            gemm("in1", "n0")

            with pe.Fori(0, SB_PAIRS) as p:
                pe.wait_ge(sem("sb_staged"), p * 3 + 3)
                for t in range(NT):
                    last = nc.tensor.transpose(ps[:, 5, t * P:t * P + P], vts[:, t * P:t * P + P], ident)
                last.then_inc(sem("sb_vt"), 1)
                for e in range(2):
                    n = p * 8 + 4 * e
                    h = slice(HD * e, HD * e + HD)
                    if e:
                        pe.wait_ge(sem("sb_w0"), p * 8 + 4)
                    for b in reversed(range(NT)):
                        nc.tensor.matmul(ps[:, b, 0:S - b * P], kst[h, b * P:b * P + P], qst[h, b * P:S],
                                         start=True, stop=True).then_inc(sem("sb_z"), 1)
                    for q, b in enumerate(reversed(range(NT))):
                        pe.wait_ge(sem("sb_sp"), n + (q + 1))
                        last = nc.tensor.matmul(ps[:, b, 0:S - b * P], negtri, spl[:, b, 0:S - b * P], start=False,
                                                stop=(b == NT - 1), skip_group_check=True)
                        for c in range(b + 1, NT):
                            last = nc.tensor.matmul(ps[:, b, (c - b) * P:S - b * P], negone, spl[:, c, 0:S - c * P],
                                                    start=False, stop=(c == NT - 1), skip_group_check=True)
                        last.then_inc(sem("sb_cum"), 1)
                    pe.wait_ge(sem("sb_v"), p + 1)
                    pe.wait_ge(sem("sb_w"), n + 4)
                    if e == 0:
                        pe.wait_ge(sem("sb_y"), p + 1)
                    for b in range(NT):
                        last = nc.tensor.matmul(ps[h, 4, b * P:S], vst[:, b, h], ab[:, b, 0:S - b * P],
                                                start=(b == 0), stop=(b == NT - 1))
                    last.then_inc(sem("sb_pv"), 1)

            def mean_squares(p):
                for w in range(2):
                    pe.wait_ge(sem("ch_sq"), p * 2 + (w + 1))
                    if not (isinstance(p, int) and p == 0):
                        pe.wait_ge(sem("ch_rs"), p * 2 + (w - 1))
                    nc.tensor.matmul(ps[:, 6 + w, :], blk64, sqb[:, w, :], start=True, stop=True
                                     ).then_inc(sem("ch_ms"), 1)

            def turn_values(p):
                pe.wait_ge(sem("ch_v"), p * 2 + 2)
                pe.wait_ge(sem("ch_vs"), p + 1)
                for t in range(NT):
                    last = nc.tensor.transpose(ps[:, 5, t * P:t * P + P], cvts[:, t * P:t * P + P], ident)
                last.then_inc(sem("ch_vt"), 1)

            def scores(p, r):
                e, i = r // NT, r % NT
                h = slice(HD * e, HD * e + HD)
                pe.wait_ge(sem("ch_qk"), p * 2 + 4)
                pe.wait_ge(sem("ch_s"), p * STEPS + (r + 1))
                nc.tensor.matmul(ps[:, r % 2, 0:(i + 1) * P], cqst[h, i * P:i * P + P], ckst[h, 0:(i + 1) * P],
                                 start=True, stop=True).then_inc(sem("ch_sc"), 1)

            def turn(p, r):
                pe.wait_ge(sem("ch_p"), p * STEPS + (r + 1))
                pe.wait_ge(sem("ch_pt"), p * STEPS + (r + 1))
                for b in range(r % NT + 1):
                    last = nc.tensor.transpose(ps[:, 2 + r % 2, b * P:b * P + P], cpr[:, r % 2, b * P:b * P + P],
                                               ident)
                last.then_inc(sem("ch_t"), 1)

            def values(p, r):
                e, i = r // NT, r % NT
                h = slice(HD * e, HD * e + HD)
                pe.wait_ge(sem("ch_pt"), p * STEPS + (r + 3))
                if i == 0:
                    pe.wait_ge(sem("ch_v"), p * 2 + (e + 3))
                    pe.wait_ge(sem("ch_y"), p * 2 + (e + 1))
                for b in range(i + 1):
                    last = nc.tensor.matmul(ps[h, 4, i * P:i * P + P], cvst[:, b, h],
                                            cpt[:, r % 2, b * P:b * P + P], start=(b == 0), stop=(b == i))
                last.then_inc(sem("ch_o"), 1)

            def step(p, r, last):
                if not last and r == 2:
                    mean_squares(p + 1)
                if not last and r == 3:
                    turn_values(p + 1)
                if not last or r + 3 < STEPS:
                    scores(*ahead(p, r, 3))
                if not last or r + 1 < STEPS:
                    turn(*ahead(p, r, 1))
                values(p, r)

            mean_squares(0)
            turn_values(0)
            for r in range(3):
                scores(0, r)
            turn(0, 0)
            all_steps(pe, CH_PAIRS, step)

            for j in range(KD):
                pe.wait_ge(sem("gn_sq"), j + 1)
                if j >= 2:
                    pe.wait_ge(sem("gn_ln"), j - 1)
                nc.tensor.matmul(ps[:, 4 + j % 2, :], blk64, sqb[:, j % 2, :], start=True, stop=True
                                 ).then_inc(sem("gn_mm"), 1)
            gemm("out1", "gn", "x_tile", 8 - 4)
            norm(1, sqb)

            pe.wait_ge(sem("sp_l"), split_base("n1") + 8 + 2)
            g0 = FIRST["ffn"]
            with pe.Fori(0, FF_TILES // 2) as i:
                slot_tiles(i * 2 + g0, 0, "mm_g", lambda half: pe.wait_ge(sem("ffn_g"), i * 2 + (half + 1)))
                slot_tiles(i * 2 + (g0 + 1), 1, "mm_u", lambda half: pe.wait_ge(sem("ffn_u"), i * 2 + (half + 1)))
            g0 = FIRST["down"]
            pe.wait_ge(sem("ffn_u"), FF_TILES + 2)

            def down(s, b, start=False, stop=False):
                pe.wait_ge(sem("w_lo"), s + (g0 + 3))
                pe.wait_ge(sem("hid_l"), s * 2 + 4)
                for j in range(2):
                    for c in range(KD):
                        last = three(ps[:, c, :], piece_down(wh, b, j, c), piece_down(wl, b, j, c),
                                     zt(hidh, s * 2 + j), zt(hidl, s * 2 + j), start and j == 0, stop and j == 1)
                last.then_inc(sem("w_used"), 1)

            down(0, g0 % 2, start=True)
            rolled(pe, COUNT["down"] - 2, 2, lambda s, r: down(s + 1, (g0 + 1 + r) % 2))
            down(COUNT["down"] - 1, (g0 + COUNT["down"] - 1) % 2, stop=True)
            norm(2, sqb, bank=0)
            gemm("in2", "n2")

            for j in range(KD):
                pe.wait_ge(sem("cv2_y"), j + 1)
                last = nc.tensor.matmul(ps[:, 6, :], mean, z2[:, GATE + j, :], start=(j == 0), stop=(j == KD - 1))
            last.then_inc(sem("ln_m"), 1)
            for j in range(KD):
                pe.wait_ge(sem("ln_sq"), j + 1)
                nc.tensor.matmul(ps[:, 7, :], mean, sqb[:, j % 2, :], start=(j == 0), stop=(j == KD - 1)
                                 ).then_inc(sem("ln_v"), 1)
            gemm("co", "ln")

            pe.wait_ge(sem("ev_in2"), Z2_TILES + 4)
            nc.tensor.matmul(ps[:, 6, :], rot, z2[:, K2, :], start=True, stop=True).then_inc(sem("rk_mm"), 1)
            for t in range(NT):
                last = nc.tensor.transpose(ps[:, 5, t * P:t * P + P], z2[:, V2, t * P:t * P + P], ident)
            last.then_inc(sem("sw_vt"), 1)
            pe.wait_ge(sem("kd"), 4)
            pe.wait_ge(sem("sw_v"), 1)
            def halves(j, kv):
                nc.tensor.matmul(ps[:, 6 + kv, :], rot, zt(z2, j + (Q2 + kv * PAIRS_PER_KV)), start=True, stop=True
                                 ).then_inc(sem("rq_mm"), 1)

            def scores(j, r):
                kv, i, c = r // NT, r % NT, swa_cols(r)
                pe.wait_ge(sem("rq"), j * 2 + (kv + 1))
                pe.wait_ge(sem("sw_s"), j * STEPS + (r + 1))
                for e in range(2):
                    h = slice(HD * e, HD * e + HD)
                    if e:
                        pe.wait_ge(sem("sw_sc0"), j * STEPS + (r + 1))
                    nc.tensor.matmul(ps[:, r % 2, 2 * P * e + c:2 * P * e + 2 * P], rq[h, kv, i * P:i * P + P],
                                     kdup[h, kv, (i - 1) * P + c:(i + 1) * P], start=True, stop=True
                                     ).then_inc(sem("sw_sc" if e else "sw_sc0"), 1)

            def turn(j, r):
                pe.wait_ge(sem("sw_p"), j * STEPS + (r + 1))
                pe.wait_ge(sem("sw_pt"), j * STEPS + (r + 1))
                for e in range(2):
                    for k in range(swa_cols(r), 2 * P, P):
                        last = nc.tensor.transpose(ps[:, 2 + r % 2, 2 * P * e + k:2 * P * e + k + P],
                                                   spr[:, r % 2, e, k:k + P], ident)
                last.then_inc(sem("sw_t"), 1)

            def values(j, r):
                kv, i, c = r // NT, r % NT, swa_cols(r)
                pe.wait_ge(sem("sw_pt"), j * STEPS + (r + 3))
                if i == 0:
                    pe.wait_ge(sem("sw_y"), j * 2 + (kv + 1))
                for e in range(2):
                    for k in range(c, 2 * P, P):
                        last = nc.tensor.matmul(ps[HD * e:HD * e + HD, 4 + kv, i * P:i * P + P],
                                                vn(i - 1 + k // P)[:, HD * kv:HD * kv + HD],
                                                spt[:, r % 2, e, k:k + P], start=(k == c), stop=(k == P))
                last.then_inc(sem("sw_o"), 1)

            def step(j, r, last):
                if not last and r % NT == 1:
                    halves(j + 1, r // NT)
                if not last or r + 3 < STEPS:
                    scores(*ahead(j, r, 3))
                if not last or r + 1 < STEPS:
                    turn(*ahead(j, r, 1))
                values(j, r)

            for kv in range(2):
                halves(0, kv)
            for r in range(3):
                scores(0, r)
            turn(0, 0)
            all_steps(pe, PAIRS_PER_KV, step)
            gemm("ao", "at")
            gemm("out2", "mg", "x_tile", 24 - 4)
            norm(3, sqb)
            gemm("pq", "n3")

            pe.wait_ge(sem("sk_loaded"), 16)
            pe.wait_ge(sem("ev_pq"), HC + 4)
            for n in range(NT * 4):
                t, c = n // 4, n % 4
                if n >= 2:
                    pe.wait_ge(sem("sc_copied"), n - 1)
                for a in range(4):
                    last = nc.tensor.matmul(ps[:, 6 + n % 2, a * P:a * P + P], qT[:, 4 * c + a, t * P:t * P + P],
                                            skT[:, 4 * c + a, :], start=True, stop=True)
                last.then_inc(sem("sc_mm"), 1)

            for grp in range(GROUPS):
                e0, n0 = grp * EG, grp * (S // TB)

                def dots(e, r):
                    pe.wait_ge(sem("u_lo"), e + (e0 + 3))
                    pe.wait_ge(sem("a_ev"), e + (e0 + 1))
                    for k in range(KD):
                        last = three(ps[:, 4 + r, :], eh[:, r, k * P:k * P + P], el[:, r, k * P:k * P + P],
                                     hh[:, k, :], hl[:, k, :], k == 0, k == KD - 1)
                    last.then_inc(sem("a_mm"), 1)

                def table(n, r):
                    pe.wait_ge(sem("oh1_1"), n * TB + (TB * n0 + TB))
                    pe.wait_ge(sem("oh1_2"), n + (n0 + 1))
                    pe.wait_ge(sem("oh1_3"), n + (n0 + 1))
                    pe.wait_ge(sem("g_mul"), n + (n0 + 1))
                    for t in range(TB):
                        for a in range(3):
                            last = nc.tensor.matmul(ps[:, r, t * EG:t * EG + EG], oh2[:, r, :, t], oh1[:, r, a, :, t],
                                                    start=(a == 0), stop=(a == 2))
                    last.then_inc(sem("g_mm"), 1)

                def gather(e, r, start=False, stop=False):
                    pe.wait_ge(sem("v_lo"), e + (e0 + 3))
                    for c in range(KD):
                        last = three(ps[:, c, :], eh[:, r, c * P:c * P + P], el[:, r, c * P:c * P + P], gah[:, r, :],
                                     gal[:, r, :], start, stop)
                    last.then_inc(sem("v_used"), 1)

                if grp:
                    pe.wait_ge(sem("e_part"), KD)
                rolled(pe, EG, 2, dots)
                pe.wait_ge(sem("a_ev"), e0 + EG + 2)
                if grp == 0:
                    pe.wait_ge(sem("gt"), 1)
                    for a in range(3):
                        for t in range(NT):
                            last = nc.tensor.transpose(ps[:, 5 + a, t * P:t * P + P], sel[:, t, a, :], ident)
                        last.then_inc(sem("slot_mm"), 1)
                rolled(pe, S // TB, 4, table)
                gather(0, 0, start=True)
                rolled(pe, EG - 2, 2, lambda e, r: gather(e + 1, (1 + r) % 2))
                gather(EG - 1, 1, stop=True)
            norm(4, fsq, bank=0)
        @block.vector
        def _(dve):
            for name in ("in1", "in2", "co", "ao", "pq"):
                dve.sem_inc(sem("ev_" + name), 4)
            for name in ("ffn_u", "ffn_g", "ch_qk", "ch_v", "ch_y", "ch_s", "ch_pt", "sw_s", "sw_pt", "sw_y", "a_ev", "v_lo"):
                dve.sem_inc(sem(name), 2)
            dve.sem_inc(sem("g_mul"), 4)
            for name in ("sb_y", "ch_vt", "tk_unit"):
                dve.sem_inc(sem(name), 1)

            chained = {}

            def chain(name, ins):
                chained[name] = chained.get(name, 0) + 1
                ins.then_inc(sem(name), 1)
                dve.wait_ge(sem(name), chained[name])

            def norm(n, gain, split):
                dve.wait_ge(sem("nm_rs"), n + 1)
                for k in range(KD):
                    dve.wait_ge(sem("sp_l"), split_base(split) + k + 1)
                    dve.scalar_tensor_tensor(tmp[:, k % 2, :], xT[:, k, :], v(gain, k), lnb[:, 1, :], ALU.mult, ALU.mult
                                             ).then_inc(sem("sp_t"), 1)

            def add_to_x(name):
                for n in range(KD):
                    tile_done(dve, name, n // 2, n % 2)
                    dve.tensor_tensor(xT[:, n, :], xT[:, n, :], ps[:, bank_of(name, n), :], ALU.add
                                      ).then_inc(sem("x_tile"), 1)

            dve.wait_ge(sem("x_loaded"), 16)
            dve.sem_inc(sem("x_tile"), KD)
            dve.wait_ge(sem("c_loaded"), 32)
            norm(0, "attn_norm", "n0")

            dve.wait_ge(sem("ev_in1"), Z1_TILES + 4)
            for c in range(CV_TILES):
                y, hc = yT[:, SB_PAIRS + CH_PAIRS + c, :], z1[:, GC + c, :]
                chain("cv", dve.tensor_tensor(hc, hc, z1[:, XC + c, :], ALU.mult))
                chain("cv", dve.tensor_scalar(y, hc, v("conv", 3 * c + 2), None, ALU.mult))
                for back in (1, 2):
                    chain("cv", dve.scalar_tensor_tensor(y[:, back:S], hc[:, 0:S - back], v("conv", 3 * c + 2 - back),
                                                         y[:, back:S], ALU.mult, ALU.add))
                dve.tensor_tensor(y, y, z1[:, GB + c, :], ALU.mult).then_inc(sem("cv_y"), 1)

            with dve.Fori(0, SB_PAIRS) as p:
                dve.wait_ge(sem("sb_y"), p + 1)
                dve.tensor_copy(kst, zt(z1, p + KA)).then_inc(sem("sb_staged"), 1)
                dve.tensor_scalar(qst, zt(z1, p + QA), SCALE, None, ALU.mult).then_inc(sem("sb_staged"), 1)
                dve.tensor_copy(vts[:, :], zt(z1, p + VA)).then_inc(sem("sb_staged"), 1)
                for e in range(2):
                    for q, b in enumerate(reversed(range(NT))):
                        dve.wait_ge(sem("sb_l"), p * 8 + (4 * e + q + 1))
                        dve.scalar_tensor_tensor(spl[:, b, 0:S - b * P], ps[:, b, 0:S - b * P], 0.0,
                                                 ab[:, b, 0:S - b * P], ALU.max, ALU.add).then_inc(sem("sb_sp0"), 1)

            dve.wait_ge(sem("sb_y"), SB_PAIRS + 1)
            dve.wait_ge(sem("bt_ready"), 1)

            def normed(p):
                if not (isinstance(p, int) and p == 0):
                    dve.wait_ge(sem("ch_sc"), p * STEPS)
                for w, (src, dst, gain) in enumerate(((QB, cqst, "qn"), (KB, ckst, "kn"))):
                    dve.wait_ge(sem("ch_rs"), p * 2 + (w + 1))
                    dve.scalar_tensor_tensor(dst[:, :], zt(z1, p + src), v(gain), lnb[:, w, :], ALU.mult, ALU.mult
                                             ).then_inc(sem("ch_qk"), 1)

            def shifted(p, r):
                e, i, n = r // NT, r % NT, p * STEPS + r
                w = (i + 1) * P
                bias = bt[:, bass.ds(p * 2 + e, 1), (3 - i) * P:S].rearrange("p a n -> p (a n)")
                dve.wait_ge(sem("ch_sc"), n + 1)
                dve.scalar_tensor_tensor(csc[:, r % 2, 0:w], ps[:, r % 2, 0:w], SCALE, bias, ALU.mult, ALU.add
                                         ).then_inc(sem("ch_s"), 1)
                dve.wait_ge(sem("ch_s"), n + 3)
                dve.tensor_reduce(cstat[:, r % 2, 0:1], csc[:, r % 2, 0:w], AX_X, ALU.max, negate=True
                                  ).then_inc(sem("ch_m"), 1)

            def divided(p, r):
                n, w = p * STEPS + r, (r % NT + 1) * P
                dve.wait_ge(sem("ch_e"), n + 1)
                dve.reciprocal(cstat[:, r % 2, 2:3], cstat[:, r % 2, 1:2]).then_inc(sem("ch_r"), 1)
                dve.wait_ge(sem("ch_r"), n + 1)
                dve.tensor_scalar(cpr[:, r % 2, 0:w], cpr[:, r % 2, 0:w], cstat[:, r % 2, 2:3], None, ALU.mult
                                  ).then_inc(sem("ch_p"), 1)

            def step(p, r, last):
                if not last and r == NT:
                    normed(p + 1)
                if not last or r + 2 < STEPS:
                    shifted(*ahead(p, r, 2))
                if not last or r + 1 < STEPS:
                    divided(*ahead(p, r, 1))

            normed(0)
            shifted(0, 0)
            shifted(0, 1)
            divided(0, 0)
            all_steps(dve, CH_PAIRS, step)

            for j in range(KD):
                dve.wait_ge(sem("gn_rs"), j + 1)
                dve.wait_ge(sem("sp_l"), split_base("gn") + j + 1)
                dve.scalar_tensor_tensor(tmp[:, j % 2, :], yT[:, j, :], v("out_norm", j), lnb[:, 1, :], ALU.mult,
                                         ALU.mult).then_inc(sem("sp_t"), 1)
            add_to_x("out1")
            norm(1, "ffn_norm", "n1")
            with dve.Fori(0, FF_TILES // 2) as i:
                for q in range(2):
                    if q:
                        dve.wait_ge(sem("w_used"), i * 2 + (FIRST["ffn"] + 4))
                    else:
                        dve.wait_ge(sem("mm_u"), i + 1)
                    dve.wait_ge(sem("ffn_g"), i * 2 + (q + 3))
                    dve.wait_ge(sem("hid_l"), i * 2 + (q + 1))
                    dve.tensor_tensor(hid[:, q, :], sg[:, q, :], ps[:, 2 + q, :], ALU.mult).then_inc(sem("ffn_u"), 1)
            dve.wait_ge(sem("w_used"), FIRST["in2"] + 2)
            for k in range(KD):
                dve.tensor_tensor(xT[:, k, :], xT[:, k, :], ps[:, k, :], ALU.add).then_inc(sem("x_tile"), 1)
            norm(2, "norm1", "n2")

            dve.wait_ge(sem("pos_loaded"), 16)
            two_pi = 2.0 * np.pi
            part1 = 6.28125
            part2 = float((np.array([two_pi - part1], np.float32).view(np.uint32) & np.uint32(0xFFFFF000))
                          .view(np.float32)[0])
            part3 = float(np.float32(two_pi - part1 - part2))
            to_whole = 1.5 * 2.0 ** 23
            limit = 3.1415925
            whole, angle = sqb[:, 0, :], sqb[:, 1, :]
            chain("rp", dve.tensor_copy(angle, pos_i[:, :]))
            chain("rp", dve.tensor_scalar(angle, angle, v("inv"), None, ALU.mult))
            for q, shift in ((0, np.pi / 2), (1, 0.0)):
                a = csin[:, q, :]
                chain("rp", dve.tensor_scalar(whole, angle, 1.0 / two_pi, shift / two_pi, ALU.mult, ALU.add))
                chain("rp", dve.tensor_scalar(whole, whole, to_whole, None, ALU.add))
                chain("rp", dve.tensor_scalar(whole, whole, -to_whole, None, ALU.add))
                chain("rp", dve.scalar_tensor_tensor(a, whole, -part1, angle, ALU.mult, ALU.add))
                chain("rp", dve.scalar_tensor_tensor(a, whole, -part2, a, ALU.mult, ALU.add))
                chain("rp", dve.scalar_tensor_tensor(a, whole, -part3, a, ALU.mult, ALU.add))
                chain("rp", dve.tensor_scalar(a, a, float(shift), limit, ALU.add, ALU.min))
                chain("rp", dve.tensor_scalar(a, a, -limit, None, ALU.max))
            dve.sem_inc(sem("rp_a"), 1)

            with dve.Fori(0, KD // 2) as i:
                dve.wait_ge(sem("ev_in2"), i * 2 + (GATE + 2 + 4))
                steps = TAPS + 1
                for q in range(2):
                    j = i * 2 + q
                    dve.tensor_tensor(zt(z2, j), zt(z2, j), zt(z2, j + GATE), ALU.mult).then_inc(sem(f"cv2_{q}"), 1)
                for back in range(TAPS):
                    for q in range(2):
                        j = i * 2 + q
                        w = vd("conv2", j * TAPS + (TAPS - 1 - back))
                        acc, u = zt(z2, j + GATE), zt(z2, j)
                        dve.wait_ge(sem(f"cv2_{q}"), i * steps + (back + 1))
                        if back == 0:
                            dve.tensor_scalar(acc, u, w, vd("conv2_b", j), ALU.mult, ALU.add
                                              ).then_inc(sem(f"cv2_{q}"), 1)
                        else:
                            dve.scalar_tensor_tensor(acc[:, back:S], u[:, 0:S - back], w, acc[:, back:S],
                                                     ALU.mult, ALU.add).then_inc(sem(f"cv2_{q}"), 1)
                for q in range(2):
                    dve.wait_ge(sem(f"cv2_{q}"), i * steps + steps)
                    dve.sem_inc(sem("cv2_y"), 1)

            dve.wait_ge(sem("ln_m"), 1)
            for j in range(KD):
                dve.tensor_tensor(z2[:, GATE + j, :], z2[:, GATE + j, :], ps[:, 6, :], ALU.subtract
                                  ).then_inc(sem("ln_x"), 1)
            dve.wait_ge(sem("ln_rs"), 1)
            for j in range(KD):
                dve.wait_ge(sem("ln_sq"), j + 1)
                dve.tensor_tensor(z2[:, GATE + j, :], z2[:, GATE + j, :], lnb[:, 1, :], ALU.mult
                                  ).then_inc(sem("ln_n"), 1)

            for n in range(KD):
                tile_done(dve, "co", n // 2, n % 2)
                dve.tensor_tensor(z2[:, GCONV + n, :], z2[:, GCONV + n, :], ps[:, bank_of("co", n), :], ALU.mult
                                  ).then_inc(sem("ev_co"), 1)

            dve.wait_ge(sem("rp_s"), 1)
            dve.wait_ge(sem("rk_mm"), 1)
            chain("rk", dve.tensor_tensor(rq[:, 0, :], z2[:, K2, :], csin[:, 0, :], ALU.mult))
            chain("rk", dve.tensor_tensor(rt[:, 0, :], ps[:, 6, :], csin[:, 1, :], ALU.mult))
            chain("rk", dve.tensor_tensor(rq[:, 0, :], rq[:, 0, :], rt[:, 0, :], ALU.add))
            chain("rk", dve.tensor_scalar(nsink[:, :], v("sinks", 0, 2 * SWA_PAIRS), -1.0, None, ALU.mult))
            for kv in range(2):
                for e in range(2):
                    dve.tensor_copy(kdup[HD * e:HD * e + HD, kv, :], rq[HD * kv:HD * kv + HD, 0, :]
                                    ).then_inc(sem("kd"), 1)
            dve.wait_ge(sem("kd"), 4)
            dve.wait_ge(sem("msk"), 3)
            def shifted(j, r):
                c, n, st = swa_cols(r), j * STEPS + r, sstat[:, r % 2, :]
                sink = nsink[:, bass.ds(j * 2 + 2 * PAIRS_PER_KV * (r // NT), 2)]
                sc2 = ps[:, r % 2, :].rearrange("p (e n) -> p e n", e=2)
                dve.wait_ge(sem("sw_sc"), n + 1)
                dve.scalar_tensor_tensor(ssc[:, r % 2, :, c:], sc2[:, :, c:], SCALE,
                                         msk[:, c:].unsqueeze(1).to_broadcast([P, 2, 2 * P - c]), ALU.mult, ALU.add
                                         ).then_inc(sem("sw_s"), 1)
                dve.wait_ge(sem("sw_s"), n + 3)
                dve.tensor_reduce(st[:, 0:2], ssc[:, r % 2, :, c:], AX_X, ALU.max, negate=True
                                  ).then_inc(sem("sw_x"), 1)
                dve.wait_ge(sem("sw_x"), n + 1)
                dve.tensor_tensor(st[:, 2:4], st[:, 0:2], sink, ALU.min).then_inc(sem("sw_m"), 1)
                dve.wait_ge(sem("sw_m"), n + 1)
                dve.tensor_tensor(st[:, 4:6], st[:, 2:4], sink, ALU.subtract).then_inc(sem("sw_d"), 1)

            def divided(j, r):
                c, n, st = swa_cols(r), j * STEPS + r, sstat[:, r % 2, :]
                p = spr[:, r % 2, :, c:]
                dve.wait_ge(sem("sw_e"), n * 3 + 3)
                dve.tensor_tensor(st[:, 10:12], st[:, 6:8], st[:, 8:10], ALU.add).then_inc(sem("sw_r"), 1)
                dve.wait_ge(sem("sw_r"), n * 2 + 1)
                dve.reciprocal(st[:, 12:14], st[:, 10:12]).then_inc(sem("sw_r"), 1)
                dve.wait_ge(sem("sw_r"), n * 2 + 2)
                dve.tensor_tensor(p, p, st[:, 12:14].unsqueeze(2).to_broadcast([P, 2, 2 * P - c]), ALU.mult
                                  ).then_inc(sem("sw_p"), 1)

            def step(j, r, last):
                if not last or r + 2 < STEPS:
                    shifted(*ahead(j, r, 2))
                if not last or r + 1 < STEPS:
                    divided(*ahead(j, r, 1))

            shifted(0, 0)
            shifted(0, 1)
            divided(0, 0)
            all_steps(dve, PAIRS_PER_KV, step)

            for n in range(KD):
                tile_done(dve, "ao", n // 2, n % 2)
                dve.tensor_tensor(z2[:, GATTN + n, :], z2[:, GATTN + n, :], ps[:, bank_of("ao", n), :], ALU.mult
                                  ).then_inc(sem("ev_ao"), 1)
            dve.wait_ge(sem("w_used"), FIRST["out2"] + 2)
            for n in range(KD):
                dve.wait_ge(sem("ev_ao"), 4 + n + 1)
                dve.wait_ge(sem("sp_l"), split_base("mg") + n + 1)
                dve.tensor_tensor(tmp[:, n % 2, :], z2[:, GATTN + n, :], z2[:, GCONV + n, :], ALU.add
                                  ).then_inc(sem("sp_t"), 1)
            add_to_x("out2")
            norm(3, "norm2", "n3")

            flat = sc[:, :, :].rearrange("p a n -> p (a n)")
            cand = flat.rearrange("p (h c) -> p h c", h=4)
            cand4 = flat.rearrange("p (h i j) -> p h i j", h=4, i=TOPK)
            pairs = top[:, :, :].rearrange("p (h c) k -> p h c k", c=2)
            keys = topf[:, :, :].rearrange("p (h c) k -> p h c k", c=2)
            grid = [P, 4, TOPK, TOPK]

            def unit(t, half, count):
                steps = 0

                def step(ins):
                    nonlocal steps
                    steps += 1
                    ins.then_inc(sem("tk"), 1)

                def settle():
                    pass_by(dve, "tk", count + steps)

                def sixteen(rows, vals, idx, n):
                    for a in range(n):
                        step(dve.max(out=vals[:, a, 0:8], in_=rows[:, a, :]))
                    settle()
                    for a in range(n):
                        step(dve.max_index(idx[:, a, 0:8], vals[:, a, 0:8], rows[:, a, :]))
                    settle()
                    for a in range(n):
                        step(dve.match_replace(out=rows[:, a, :], in_to_replace=vals[:, a, 0:8],
                                               in_values=rows[:, a, :], imm_value=-3.0e38))
                    settle()
                    for a in range(n):
                        step(dve.max(out=vals[:, a, 8:16], in_=rows[:, a, :]))
                    settle()
                    for a in range(n):
                        step(dve.max_index(idx[:, a, 8:16], vals[:, a, 8:16], rows[:, a, :]))
                    settle()

                pass_by(dve, "sc_in", t * 32 + (16 * half + 16))
                sixteen(sc, top, topi, 8)
                step(dve.tensor_copy(topf[:, :, :], topi[:, :, :]))
                step(dve.tensor_tensor(cand4, pairs[:, :, 0, :].unsqueeze(3).to_broadcast(grid),
                                       pairs[:, :, 1, :].unsqueeze(2).to_broadcast(grid), ALU.add))
                settle()
                sixteen(cand, best, bpos, 4)
                where = bpos[:, :, :].rearrange("p h k -> p (h k)")
                step(dve.tensor_scalar(bab[:, 0, :], where, 4, None, ALU.logical_shift_right))
                step(dve.tensor_scalar(bab[:, 1, :], where, TOPK - 1, None, ALU.bitwise_and))
                settle()
                step(dve.tensor_copy(bfl[:, :, :], bab[:, :, :]))
                settle()
                chosen = sel[:, bass.ds(t, 1), :, half * 4 * TOPK:(half + 1) * 4 * TOPK].rearrange(
                    "p t a s -> p (t a) s")
                for c in range(2):
                    at = bfl[:, c, :].rearrange("p (h k) -> p h k", h=4)
                    step(dve.tensor_tensor(cand4, at.unsqueeze(3).to_broadcast(grid),
                                           iota[:, 0:TOPK].unsqueeze(1).unsqueeze(1).to_broadcast(grid),
                                           ALU.is_equal))
                    settle()
                    step(dve.tensor_tensor(cand4, cand4, keys[:, :, c, :].unsqueeze(2).to_broadcast(grid), ALU.mult))
                    settle()
                    step(dve.tensor_reduce(chosen[:, c, :], flat.rearrange("p (s j) -> p s j", j=TOPK), AX_X, ALU.add))
                    settle()
                step(dve.tensor_tensor(chosen[:, 2, :].rearrange("p (h k) -> p h k", h=4), best[:, :, :],
                                       best[:, :, 0:1].to_broadcast([P, 4, TOPK]), ALU.subtract))
                settle()
                dve.sem_inc(sem("tk_unit"), 1)
                return steps

            UNIT_STEPS = 5 * 8 + 2 + 5 * 4 + 3 + 6 + 1
            with dve.Fori(0, NT) as t:
                for half in range(2):
                    n = unit(t, half, t * (2 * UNIT_STEPS) + half * UNIT_STEPS)
                    assert n == UNIT_STEPS
            dve.wait_ge(sem("gt_e"), 1)
            gates = sel[:, :, 2, :].rearrange("p t (h k) -> p t h k", k=TOPK)
            sums = den[:, 0, :].rearrange("p (t h) -> p t h", t=NT)
            rec = den[:, 1, :].rearrange("p (t h) -> p t h", t=NT)
            chain("gt_s", dve.tensor_reduce(sums, gates, AX_X, ALU.add))
            chain("gt_s", dve.reciprocal(rec, sums))
            dve.tensor_tensor(gates, gates, rec.unsqueeze(3).to_broadcast([P, NT, PH, TOPK]), ALU.mult
                              ).then_inc(sem("gt"), 1)

            for grp in range(GROUPS):
                e0, n0 = grp * EG, grp * (S // TB)

                def hot(n, r):
                    def tokens(a, keys):
                        return slot_t[:, a, bass.ds(n * TB, TB)].unsqueeze(1).to_broadcast([P, keys, TB])

                    dve.wait_ge(sem("g_mm"), n + (n0 + 1))
                    dve.tensor_tensor(eq1[:, r, :, :], iota_t[:, e0:e0 + EG, :], tokens(0, EG), ALU.is_equal
                                      ).then_inc(sem("oh1_eq"), 1)
                    dve.tensor_tensor(oh2[:, r, :, :], iota_t[:, :, :], tokens(1, NKEYS), ALU.is_equal
                                      ).then_inc(sem("oh2"), 1)
                    dve.wait_ge(sem("oh1_eq"), n + (n0 + 1))
                    dve.tensor_tensor(oh1[:, r, 2, :, :], eq1[:, r, :, :], tokens(4, EG), ALU.mult
                                      ).then_inc(sem("oh1_3"), 1)

                def weigh(n, r):
                    dve.wait_ge(sem("g_mm"), n + (n0 + 1 + 4))
                    at = ga[:, :, bass.ds(n * TB, TB)]
                    dve.tensor_tensor(at, at, ps[:, r, :].rearrange("p (t e) -> p e t", t=TB), ALU.mult
                                      ).then_inc(sem("g_mul"), 1)

                def low_v(e, r):
                    dve.wait_ge(sem("v_hi"), e * 2 + (2 * e0 + 2))
                    dve.tensor_tensor(gal[:, r, :], zt(ga, e), gah[:, r, :].bitcast(F32), ALU.subtract
                                      ).then_inc(sem("ga_lo"), 1)
                    dve.tensor_tensor(el[:, r, :], er[:, r, :], eh[:, r, :].bitcast(F32), ALU.subtract
                                      ).then_inc(sem("v_lo"), 1)

                if grp:
                    dve.wait_ge(sem("a_ev"), e0 + EG + 2)
                dve.wait_ge(sem("a_mm"), e0 + EG + 2)
                dve.wait_ge(sem("slot_t"), 4)
                if grp == 0:
                    dve.tensor_tensor(rest[:, 0, :], gate_t, slot_t[:, 2, :], ALU.subtract).then_inc(sem("gate_r"), 1)
                    dve.wait_ge(sem("gate_r"), 1)
                    dve.tensor_copy(slot_t[:, 3, :], rest[:, 0, :]).then_inc(sem("gate_r"), 1)
                    dve.wait_ge(sem("gate_r"), 2)
                    dve.tensor_tensor(rest[:, 1, :], rest[:, 0, :], slot_t[:, 3, :], ALU.subtract
                                      ).then_inc(sem("gate_r"), 1)
                    dve.wait_ge(sem("gate_r"), 3)
                    dve.tensor_copy(slot_t[:, 4, :], rest[:, 1, :]).then_inc(sem("gate_p"), 1)
                    dve.wait_ge(sem("gate_p"), 1)
                dve.tensor_copy(iota_t[:, :, :], iota.unsqueeze(2).to_broadcast([P, NKEYS, TB])
                                ).then_inc(sem("iota_t"), 1)
                dve.wait_ge(sem("iota_t"), grp + 1)
                hot(0, 0)
                hot(1, 1)
                with dve.Fori(0, S // TB // 4 - 1) as i:
                    for r in range(4):
                        hot(i * 4 + (r + 2), (r + 2) % 4)
                        weigh(i * 4 + r, r)
                n = S // TB
                hot(n - 2, 2)
                weigh(n - 4, 0)
                hot(n - 1, 3)
                for r in range(1, 4):
                    weigh(n - 4 + r, r)
                rolled(dve, EG, 2, low_v)
                dve.wait_ge(sem("v_used"), e0 + EG + 2)
                if grp == 0:
                    for c in range(KD):
                        dve.tensor_copy(ga[:, c, :], ps[:, c, :]).then_inc(sem("e_part"), 1)
            dve.wait_ge(sem("x_back"), 32)
            for c in range(KD):
                dve.tensor_tensor(xf[:, c, :], xf[:, c, :], pf[:, c, :], ALU.add).then_inc(sem("y_part"), 1)
            dve.wait_ge(sem("v_used"), GROUPS * EG + 2)
            for c in range(KD):
                dve.wait_ge(sem("y_part"), c + 1)
                dve.tensor_tensor(xf[:, c, :], xf[:, c, :], ps[:, c, :], ALU.add).then_inc(sem("y_sum"), 1)
            dve.wait_ge(sem("nm_rs"), 5)
            for k in range(KD):
                dve.scalar_tensor_tensor(pf[:, k, :], xf[:, k, :], v("final", k), fln[:, 1, :], ALU.mult, ALU.mult
                                         ).then_inc(sem("y_t"), 1)


def constants():
    i = np.arange(P)
    same64 = (i[:, None] // HD == i[None, :] // HD).astype(np.float32)
    half = HD // 2
    turn = np.zeros((P, P), np.float32)
    for m in range(P):
        if m % HD < half:
            turn[m + half, m] = -1.0
        else:
            turn[m - half, m] = 1.0
    tables = {
        "ident": np.eye(P, dtype=np.float32),
        "blk64": same64 / HD,
        "mean": np.full((P, P), 1.0 / D, np.float32),
        "negtri": -(i[:, None] >= i[None, :]).astype(np.float32),
        "negone": np.full((P, P), -1.0, np.float32),
        "rot": turn,
        "iota": np.broadcast_to(i.astype(np.float32)[None, :], (P, P)),
    }
    return np.ascontiguousarray(np.stack([tables[n] for n in CST], axis=1).astype(np.float32))


def kernel(**inputs):
    import concourse.bacc as bacc
    from concourse.bass_utils import run_bass_kernel_spmd

    a = {k: np.asarray(x) for k, x in inputs.items()}

    def cols(x):
        return x.reshape(-1, P).T

    half = HD // 2
    inv = 10000.0 ** (-(np.arange(half, dtype=np.float32) * np.float32(2.0) / np.float32(HD)))
    packed = {
        "attn_norm": cols(a["attn_norm_w"][0]), "ffn_norm": cols(a["ffn_norm_w"][0]), "norm1": cols(a["norm1_g_2"][0]),
        "norm2": cols(a["norm2_g_2"][0]), "final": cols(a["final_g_2"]), "out_norm": cols(a["out_norm_w"][0]),
        "qn": np.tile(a["q_norm_w"][0], 2)[:, None], "kn": np.tile(a["k_norm_w"][0], 2)[:, None],
        "conv": a["conv_w"][0].reshape(3, CV_TILES, P).transpose(2, 1, 0).reshape(P, -1),
        "b_in": cols(a["b_in_2"][0]),
        "conv2": a["conv_w_2"][0].reshape(TAPS, KD, P).transpose(2, 1, 0).reshape(P, -1),
        "conv2_b": cols(a["conv_b_2"][0]), "ln_g": cols(a["conv_ln_g_2"][0]), "ln_b": cols(a["conv_ln_b_2"][0]),
        "sinks": np.tile(a["attn_sinks_2"], (P, 1)),
        "inv": np.tile(inv.astype(np.float32), P // half)[:, None],
        "eps": np.full((P, 1), EPS, np.float32), "one": np.ones((P, 1), np.float32),
    }
    vec = np.concatenate([packed[n] for n, _ in VECS], axis=1)
    assert vec.shape == (P, NVEC)
    far = np.clip(S - P + np.arange(P)[:, None] - np.arange(S)[None, :], -P, P) + P

    def by_cols(w):
        return w.reshape(KD, P, -1, 256).transpose(2, 1, 0, 3).reshape(-1, P, 2048)

    gate_up = np.stack([by_cols(a["w_gate"][0]), by_cols(a["w_up"][0])], axis=1).reshape(-1, P, 2048)
    down = a["w_down"][0].reshape(-1, 2, P, D).transpose(0, 2, 1, 3).reshape(-1, P, 2048)
    slots = [by_cols(a["w_in"][0]), by_cols(a["w_out"][0]), gate_up, down, by_cols(a["w_in_2"][0]),
             by_cols(a["w_conv_out_2"][0]), by_cols(a["w_attn_o_2"][0]), by_cols(a["w_out_2"][0]),
             by_cols(a["w_peer_q_2"][0])]
    assert [x.shape[0] for x in slots] == [c for _, c in SLOTS]
    arrays = {
        "x": a["x"][0].reshape(S, KD, P).transpose(2, 1, 0), "cst": constants(), "vec": vec,
        "rel_tiles": a["rel_bias"][0][:, far], "positions": np.tile(a["positions_2"], (P, 1)),
        "w_slots": np.concatenate(slots),
        "sub_keys": a["peer_sub_keys_2"][0].reshape(HC, NKEYS, P).transpose(2, 0, 1),
        "u_tiles": a["peer_u_2"][0].reshape(NKEYS, P, KD, P).transpose(0, 3, 2, 1).reshape(NKEYS, P, D),
        "v_tiles": a["peer_v_2"][0].reshape(NKEYS, P, D),
    }
    arrays = {f"in_{n}": np.ascontiguousarray(x) for n, x in arrays.items()}

    nc = bacc.Bacc("TRN2", target_bir_lowering=False, num_devices=1)
    ins = {n[3:]: nc.dram_tensor(n, x.shape, mybir.dt.from_np(x.dtype), kind="ExternalInput").ap()
           for n, x in arrays.items()}
    out = nc.dram_tensor("out", (P, KD, S), F32, kind="ExternalOutput").ap()
    build(nc, ins, out)
    r = run_bass_kernel_spmd(nc, [arrays], core_ids=[0])
    return r.results[0]["out"].transpose(2, 1, 0).reshape(1, S, D)
```

```python
from contextlib import ExitStack

import concourse.bass as bass
import numpy as np
from concourse import mybir

F32 = mybir.dt.float32
F32R = mybir.dt.float32r
F16 = mybir.dt.float16
I32 = mybir.dt.int32
U32 = mybir.dt.uint32
ALU = mybir.AluOpType
ACT = mybir.ActivationFunctionType
AX_X = mybir.AxisListType.X

P = 128
S = 512
D = 1024
KD = D // P
NT = S // P
EPS = 1e-6
HD = 64
SCALE = HD ** -0.5
NEG = -1e30

SB_PAIRS, CH_PAIRS, CV_TILES = 2, 4, 2
QA, KA, VA = 0, 2, 4
QB, KB, VB = 6, 10, 14
GB, GC, XC = 18, 20, 22
Z1_TILES = 24
FF_TILES = 22

VAL, GATE, Q2, K2, V2, GCONV, GATTN = 0, 8, 16, 24, 25, 26, 34
Z2_TILES = 42
TAPS = 31
SWA_PAIRS = 8
PAIRS_PER_KV = 4
STEPS = 2 * NT

PH = 8
HC = 2 * PH
NKEYS = 128
TOPK = 16
GROUPS = 2
EG = NKEYS // GROUPS
TB = 8
GATE_SCALE = 2.0 ** 15

TB_ACT = 6

SLOTS = [("in1", Z1_TILES // 2), ("out1", 4), ("ffn", FF_TILES), ("down", FF_TILES // 2),
         ("in2", Z2_TILES // 2), ("co", 4), ("ao", 4), ("out2", 4), ("pq", 8)]
FIRST = {}
_at = 0
for _n, _c in SLOTS:
    FIRST[_n] = _at
    _at += _c
N_SLOTS = _at
COUNT = dict(SLOTS)

CST = ["ident", "mean", "iota", "blk64", "negtri", "negone", "rot"]
VECS = [("attn_norm", 8), ("ffn_norm", 8), ("norm1", 8), ("norm2", 8), ("final", 8), ("out_norm", 8),
        ("qn", 1), ("kn", 1), ("conv", 6), ("b_in", Z2_TILES), ("conv2", TAPS * 8), ("conv2_b", 8),
        ("ln_g", 8), ("ln_b", 8), ("sinks", 16), ("inv", 1), ("eps", 1), ("one", 1)]
VAT = {}
_at = 0
for _n, _c in VECS:
    VAT[_n] = _at
    _at += _c
NVEC = _at

SPLITS = ["n0", "gn", "n1", "n2", "ln", "at", "mg", "n3"]


def rolled(eng, n, unroll, body):
    full = n // unroll
    if full > 1:
        with eng.Fori(0, full) as i:
            for r in range(unroll):
                body(i * unroll + r, r)
    elif full == 1:
        for r in range(unroll):
            body(r, r)
    for r in range(n - full * unroll):
        body(full * unroll + r, r)


def build(nc, ins, out):
    with ExitStack() as ctx:
        def sb(name, shape, dt=F32):
            return ctx.enter_context(nc.sbuf_tensor(name, shape, dt))

        sems = {}

        def sem(name):
            if name not in sems:
                sems[name] = ctx.enter_context(nc.semaphore(name))
            return sems[name]

        cst = sb("cst", [P, len(CST), P])
        vec = sb("vec", [P, NVEC])
        ident, mean, iota, blk64, negtri, negone, rot = (cst[:, i, :] for i in range(len(CST)))

        def v(name, i=0, n=1):
            return vec[:, VAT[name] + i:VAT[name] + i + n]

        def vd(name, i, n=1):
            return vec[:, VAT[name]:VAT[name] + dict(VECS)[name]][:, bass.ds(i, n)]

        ps = ctx.enter_context(nc.psum_tensor("ps", [P, 8, S], F32))
        hh = sb("hh", [P, KD, S], F32R)
        hl = sb("hl", [P, KD, S], F32R)

        early = ExitStack()

        def esb(name, shape, dt=F32, stack=None):
            return (stack or early).enter_context(nc.sbuf_tensor(name, shape, dt))

        xT = esb("xT", [P, KD, S])
        raw = esb("raw", [P, 2, 2048])
        wh = esb("wh", [P, 2, 2048], F32R)
        wl = esb("wl", [P, 2, 2048], F32R)
        tmp = esb("tmp", [P, 2, S])
        sqb = esb("sqb", [P, 2, S])
        lnb = esb("lnb", [P, 2, S])

        one = ExitStack()
        z1 = esb("z1", [P, Z1_TILES, S], stack=one)
        yT = esb("yT", [P, KD, S], stack=one)
        bt = esb("bt", [P, 8, S], stack=one)
        kst, qst = tmp[:, 0, :], tmp[:, 1, :]
        spl = yT[:, SB_PAIRS:SB_PAIRS + NT, :]
        sb_in = ExitStack()
        vts = esb("vts", [P, S], stack=sb_in)
        vst = esb("vst", [P, NT, P], stack=sb_in)
        ab = esb("ab", [P, NT, S], stack=sb_in)
        sb_in.close()
        csc, cpr, cpt = (z1[:, 2 * i:2 * i + 2, :] for i in range(3))
        ch_in = ExitStack()
        ckst = esb("ckst", [P, S], stack=ch_in)
        cqst = esb("cqst", [P, S], stack=ch_in)
        cvts = esb("cvts", [P, S], stack=ch_in)
        cvst = esb("cvst", [P, NT, P], stack=ch_in)
        cstat = esb("cstat", [P, 2, 4], stack=ch_in)
        ch_in.close()
        one.close()

        ffn = ExitStack()
        hidh = esb("hidh", [P, FF_TILES, S], F32R, stack=ffn)
        hidl = esb("hidl", [P, FF_TILES, S], F32R, stack=ffn)
        sg, hid = sqb, tmp
        ffn.close()

        two = ExitStack()
        z2 = esb("z2", [P, Z2_TILES, S], stack=two)
        csin = esb("csin", [P, 2, S], stack=two)
        msk = esb("msk", [P, 2 * P], stack=two)
        sstat = esb("sstat", [P, 2, 16], stack=two)
        nsink = esb("nsink", [P, 2 * SWA_PAIRS], stack=two)
        pos_in = ExitStack()
        pos_i = esb("pos_i", [P, S], I32, stack=pos_in)
        pos_in.close()
        kdup = esb("kdup", [P, 2, S], stack=two)
        rq = sqb
        rt = z2[:, GATE + 6:GATE + 8, :]
        ssc, spr, spt = (z2[:, GATE + 2 * i:GATE + 2 * i + 2, :].rearrange("p r (e n) -> p r e n", e=2)
                         for i in range(3))
        vn_pairs = tmp[:, :, 2 * P:4 * P]
        two.close()

        rout = ExitStack()
        qT = esb("qT", [P, HC, S], stack=rout)
        skT = esb("skT", [P, HC, P], stack=rout)
        scev = esb("scev", [P, 4, 4, P], stack=rout)
        rout.close()
        early.close()

        late = ExitStack()
        ga = esb("ga", [P, EG, S], stack=late)
        er = esb("er", [P, 2, D], stack=late)
        slot_t = esb("slot_t", [P, 4, S], F16, stack=late)
        gate_t = cst[:, CST.index("blk64"):, :].rearrange("p a n -> p (a n)")
        uv = ExitStack()
        eh = esb("eh", [P, 2, D], F32R, stack=uv)
        el = esb("el", [P, 2, D], F32R, stack=uv)
        tk = ExitStack()
        sc = esb("sc", [P, 8, NKEYS], stack=tk)
        top = esb("top", [P, 8, TOPK], stack=tk)
        topi = esb("topi", [P, 8, TOPK], U32, stack=tk)
        topf = esb("topf", [P, 8, TOPK], stack=tk)
        best = esb("best", [P, 4, TOPK], stack=tk)
        bpos = esb("bpos", [P, 4, TOPK], U32, stack=tk)
        sel = esb("sel", [P, NT, 3, PH * TOPK], stack=tk)
        bab = esb("bab", [P, 2, 4 * TOPK], U32, stack=tk)
        bfl = esb("bfl", [P, 2, 4 * TOPK], stack=tk)
        den = esb("den", [P, 2, NT * PH], stack=tk)
        tk.close()
        gv = ExitStack()
        gah = esb("gah", [P, 2, S], F32R, stack=gv)
        gal = esb("gal", [P, 2, S], F32R, stack=gv)
        iota_t = esb("iota_t", [P, NKEYS, TB], F16, stack=gv)
        gv.close()
        uv.close()
        oh = ExitStack()
        oh2 = esb("oh2", [P, 4, NKEYS, TB], F16, stack=oh)
        eq1 = esb("eq1", [P, 4, EG, TB], F16, stack=oh)
        oh1 = esb("oh1", [P, 4, 2, EG, TB], F16, stack=oh)
        oh.close()
        late.close()
        xf, pf = ga[:, 0:KD, :], ga[:, KD:2 * KD, :]
        fsq, fln = ga[:, 2 * KD:2 * KD + 2, :], ga[:, 2 * KD + 2:2 * KD + 4, :]

        x_dram = nc.dram_tensor("x_spill", [P, KD, S], F32).ap()
        e_dram = nc.dram_tensor("expert_spill", [P, KD, S], F32).ap()
        sc_dram = nc.dram_tensor("score_spill", [2 * NT, P, PH, NKEYS], F32).ap()

        u_tiles, v_tiles = ins["u_tiles"], ins["v_tiles"]

        def piece(w, b, k, half):
            return w[:, b, :].rearrange("p (k n) -> p k n", k=KD)[:, k, half * P:half * P + P]

        def piece_down(w, b, j, c):
            return w[:, b, :].rearrange("p (j n) -> p j n", j=2)[:, j, c * P:c * P + P]

        def vn(t):
            return vn_pairs[:, t // 2, (t % 2) * P:(t % 2) * P + P]

        def split_base(name):
            return 8 * SPLITS.index(name)

        block = ctx.enter_context(nc.Block())

        def zt(z, n):
            return z[:, bass.ds(n, 1), :].rearrange("p a n -> p (a n)")

        def tile_done(eng, name, s, half):
            if half:
                eng.wait_ge(sem("w_used"), s + (FIRST[name] + 3))
            else:
                eng.wait_ge(sem("mm_" + name), s + 1)

        def pass_by(eng, signal, count):
            eng.wait_ge(sem(signal), count)
            eng.sem_inc(sem("waits_past"), 1)

        def all_steps(eng, rounds, step):
            with eng.Fori(0, rounds - 1) as j:
                for r in range(STEPS):
                    step(j, r, False)
            for r in range(STEPS):
                step(rounds - 1, r, True)

        def ahead(j, r, n):
            return (j + 1, r + n - STEPS) if r + n >= STEPS else (j, r + n)

        def swa_cols(r):
            return P if r % NT == 0 else 0

        def bank_of(name, n):
            return (2 * FIRST[name] + n) % 4

        @block.sync
        def _(sp):
            for a in range(2):
                sp.dma_start(xT[:, 4 * a:4 * a + 4, :], ins["x"][:, 4 * a:4 * a + 4, :]).then_inc(sem(f"x_in{a}"), 16)

            def load(g, b):
                sp.wait_ge(sem("w_lo"), g + 1)
                sp.dma_start(raw[:, b, :], ins["w_slots"][bass.ds(g, 1), :, :].rearrange("g p n -> p (g n)")
                             ).then_inc(sem(f"w_raw{b}"), 16)

            rolled(sp, N_SLOTS, 2, load)
            sp.wait_ge(sem("x_tile"), 8 * 4)
            sp.dma_start(x_dram, xT[:, :, :]).then_inc(sem("x_spilled"), 16)
            sp.dma_start(skT[:, :, :], ins["sub_keys"]).then_inc(sem("sk_loaded"), 16)
            def load_u(e, r):
                sp.wait_ge(sem("u_lo"), e + 1)
                sp.dma_start(er[:, r, :], u_tiles[bass.ds(e, 1), :, :].rearrange("e p n -> p (e n)")
                             ).then_inc(sem(f"u_in{r}"), 16)

            def load_v(e, r):
                sp.wait_ge(sem("v_lo"), e + 1)
                sp.dma_start(er[:, r, :], v_tiles[bass.ds(e, 1), :, :].rearrange("e p n -> p (e n)")
                             ).then_inc(sem(f"v_in{r}"), 16)

            load_u(0, 0)
            load_u(1, 1)
            for n in range(NT * 4):
                sp.wait_ge(sem("sc_copied"), n + 1)
                sp.dma_start(sc_dram[n // 2, :, 4 * (n % 2):4 * (n % 2) + 4, :], scev[:, n % 4, :, :]
                             ).then_inc(sem(f"sc_out{n % 4}"), 16)
            for r in range(4):
                sp.wait_ge(sem(f"sc_out{r}"), 16 * NT)
            sp.wait_ge(sem("x_spilled"), 16)
            sp.sem_inc(sem("late_free"), 1)
            for grp in range(GROUPS):
                e0 = grp * EG

                if grp:
                    rolled(sp, EG - 2, 2, lambda e, r: load_u(e + (e0 + 2), r))
                else:
                    per_unit = EG // (2 * NT)

                    def load_scores(m, tiles):
                        sp.wait_ge(sem("tk_unit"), m + 1)
                        sp.dma_start(sc[:, :, :], sc_dram[bass.ds(m, 1), :, :, :].rearrange("m p a n -> p (m a) n")
                                     ).then_inc(sem("sc_in"), 16)
                        for j in range(tiles):
                            load_u(m * per_unit + (j + 2), j % 2)

                    with sp.Fori(0, 2 * NT - 1) as m:
                        load_scores(m, per_unit)
                    load_scores(2 * NT - 1, per_unit - 2)
                sp.wait_ge(sem("u_lo"), e0 + EG + 2)
                rolled(sp, EG, 2, lambda e, r: load_v(e + e0, r))
                if grp == 0:
                    sp.wait_ge(sem("v_lo"), EG + 2)
                    load_u(EG, 0)
                    load_u(EG + 1, 1)
                    sp.wait_ge(sem("e_part"), KD)
                    sp.dma_start(e_dram, ga[:, 0:KD, :]).then_inc(sem("e_spilled"), 16)
            sp.wait_ge(sem("v_used"), (GROUPS - 1) * EG + 2 * KD + 4 + 2)
            sp.dma_start(xf, x_dram).then_inc(sem("x_back"), 16)
            sp.dma_start(pf, e_dram).then_inc(sem("x_back"), 16)
            for k in range(KD):
                sp.wait_ge(sem("y_t"), k + 1)
                sp.dma_start(out[:, k, :], pf[:, k, :]).then_inc(sem("out_done"), 16)
            sp.wait_ge(sem("out_done"), 16 * KD)

        @block.gpsimd
        def _(pool):
            for name in ("w_lo", "sp_l", "hid_l", "u_lo"):
                pool.sem_inc(sem(name), 2)
            def low(g, b):
                pool.wait_ge(sem("w_hi"), g + 1)
                pool.tensor_tensor(wl[:, b, :], raw[:, b, :], wh[:, b, :].bitcast(F32), ALU.subtract
                                   ).then_inc(sem("w_lo"), 1)

            def lows(a, b):
                rolled(pool, b - a, 2, lambda s, r: low(s + a, (a + r) % 2))

            def split_low(name):
                base = split_base(name)
                for k in range(KD):
                    pool.wait_ge(sem("sp_h"), base + k + 1)
                    pool.tensor_tensor(hl[:, k, :], tmp[:, k % 2, :], hh[:, k, :].bitcast(F32), ALU.subtract
                                       ).then_inc(sem("sp_l"), 1)

            lows(0, 2)
            split_low("n0")
            pool.dma_start(bt[:, :, :], ins["rel_tiles"].rearrange("h p m -> p h m")).then_inc(sem("bt_loaded"), 16)
            lows(2, FIRST["out1"] + 2)
            pool.wait_ge(sem("bt_loaded"), 16)
            pool.memset(bt[0:64, :, 448:512], NEG).then_inc(sem("bt_ready"), 1)
            with pool.Fori(0, SB_PAIRS) as p:
                for e in range(2):
                    for tile, ready, done in ((spl, "sb_sp0", "sb_sp"), (ab, "sb_w0", "sb_w")):
                        for q, b in enumerate(reversed(range(NT))):
                            pass_by(pool, ready, p * 8 + (4 * e + q + 1))
                            pool.affine_select(out=tile[:, b, 0:P], in_=tile[:, b, 0:P], pattern=[[1, P]],
                                               compare_op=ALU.is_gt, fill=0.0, base=0, channel_multiplier=-1
                                               ).then_inc(sem(done), 1)
            pool.wait_ge(sem("sb_y"), SB_PAIRS + 1)
            with pool.Fori(0, CH_PAIRS) as p:
                pool.wait_ge(sem("ch_vt"), p + 1)
                pool.tensor_copy(cvts[:, :], zt(z1, p + VB)).then_inc(sem("ch_vs"), 1)
            split_low("gn")
            lows(FIRST["out1"] + 2, FIRST["ffn"] + 2)
            split_low("n1")
            with pool.Fori(0, FF_TILES // 2) as i:
                for q in range(2):
                    low(i * 2 + (FIRST["ffn"] + 2 + q), q)
                for q in range(2):
                    pool.wait_ge(sem("hid_h"), i * 2 + (q + 1))
                    pool.tensor_tensor(zt(hidl, i * 2 + q), hid[:, q, :], zt(hidh, i * 2 + q).bitcast(F32),
                                       ALU.subtract).then_inc(sem("hid_l"), 1)
            lows(FIRST["down"] + 2, FIRST["in2"] + 2)
            split_low("n2")
            pool.memset(msk[:, :], 0.0).then_inc(sem("msk"), 1)
            pool.wait_ge(sem("msk"), 1)
            pool.affine_select(out=msk[:, :], in_=msk[:, :], pattern=[[1, 2 * P]], compare_op=ALU.is_gt, fill=NEG,
                               base=0, channel_multiplier=-1).then_inc(sem("msk"), 1)
            pool.wait_ge(sem("msk"), 2)
            pool.affine_select(out=msk[:, :], in_=msk[:, :], pattern=[[-1, 2 * P]], compare_op=ALU.is_ge, fill=NEG,
                               base=P, channel_multiplier=1).then_inc(sem("msk"), 1)
            lows(FIRST["in2"] + 2, FIRST["co"] + 2)
            split_low("ln")
            lows(FIRST["co"] + 2, FIRST["ao"] + 2)
            pool.wait_ge(sem("kd"), 4)

            def rotary(j, kv):
                n = j * 2 + kv
                if not (isinstance(j, int) and j == 0):
                    pool.wait_ge(sem("sw_sc"), (j - 1) * STEPS + (kv * NT + NT))
                pool.wait_ge(sem("rh"), n + 1)
                pool.tensor_tensor(rt[:, kv, :], rt[:, kv, :], csin[:, 1, :], ALU.mult).then_inc(sem("rq_a"), 1)
                pool.tensor_tensor(rq[:, kv, :], zt(z2, j + (Q2 + kv * PAIRS_PER_KV)), csin[:, 0, :], ALU.mult
                                   ).then_inc(sem("rq_a"), 1)
                pool.wait_ge(sem("rq_a"), n * 2 + 2)
                pool.tensor_tensor(rq[:, kv, :], rq[:, kv, :], rt[:, kv, :], ALU.add).then_inc(sem("rq"), 1)

            for kv in range(2):
                rotary(0, kv)

            def low_out(j, kv):
                pool.wait_ge(sem("sp_h"), j * 2 + (split_base("at") + kv + 1))
                k = j + kv * PAIRS_PER_KV
                pool.tensor_tensor(zt(hl, k), zt(z2, k), zt(hh, k).bitcast(F32), ALU.subtract).then_inc(sem("sp_l"), 1)

            with pool.Fori(1, PAIRS_PER_KV) as j:
                for kv in range(2):
                    rotary(j, kv)
                    low_out(j - 1, kv)
            for kv in range(2):
                low_out(PAIRS_PER_KV - 1, kv)
            lows(FIRST["ao"] + 2, FIRST["out2"] + 2)
            split_low("mg")
            lows(FIRST["out2"] + 2, FIRST["pq"] + 2)
            split_low("n3")
            lows(FIRST["pq"] + 2, N_SLOTS)

            for grp in range(GROUPS):
                def low_u(e, r):
                    pool.wait_ge(sem("u_hi"), e + (grp * EG + 1))
                    pool.tensor_tensor(el[:, r, :], er[:, r, :], eh[:, r, :].bitcast(F32), ALU.subtract
                                       ).then_inc(sem("u_lo"), 1)

                def second_part(n, r):
                    gn = n + (grp * (S // TB) + 1)
                    pool.wait_ge(sem("g_mm"), gn)
                    pass_by(pool, "oh1_eq", gn)
                    pool.tensor_tensor(oh1[:, r, 1, :, :], eq1[:, r, :, :],
                                       slot_t[:, 3, bass.ds(n * TB, TB)].unsqueeze(1).to_broadcast([P, EG, TB]),
                                       ALU.mult).then_inc(sem("oh1_2"), 1)
                    pool.tensor_tensor(oh1[:, r, 0, :, TB_ACT:], eq1[:, r, :, TB_ACT:],
                                       slot_t[:, 2, bass.ds(n * TB + TB_ACT, TB - TB_ACT)].unsqueeze(1
                                                                           ).to_broadcast([P, EG, TB - TB_ACT]),
                                       ALU.mult).then_inc(sem("oh1_2"), 1)

                rolled(pool, EG, 2, low_u)
                pool.wait_ge(sem("gate_p"), 1)
                rolled(pool, S // TB, 4, second_part)

        @block.scalar
        def _(act):
            act.dma_start(cst[:, :, :], ins["cst"]).then_inc(sem("c_loaded"), 16)
            act.dma_start(vec[:, :], ins["vec"]).then_inc(sem("c_loaded"), 16)

            def high(g, b):
                act.wait_ge(sem(f"w_raw{b}"), g * 8 + (16 - 8 * b))
                act.wait_ge(sem("w_used"), g + 1)
                act.activation(wh[:, b, :], raw[:, b, :], ACT.Copy).then_inc(sem("w_hi"), 1)

            def highs_and_squares(name, n):
                for s in range(COUNT[name]):
                    if s:
                        for k in (2 * s - 2, 2 * s - 1):
                            x_squares(n, k, xT, "x_tile", 8 * n, sqb)
                    high(s + (FIRST[name] + 2), (FIRST[name] + s) % 2)

            def highs(name):
                g0 = FIRST[name]
                rolled(act, COUNT[name], 2, lambda s, r: high(s + (g0 + 2), (g0 + r) % 2))

            def split_high(name):
                base = split_base(name)
                for k in range(KD):
                    act.wait_ge(sem("sp_t"), base + k + 1)
                    act.activation(hh[:, k, :], tmp[:, k % 2, :], ACT.Copy).then_inc(sem("sp_h"), 1)

            def rstd(ms, scratch, dst, done, count):
                act.activation(scratch, ms, ACT.Ln, bias=v("eps")).then_inc(sem(done + "_ln"), 1)
                act.wait_ge(sem(done + "_ln"), count)
                act.activation(dst, scratch, ACT.Exp, scale=-0.5).then_inc(sem(done + "_rs"), 1)

            def x_squares(n, k, x, ready, first, sq):
                act.wait_ge(sem(ready), first + k + 1)
                act.wait_ge(sem("nm_mm"), 8 * n + k + 1)
                act.activation(sq[:, k % 2, :], x[:, k, :], ACT.Square).then_inc(sem("nm_sq"), 1)

            def norm(n, x, ready, first, sq, ln, bank=4, done=0):
                for k in range(done, KD):
                    x_squares(n, k, x, ready, first, sq)
                act.wait_ge(sem("nm_mm"), 8 * n + 8 + 2)
                rstd(ps[:, bank, :], ln[:, 0, :], ln[:, 1, :], "nm", n + 1)

            def evacuate(name, first, last, tile, ahead=True):
                g0 = FIRST[name]

                def slot(s, r):
                    g = g0 + first // 2 + r
                    for half in range(2):
                        tile_done(act, name, s + first // 2, half)
                        tile(s * 2 + (first + half), 2 * (g % 2) + half)
                    if ahead:
                        high(s + (g0 + first // 2 + 2), g % 2)

                rolled(act, (last - first) // 2, 2, slot)

            def ln_exp_tables():
                act.preload_act_table_set("natural_log_exp_and_others")

            ln_exp_tables()
            for a in range(2):
                for k in range(4 * a, 4 * a + 4):
                    x_squares(0, k, xT, "x_tile", 0, sqb)
                high(a, a)
            act.wait_ge(sem("c_loaded"), 32)
            norm(0, xT, "x_tile", 0, sqb, lnb, done=KD)
            split_high("n0")

            def z1_tile(n, bank):
                act.activation(zt(z1, n), ps[:, bank, :], ACT.Copy).then_inc(sem("ev_in1"), 1)

            evacuate("in1", 0, Z1_TILES, z1_tile)

            with act.Fori(0, SB_PAIRS) as p:
                act.wait_ge(sem("sb_vt"), p + 1)
                act.activation(vst[:, :, :], ps[:, 5, :].rearrange("p (t n) -> p t n", t=NT), ACT.Copy
                               ).then_inc(sem("sb_v"), 1)
                for e in range(2):
                    if e:
                        act.wait_ge(sem("sb_pv"), p * 2 + 1)
                    for q, b in enumerate(reversed(range(NT))):
                        w = S - b * P
                        n = p * 8 + (4 * e + q + 1)
                        act.wait_ge(sem("sb_z"), n)
                        act.activation(ab[:, b, 0:w], ps[:, b, 0:w], ACT.Abs).then_inc(sem("sb_abs"), 1)
                        act.wait_ge(sem("sb_abs"), n)
                        act.activation(ab[:, b, 0:w], ab[:, b, 0:w], ACT.Exp, scale=-1.0).then_inc(sem("sb_e"), 1)
                        act.wait_ge(sem("sb_e"), n)
                        act.activation(ab[:, b, 0:w], ab[:, b, 0:w], ACT.Ln, bias=v("one")).then_inc(sem("sb_l"), 1)
                    for q, b in enumerate(reversed(range(NT))):
                        w = S - b * P
                        n = p * 8 + (4 * e + q + 1)
                        act.wait_ge(sem("sb_cum"), n)
                        act.activation(ab[:, b, 0:w], ps[:, b, 0:w], ACT.Exp).then_inc(sem("sb_w0"), 1)
                act.wait_ge(sem("sb_pv"), p * 2 + 2)
                act.activation(zt(yT, p), ps[:, 4, :], ACT.Copy).then_inc(sem("sb_y"), 1)

            act.wait_ge(sem("sb_y"), SB_PAIRS + 1)

            def squares(p):
                for w, src in enumerate((QB, KB)):
                    if not (isinstance(p, int) and p == 0):
                        act.wait_ge(sem("ch_ms"), p * 2 + (w - 1))
                    act.activation(sqb[:, w, :], zt(z1, p + src), ACT.Square).then_inc(sem("ch_sq"), 1)

            def rstds(p):
                act.wait_ge(sem("ch_qk"), p * 4 + 2)
                for w in range(2):
                    act.wait_ge(sem("ch_ms"), p * 2 + (w + 1))
                    rstd(ps[:, 6 + w, :], lnb[:, w, :], lnb[:, w, :], "ch", p * 2 + (w + 1))

            def turned_values(p, e):
                act.wait_ge(sem("ch_vt"), p + 2)
                act.wait_ge(sem("ch_o"), p * STEPS + (NT * e + 2 - NT))
                act.activation(cvst[:, :, HD * e:HD * e + HD],
                               ps[:, 5, :].rearrange("p (t n) -> p t n", t=NT)[:, :, HD * e:HD * e + HD], ACT.Copy
                               ).then_inc(sem("ch_v"), 1)

            def weights(p, r):
                w = (r % NT + 1) * P
                act.wait_ge(sem("ch_m"), p * STEPS + (r + 1))
                act.activation(cpr[:, r % 2, 0:w], csc[:, r % 2, 0:w], ACT.Exp, bias=cstat[:, r % 2, 0:1],
                               accum_out=cstat[:, r % 2, 1:2]).then_inc(sem("ch_e"), 1)

            def turned_weights(p, r):
                w = (r % NT + 1) * P
                act.wait_ge(sem("ch_t"), p * STEPS + (r + 1))
                act.wait_ge(sem("ch_o"), p * STEPS + (r + 1))
                act.activation(cpt[:, r % 2, 0:w], ps[:, 2 + r % 2, 0:w], ACT.Copy).then_inc(sem("ch_pt"), 1)

            def head_out(p, e):
                h = slice(HD * e, HD * e + HD)
                act.wait_ge(sem("ch_o"), p * STEPS + (NT * e + NT + 2))
                act.activation(zt(yT, p + SB_PAIRS)[h, :], ps[h, 4, :], ACT.Copy).then_inc(sem("ch_y"), 1)

            def step(p, r, last):
                if not last and r == 1:
                    squares(p + 1)
                if not last and r == 3:
                    rstds(p + 1)
                if not last or r + 1 < STEPS:
                    weights(*ahead(p, r, 1))
                turned_weights(p, r)
                if r == 1:
                    turned_values(p, 1)
                if r == NT + 1:
                    head_out(p, 0)
                    if not last:
                        turned_values(p + 1, 0)
                if r == STEPS - 1:
                    head_out(p, 1)

            squares(0)
            rstds(0)
            act.wait_ge(sem("ch_vt"), 2)
            act.activation(cvst[:, :, 0:HD], ps[:, 5, :].rearrange("p (t n) -> p t n", t=NT)[:, :, 0:HD], ACT.Copy
                           ).then_inc(sem("ch_v"), 1)
            weights(0, 0)
            all_steps(act, CH_PAIRS, step)

            act.wait_ge(sem("cv_y"), CV_TILES)
            act.wait_ge(sem("ch_y"), 2 * CH_PAIRS + 2)

            def group_squares(j):
                act.wait_ge(sem("gn_mm"), j + 1)
                act.activation(sqb[:, j % 2, :], yT[:, j, :], ACT.Square).then_inc(sem("gn_sq"), 1)

            def group_high(j):
                act.wait_ge(sem("sp_t"), split_base("gn") + j + 1)
                act.activation(hh[:, j, :], tmp[:, j % 2, :], ACT.Copy).then_inc(sem("sp_h"), 1)

            group_squares(0)
            for j in range(KD):
                if j + 1 < KD:
                    group_squares(j + 1)
                act.wait_ge(sem("gn_mm"), j + 3)
                act.wait_ge(sem("sp_t"), split_base("gn") + j - 1)
                rstd(ps[:, 4 + j % 2, :], lnb[:, j % 2, :], lnb[:, j % 2, :], "gn", j + 1)
                if j:
                    group_high(j - 1)
            group_high(KD - 1)
            highs_and_squares("out1", 1)
            norm(1, xT, "x_tile", 8, sqb, lnb, done=6)
            split_high("n1")

            g0 = FIRST["ffn"]
            act.preload_act_table(ACT.Silu)
            with act.Fori(0, FF_TILES // 2) as i:
                for q in range(2):
                    if q:
                        act.wait_ge(sem("w_used"), i * 2 + (g0 + 3))
                    else:
                        act.wait_ge(sem("mm_g"), i + 1)
                    act.wait_ge(sem("ffn_u"), i * 2 + (q + 1))
                    act.activation(sg[:, q, :], ps[:, q, :], ACT.Silu).then_inc(sem("ffn_g"), 1)
                for q in range(2):
                    high(i * 2 + (g0 + 2 + q), q)
                for q in range(2):
                    act.wait_ge(sem("ffn_u"), i * 2 + (q + 3))
                    act.activation(zt(hidh, i * 2 + q), hid[:, q, :], ACT.Copy).then_inc(sem("hid_h"), 1)
            highs("down")
            act.wait_ge(sem("w_used"), FIRST["in2"] + 2)
            act.dma_start(pos_i[:, :], ins["positions"]).then_inc(sem("pos_loaded"), 16)
            ln_exp_tables()
            norm(2, xT, "x_tile", 16, sqb, lnb, bank=0)
            split_high("n2")

            def z2_tile(func):
                def tile(n, bank):
                    act.activation(zt(z2, n), ps[:, bank, :], func, bias=vd("b_in", n)).then_inc(sem("ev_in2"), 1)
                return tile

            act.preload_act_table(ACT.Sigmoid)
            evacuate("in2", VAL, GATE, z2_tile(ACT.Identity))
            evacuate("in2", GATE, Q2, z2_tile(ACT.Sigmoid))
            evacuate("in2", Q2, GCONV, z2_tile(ACT.Identity))
            evacuate("in2", GCONV, Z2_TILES, z2_tile(ACT.Sigmoid))

            act.wait_ge(sem("rp_a"), 1)
            act.activation(csin[:, :, :], csin[:, :, :], ACT.Sin).then_inc(sem("rp_s"), 1)

            ln_exp_tables()
            for j in range(KD):
                act.wait_ge(sem("ln_x"), j + 1)
                act.wait_ge(sem("ln_v"), j + 1)
                act.activation(sqb[:, j % 2, :], z2[:, GATE + j, :], ACT.Square).then_inc(sem("ln_sq"), 1)
            act.wait_ge(sem("ln_v"), KD + 2)
            rstd(ps[:, 7, :], lnb[:, 0, :], lnb[:, 1, :], "ln", 1)
            act.preload_act_table(ACT.Silu)
            base = split_base("ln")
            for j in range(KD):
                act.wait_ge(sem("ln_n"), j + 1)
                act.wait_ge(sem("sp_l"), base + j + 1)
                act.activation(tmp[:, j % 2, :], z2[:, GATE + j, :], ACT.Silu, scale=v("ln_g", j), bias=v("ln_b", j)
                               ).then_inc(sem("sp_t"), 1)
                act.wait_ge(sem("sp_t"), base + j + 1)
                act.activation(hh[:, j, :], tmp[:, j % 2, :], ACT.Copy).then_inc(sem("sp_h"), 1)
            ln_exp_tables()
            highs("co")

            act.wait_ge(sem("sw_vt"), 1)
            act.activation(vn_pairs, ps[:, 5, :].rearrange("p (a n) -> p a n", a=2), ACT.Copy
                           ).then_inc(sem("sw_v"), 1)

            def weights(j, r):
                c, n, st = swa_cols(r), j * STEPS + r, sstat[:, r % 2, :]
                act.wait_ge(sem("sw_m"), n + 1)
                for e in range(2):
                    act.activation(spr[:, r % 2, e, c:], ssc[:, r % 2, e, c:], ACT.Exp, bias=st[:, 2 + e:3 + e],
                                   accum_out=st[:, 6 + e:7 + e]).then_inc(sem("sw_e"), 1)
                act.wait_ge(sem("sw_d"), n + 1)
                act.activation(st[:, 8:10], st[:, 4:6], ACT.Exp).then_inc(sem("sw_e"), 1)

            def turned_weights(j, r):
                n, b = j * STEPS + r, swa_cols(r) // P
                act.wait_ge(sem("sw_t"), n + 1)
                act.wait_ge(sem("sw_o"), n + 1)
                act.activation(spt[:, r % 2, :, :].rearrange("p e (b n) -> p e b n", b=2)[:, :, b:, :],
                               ps[:, 2 + r % 2, :].rearrange("p (e b n) -> p e b n", e=2, b=2)[:, :, b:, :], ACT.Copy
                               ).then_inc(sem("sw_pt"), 1)

            def heads_out(j, kv):
                act.wait_ge(sem("sw_o"), j * STEPS + (kv * NT + NT + 2))
                act.activation(zt(z2, j + kv * PAIRS_PER_KV), ps[:, 4 + kv, :], ACT.Copy).then_inc(sem("sw_y"), 1)
                act.wait_ge(sem("sw_y"), j * 2 + (kv + 3))
                act.activation(zt(hh, j + kv * PAIRS_PER_KV), zt(z2, j + kv * PAIRS_PER_KV), ACT.Copy
                               ).then_inc(sem("sp_h"), 1)

            def halves_out(j, kv):
                if not (isinstance(j, int) and j == 0):
                    act.wait_ge(sem("rq"), j * 2 + (kv - 1))
                act.wait_ge(sem("rq_mm"), j * 2 + (kv + 1))
                act.activation(rt[:, kv, :], ps[:, 6 + kv, :], ACT.Copy).then_inc(sem("rh"), 1)

            def step(j, r, last):
                if not last and r % NT == 1:
                    halves_out(j + 1, r // NT)
                if not last or r + 1 < STEPS:
                    weights(*ahead(j, r, 1))
                turned_weights(j, r)
                if r == NT:
                    heads_out(j, 0)
                if r == STEPS - 1:
                    heads_out(j, 1)

            for kv in range(2):
                halves_out(0, kv)
            weights(0, 0)
            act.wait_ge(sem("w_used"), FIRST["ao"] + 2)
            all_steps(act, PAIRS_PER_KV, step)
            act.sem_inc(sem("sp_t"), KD)
            highs("ao")
            split_high("mg")
            highs_and_squares("out2", 3)
            norm(3, xT, "x_tile", 24, sqb, lnb, done=6)
            split_high("n3")

            def q_tile(n, bank):
                act.activation(zt(qT, n), ps[:, bank, :], ACT.Copy).then_inc(sem("ev_pq"), 1)

            evacuate("pq", 0, HC - 4, q_tile)
            evacuate("pq", HC - 4, HC, q_tile, ahead=False)
            def high_u(e, r):
                act.wait_ge(sem(f"u_in{r}"), e * 8 + (16 - 8 * r))
                act.wait_ge(sem("a_mm"), e + 1)
                act.activation(eh[:, r, :], er[:, r, :], ACT.Copy).then_inc(sem("u_hi"), 1)

            high_u(0, 0)
            high_u(1, 1)
            for n in range(NT * 4):
                act.wait_ge(sem("sc_mm"), n + 1)
                if n >= 4:
                    act.wait_ge(sem(f"sc_out{n % 4}"), 16 * (n // 4))
                act.activation(scev[:, n % 4, :, :], ps[:, 6 + n % 2, :].rearrange("p (a n) -> p a n", a=4), ACT.Copy
                               ).then_inc(sem("sc_copied"), 1)
            act.wait_ge(sem("late_free"), 1)

            for grp in range(GROUPS):
                e0 = grp * EG

                def gelu(e, r):
                    act.wait_ge(sem("a_mm"), e + (e0 + 1 + 2))
                    act.activation(zt(ga, e), ps[:, 4 + r, :], ACT.Gelu).then_inc(sem("a_ev"), 1)

                def high_v(e, r):
                    act.wait_ge(sem(f"v_in{r}"), e * 8 + (16 - 8 * r + 8 * e0))
                    act.wait_ge(sem("v_used"), e + (e0 + 1))
                    act.activation(eh[:, r, :], er[:, r, :], ACT.Copy).then_inc(sem("v_hi"), 1)
                    act.activation(gah[:, r, :], zt(ga, e), ACT.Copy).then_inc(sem("v_hi"), 1)

                act.preload_act_table(ACT.Gelu)
                if grp:
                    act.wait_ge(sem("v_used"), e0 + 2)
                    high_u(e0, 0)
                    high_u(e0 + 1, 1)
                    act.wait_ge(sem("e_spilled"), 16)

                def tile(e, r):
                    gelu(e, r)
                    high_u(e + (e0 + 2), r)

                rolled(act, EG - 2, 2, tile)
                if grp == 0:
                    act.wait_ge(sem("tk_unit"), 2 * NT + 1)
                    act.activation(sel[:, :, 2, :], sel[:, :, 2, :], ACT.Exp).then_inc(sem("gt_e"), 1)
                gelu(EG - 2, 0)
                if grp == 0:
                    for a, dst in enumerate((slot_t[:, 0, :], slot_t[:, 1, :], gate_t)):
                        act.wait_ge(sem("slot_mm"), a + 1)
                        act.activation(dst, ps[:, a, :], ACT.Copy).then_inc(sem("slot_t"), 1)
                    act.wait_ge(sem("slot_t"), 3)
                    act.activation(slot_t[:, 2, :], gate_t, ACT.Copy).then_inc(sem("slot_t"), 1)
                gelu(EG - 1, 1)

                def gated(n, r):
                    act.wait_ge(sem("oh1_eq"), n + (grp * (S // TB) + 1))
                    act.wait_ge(sem("g_mm"), n + (grp * (S // TB) + 1))
                    for t in range(TB_ACT):
                        act.activation(oh1[:, r, 0, :, t], eq1[:, r, :, t], ACT.Identity,
                                       scale=gate_t[:, bass.ds(n * TB + t, 1)]).then_inc(sem("oh1_1"), 1)

                rolled(act, S // TB, 4, gated)
                act.wait_ge(sem("g_mul"), (grp + 1) * (S // TB) + 4)
                rolled(act, EG, 2, high_v)
            norm(4, xf, "y_sum", 0, fsq, fln, bank=0)

        @block.tensor
        def _(pe):
            for name in ("w_used", "nm_mm", "gn_mm", "ln_v", "ch_o", "sw_o", "a_mm", "v_used"):
                pe.sem_inc(sem(name), 2)
            pe.sem_inc(sem("g_mm"), 4)

            def three(bank, whi, wlo, xhi, xlo, start, stop):
                nc.tensor.matmul(bank, whi, xhi, start=start, stop=False)
                nc.tensor.matmul(bank, whi, xlo, start=False, stop=False)
                return nc.tensor.matmul(bank, wlo, xhi, start=False, stop=stop)

            def mean_square(n, k, sq, bank=4):
                pe.wait_ge(sem("nm_sq"), 8 * n + k + 1)
                nc.tensor.matmul(ps[:, bank, :], mean, sq[:, k % 2, :], start=(k == 0), stop=(k == KD - 1)
                                 ).then_inc(sem("nm_mm"), 1)

            def norm(n, sq, bank=4):
                for k in range(KD):
                    mean_square(n, k, sq, bank)

            def slot_tiles(g, b, first_done, bank_free):
                pe.wait_ge(sem("w_lo"), g + 3)
                for half in range(2):
                    bank_free(half)
                    for k in range(KD):
                        last = three(ps[:, 2 * b + half, :], piece(wh, b, k, half), piece(wl, b, k, half),
                                     hh[:, k, :], hl[:, k, :], k == 0, k == KD - 1)
                    last.then_inc(sem("w_used" if half else first_done), 1)

            def first_slot(g, b, split, first_done, bank_free, order=range(KD)):
                pe.wait_ge(sem("w_lo"), g + 3)
                for half in range(2):
                    bank_free(half)
                for n, k in enumerate(order):
                    pe.wait_ge(sem("sp_l"), split_base(split) + n + 1 + 2)
                    for half in range(2):
                        last = three(ps[:, 2 * b + half, :], piece(wh, b, k, half), piece(wl, b, k, half),
                                     hh[:, k, :], hl[:, k, :], n == 0, n == KD - 1)
                        if n == KD - 1:
                            last.then_inc(sem("w_used" if half else first_done), 1)

            def gemm(name, split, freed=None, base=0, order=range(KD), then=None):
                g0 = FIRST[name]

                def bank_free(s, half):
                    pe.wait_ge(sem(freed or "ev_" + name), s * 2 + (half + 1 + base))

                first_slot(g0, g0 % 2, split, "mm_" + name, lambda half: bank_free(0, half), order)
                if then:
                    for s in range(1, COUNT[name]):
                        slot_tiles(g0 + s, (g0 + s) % 2, "mm_" + name, lambda half: bank_free(s, half))
                        then(s)
                    return
                rolled(pe, COUNT[name] - 1, 2, lambda s, r: slot_tiles(
                    s + (g0 + 1), (g0 + 1 + r) % 2, "mm_" + name, lambda half: bank_free(s + 1, half)))

            pe.wait_ge(sem("c_loaded"), 32)
            norm(0, sqb)
            gemm("in1", "n0")

            with pe.Fori(0, SB_PAIRS) as p:
                pe.wait_ge(sem("sb_staged"), p * 3 + 3)
                for t in range(NT):
                    last = nc.tensor.transpose(ps[:, 5, t * P:t * P + P], vts[:, t * P:t * P + P], ident)
                last.then_inc(sem("sb_vt"), 1)
                for e in range(2):
                    n = p * 8 + 4 * e
                    h = slice(HD * e, HD * e + HD)
                    if e:
                        pe.wait_ge(sem("sb_w0"), p * 8 + 4)
                    for b in reversed(range(NT)):
                        nc.tensor.matmul(ps[:, b, 0:S - b * P], kst[h, b * P:b * P + P], qst[h, b * P:S],
                                         start=True, stop=True).then_inc(sem("sb_z"), 1)
                    for q, b in enumerate(reversed(range(NT))):
                        pe.wait_ge(sem("sb_sp"), n + (q + 1))
                        last = nc.tensor.matmul(ps[:, b, 0:S - b * P], negtri, spl[:, b, 0:S - b * P], start=False,
                                                stop=(b == NT - 1), skip_group_check=True)
                        for c in range(b + 1, NT):
                            last = nc.tensor.matmul(ps[:, b, (c - b) * P:S - b * P], negone, spl[:, c, 0:S - c * P],
                                                    start=False, stop=(c == NT - 1), skip_group_check=True)
                        last.then_inc(sem("sb_cum"), 1)
                    pe.wait_ge(sem("sb_v"), p + 1)
                    pe.wait_ge(sem("sb_w"), n + 4)
                    if e == 0:
                        pe.wait_ge(sem("sb_y"), p + 1)
                    for b in range(NT):
                        last = nc.tensor.matmul(ps[h, 4, b * P:S], vst[:, b, h], ab[:, b, 0:S - b * P],
                                                start=(b == 0), stop=(b == NT - 1))
                    last.then_inc(sem("sb_pv"), 1)

            def mean_squares(p):
                for w in range(2):
                    pe.wait_ge(sem("ch_sq"), p * 2 + (w + 1))
                    if not (isinstance(p, int) and p == 0):
                        pe.wait_ge(sem("ch_rs"), p * 2 + (w - 1))
                    nc.tensor.matmul(ps[:, 6 + w, :], blk64, sqb[:, w, :], start=True, stop=True
                                     ).then_inc(sem("ch_ms"), 1)

            def turn_values(p):
                pe.wait_ge(sem("ch_v"), p * 2 + 2)
                pe.wait_ge(sem("ch_vs"), p + 1)
                for t in range(NT):
                    last = nc.tensor.transpose(ps[:, 5, t * P:t * P + P], cvts[:, t * P:t * P + P], ident)
                last.then_inc(sem("ch_vt"), 1)

            def scores(p, r):
                e, i = r // NT, r % NT
                h = slice(HD * e, HD * e + HD)
                pe.wait_ge(sem("ch_qk"), p * 4 + (2 * e + 4))
                pe.wait_ge(sem("ch_s"), p * STEPS + (r + 1))
                nc.tensor.matmul(ps[:, r % 2, 0:(i + 1) * P], cqst[h, i * P:i * P + P], ckst[h, 0:(i + 1) * P],
                                 start=True, stop=True).then_inc(sem("ch_sc"), 1)

            def turn(p, r):
                pe.wait_ge(sem("ch_p"), p * STEPS + (r + 1))
                pe.wait_ge(sem("ch_pt"), p * STEPS + (r + 1))
                for b in range(r % NT + 1):
                    last = nc.tensor.transpose(ps[:, 2 + r % 2, b * P:b * P + P], cpr[:, r % 2, b * P:b * P + P],
                                               ident)
                last.then_inc(sem("ch_t"), 1)

            def values(p, r):
                e, i = r // NT, r % NT
                h = slice(HD * e, HD * e + HD)
                pe.wait_ge(sem("ch_pt"), p * STEPS + (r + 3))
                if i == 0:
                    pe.wait_ge(sem("ch_v"), p * 2 + (e + 3))
                    pe.wait_ge(sem("ch_y"), p * 2 + (e + 1))
                for b in range(i + 1):
                    last = nc.tensor.matmul(ps[h, 4, i * P:i * P + P], cvst[:, b, h],
                                            cpt[:, r % 2, b * P:b * P + P], start=(b == 0), stop=(b == i))
                last.then_inc(sem("ch_o"), 1)

            def step(p, r, last):
                if not last and r == 2:
                    mean_squares(p + 1)
                if not last and r == 3:
                    turn_values(p + 1)
                if not last or r + 3 < STEPS:
                    scores(*ahead(p, r, 3))
                values(p, r)
                if not last or r + 1 < STEPS:
                    turn(*ahead(p, r, 1))

            mean_squares(0)
            turn_values(0)
            for r in range(3):
                scores(0, r)
            turn(0, 0)
            all_steps(pe, CH_PAIRS, step)

            for j in range(KD):
                pe.wait_ge(sem("gn_sq"), j + 1)
                if j >= 2:
                    pe.wait_ge(sem("gn_ln"), j - 1)
                nc.tensor.matmul(ps[:, 4 + j % 2, :], blk64, sqb[:, j % 2, :], start=True, stop=True
                                 ).then_inc(sem("gn_mm"), 1)
            def gemm_and_norm(name, split, n):
                def tiles_before(s):
                    for k in (2 * s - 2, 2 * s - 1):
                        mean_square(n, k, sqb)

                gemm(name, split, "x_tile", 8 * n - 4, then=tiles_before)
                for k in (KD - 2, KD - 1):
                    mean_square(n, k, sqb)

            gemm_and_norm("out1", "gn", 1)

            g0 = FIRST["ffn"]
            first_slot(g0, 0, "n1", "mm_g", lambda half: pe.wait_ge(sem("ffn_g"), half + 1))
            slot_tiles(g0 + 1, 1, "mm_u", lambda half: pe.wait_ge(sem("ffn_u"), half + 1))
            with pe.Fori(1, FF_TILES // 2) as i:
                slot_tiles(i * 2 + g0, 0, "mm_g", lambda half: pe.wait_ge(sem("ffn_g"), i * 2 + (half + 1)))
                slot_tiles(i * 2 + (g0 + 1), 1, "mm_u", lambda half: pe.wait_ge(sem("ffn_u"), i * 2 + (half + 1)))
            g0 = FIRST["down"]
            pe.wait_ge(sem("ffn_u"), FF_TILES + 2)

            def down(s, b, start=False, stop=False):
                pe.wait_ge(sem("w_lo"), s + (g0 + 3))
                pe.wait_ge(sem("hid_l"), s * 2 + 4)
                for j in range(2):
                    for c in range(KD):
                        last = three(ps[:, c, :], piece_down(wh, b, j, c), piece_down(wl, b, j, c),
                                     zt(hidh, s * 2 + j), zt(hidl, s * 2 + j), start and j == 0, stop and j == 1)
                        if stop and j == 1 and c < KD - 1:
                            last.then_inc(sem("down_sum"), 1)
                last.then_inc(sem("w_used"), 1)

            down(0, g0 % 2, start=True)
            rolled(pe, COUNT["down"] - 2, 2, lambda s, r: down(s + 1, (g0 + 1 + r) % 2))
            down(COUNT["down"] - 1, (g0 + COUNT["down"] - 1) % 2, stop=True)
            norm(2, sqb, bank=0)
            gemm("in2", "n2")

            for j in range(KD):
                pe.wait_ge(sem("cv2_y"), j + 1)
                last = nc.tensor.matmul(ps[:, 6, :], mean, z2[:, GATE + j, :], start=(j == 0), stop=(j == KD - 1))
            last.then_inc(sem("ln_m"), 1)
            for j in range(KD):
                pe.wait_ge(sem("ln_sq"), j + 1)
                nc.tensor.matmul(ps[:, 7, :], mean, sqb[:, j % 2, :], start=(j == 0), stop=(j == KD - 1)
                                 ).then_inc(sem("ln_v"), 1)
            gemm("co", "ln")

            pe.wait_ge(sem("ev_in2"), Z2_TILES + 4)
            nc.tensor.matmul(ps[:, 6, :], rot, z2[:, K2, :], start=True, stop=True).then_inc(sem("rk_mm"), 1)
            for t in range(NT):
                last = nc.tensor.transpose(ps[:, 5, t * P:t * P + P], z2[:, V2, t * P:t * P + P], ident)
            last.then_inc(sem("sw_vt"), 1)
            pe.wait_ge(sem("kd"), 4)
            pe.wait_ge(sem("sw_v"), 1)
            def halves(j, kv):
                nc.tensor.matmul(ps[:, 6 + kv, :], rot, zt(z2, j + (Q2 + kv * PAIRS_PER_KV)), start=True, stop=True
                                 ).then_inc(sem("rq_mm"), 1)

            def scores(j, r, e):
                kv, i, c = r // NT, r % NT, swa_cols(r)
                h = slice(HD * e, HD * e + HD)
                if e:
                    pe.wait_ge(sem("sw_sc0"), j * STEPS + (r + 1))
                else:
                    pe.wait_ge(sem("rq"), j * 2 + (kv + 1))
                    pe.wait_ge(sem("sw_s"), j * STEPS + (r + 1))
                nc.tensor.matmul(ps[:, r % 2, 2 * P * e + c:2 * P * e + 2 * P], rq[h, kv, i * P:i * P + P],
                                 kdup[h, kv, (i - 1) * P + c:(i + 1) * P], start=True, stop=True
                                 ).then_inc(sem("sw_sc" if e else "sw_sc0"), 1)

            def turn(j, r):
                pe.wait_ge(sem("sw_p"), j * STEPS + (r + 1))
                pe.wait_ge(sem("sw_pt"), j * STEPS + (r + 1))
                for e in range(2):
                    for k in range(swa_cols(r), 2 * P, P):
                        last = nc.tensor.transpose(ps[:, 2 + r % 2, 2 * P * e + k:2 * P * e + k + P],
                                                   spr[:, r % 2, e, k:k + P], ident)
                last.then_inc(sem("sw_t"), 1)

            def values(j, r):
                kv, i, c = r // NT, r % NT, swa_cols(r)
                pe.wait_ge(sem("sw_pt"), j * STEPS + (r + 3))
                if i == 0:
                    pe.wait_ge(sem("sw_y"), j * 2 + (kv + 1))
                for e in range(2):
                    for k in range(c, 2 * P, P):
                        last = nc.tensor.matmul(ps[HD * e:HD * e + HD, 4 + kv, i * P:i * P + P],
                                                vn(i - 1 + k // P)[:, HD * kv:HD * kv + HD],
                                                spt[:, r % 2, e, k:k + P], start=(k == c), stop=(k == P))
                last.then_inc(sem("sw_o"), 1)

            def step(j, r, last):
                if not last and r % NT == 1:
                    halves(j + 1, r // NT)
                if not last or r + 3 < STEPS:
                    scores(*ahead(j, r, 3), 0)
                values(j, r)
                if not last or r + 3 < STEPS:
                    scores(*ahead(j, r, 3), 1)
                if not last or r + 1 < STEPS:
                    turn(*ahead(j, r, 1))

            for kv in range(2):
                halves(0, kv)
            for r in range(3):
                for e in range(2):
                    scores(0, r, e)
            turn(0, 0)
            all_steps(pe, PAIRS_PER_KV, step)
            gemm("ao", "at", order=[j + PAIRS_PER_KV * kv for j in range(PAIRS_PER_KV) for kv in range(2)])
            gemm_and_norm("out2", "mg", 3)
            gemm("pq", "n3")

            pe.wait_ge(sem("sk_loaded"), 16)
            pe.wait_ge(sem("ev_pq"), HC + 4)
            for n in range(NT * 4):
                t, c = n // 4, n % 4
                if n >= 2:
                    pe.wait_ge(sem("sc_copied"), n - 1)
                for a in range(4):
                    last = nc.tensor.matmul(ps[:, 6 + n % 2, a * P:a * P + P], qT[:, 4 * c + a, t * P:t * P + P],
                                            skT[:, 4 * c + a, :], start=True, stop=True)
                last.then_inc(sem("sc_mm"), 1)

            for grp in range(GROUPS):
                e0, n0 = grp * EG, grp * (S // TB)

                def dots(e, r):
                    pe.wait_ge(sem("u_lo"), e + (e0 + 3))
                    pe.wait_ge(sem("a_ev"), e + (e0 + 1))
                    for k in range(KD):
                        last = three(ps[:, 4 + r, :], eh[:, r, k * P:k * P + P], el[:, r, k * P:k * P + P],
                                     hh[:, k, :], hl[:, k, :], k == 0, k == KD - 1)
                    last.then_inc(sem("a_mm"), 1)

                def table(n, r):
                    pe.wait_ge(sem("oh1_1"), n * TB_ACT + (TB_ACT * n0 + TB_ACT))
                    pe.wait_ge(sem("oh1_2"), n * 2 + (2 * n0 + 2))
                    pe.wait_ge(sem("oh2"), n + (n0 + 1))
                    pe.wait_ge(sem("g_mul"), n + (n0 + 1))
                    for t in range(TB):
                        for a in range(2):
                            last = nc.tensor.matmul(ps[:, r, t * EG:t * EG + EG], oh2[:, r, :, t], oh1[:, r, a, :, t],
                                                    start=(a == 0), stop=(a == 1))
                    last.then_inc(sem("g_mm"), 1)

                def gather(e, r, start=False, stop=False):
                    pe.wait_ge(sem("v_lo"), e + (e0 + 3))
                    for c in range(KD):
                        last = three(ps[:, c, :], eh[:, r, c * P:c * P + P], el[:, r, c * P:c * P + P], gah[:, r, :],
                                     gal[:, r, :], start, stop)
                        if stop and c < KD - 1:
                            last.then_inc(sem("v_sum"), 1)
                    last.then_inc(sem("v_used"), 1)

                if grp:
                    pe.wait_ge(sem("e_part"), 6)
                if grp == 0:
                    rolled(pe, EG - 2, 2, dots)
                    dots(EG - 2, 0)
                    pe.wait_ge(sem("gt"), 1)
                    for a in range(3):
                        for t in range(NT):
                            last = nc.tensor.transpose(ps[:, a, t * P:t * P + P], sel[:, t, a, :], ident)
                        last.then_inc(sem("slot_mm"), 1)
                    dots(EG - 1, 1)
                    pe.wait_ge(sem("slot_t"), 3)
                else:
                    rolled(pe, EG, 2, dots)
                rolled(pe, S // TB, 4, table)
                gather(0, 0, start=True)
                rolled(pe, EG - 2, 2, lambda e, r: gather(e + 1, (1 + r) % 2))
                gather(EG - 1, 1, stop=True)
            norm(4, fsq, bank=0)
        @block.vector
        def _(dve):
            for name in ("in1", "in2", "co", "ao", "pq"):
                dve.sem_inc(sem("ev_" + name), 4)
            for name in ("ffn_u", "ffn_g", "ch_qk", "ch_v", "ch_y", "ch_s", "ch_pt", "sw_s", "sw_pt", "sw_y", "a_ev", "v_lo"):
                dve.sem_inc(sem(name), 2)
            dve.sem_inc(sem("g_mul"), 4)
            for name in ("sb_y", "ch_vt", "tk_unit"):
                dve.sem_inc(sem(name), 1)

            chained = 0

            def chain(ins):
                nonlocal chained
                chained += 1
                ins.then_inc(sem("step"), 1)
                dve.wait_ge(sem("step"), chained)

            def norm(n, gain, split):
                dve.wait_ge(sem("nm_rs"), n + 1)
                for k in range(KD):
                    dve.wait_ge(sem("sp_l"), split_base(split) + k + 1)
                    dve.scalar_tensor_tensor(tmp[:, k % 2, :], xT[:, k, :], v(gain, k), lnb[:, 1, :], ALU.mult, ALU.mult
                                             ).then_inc(sem("sp_t"), 1)

            def add_to_x(name):
                for n in range(KD):
                    tile_done(dve, name, n // 2, n % 2)
                    dve.tensor_tensor(xT[:, n, :], xT[:, n, :], ps[:, bank_of(name, n), :], ALU.add
                                      ).then_inc(sem("x_tile"), 1)

            for a in range(2):
                dve.wait_ge(sem(f"x_in{a}"), 16)
                dve.sem_inc(sem("x_tile"), 4)
            dve.wait_ge(sem("c_loaded"), 32)
            norm(0, "attn_norm", "n0")

            dve.wait_ge(sem("ev_in1"), Z1_TILES + 4)
            for c in range(CV_TILES):
                y, hc = yT[:, SB_PAIRS + CH_PAIRS + c, :], z1[:, GC + c, :]
                chain(dve.tensor_tensor(hc, hc, z1[:, XC + c, :], ALU.mult))
                chain(dve.tensor_scalar(y, hc, v("conv", 3 * c + 2), None, ALU.mult))
                for back in (1, 2):
                    chain(dve.scalar_tensor_tensor(y[:, back:S], hc[:, 0:S - back], v("conv", 3 * c + 2 - back),
                                                         y[:, back:S], ALU.mult, ALU.add))
                dve.tensor_tensor(y, y, z1[:, GB + c, :], ALU.mult).then_inc(sem("cv_y"), 1)

            with dve.Fori(0, SB_PAIRS) as p:
                dve.wait_ge(sem("sb_y"), p + 1)
                dve.tensor_copy(kst, zt(z1, p + KA)).then_inc(sem("sb_staged"), 1)
                dve.tensor_scalar(qst, zt(z1, p + QA), SCALE, None, ALU.mult).then_inc(sem("sb_staged"), 1)
                dve.tensor_copy(vts[:, :], zt(z1, p + VA)).then_inc(sem("sb_staged"), 1)
                for e in range(2):
                    for q, b in enumerate(reversed(range(NT))):
                        dve.wait_ge(sem("sb_l"), p * 8 + (4 * e + q + 1))
                        dve.scalar_tensor_tensor(spl[:, b, 0:S - b * P], ps[:, b, 0:S - b * P], 0.0,
                                                 ab[:, b, 0:S - b * P], ALU.max, ALU.add).then_inc(sem("sb_sp0"), 1)

            dve.wait_ge(sem("sb_y"), SB_PAIRS + 1)
            dve.wait_ge(sem("bt_ready"), 1)

            def normed(p, e):
                h = slice(HD * e, HD * e + HD)
                if not (isinstance(p, int) and p == 0):
                    dve.wait_ge(sem("ch_sc"), p * STEPS + (NT * e + NT - STEPS))
                for w, (src, dst, gain) in enumerate(((QB, cqst, "qn"), (KB, ckst, "kn"))):
                    dve.wait_ge(sem("ch_rs"), p * 2 + (w + 1))
                    dve.scalar_tensor_tensor(dst[h, :], zt(z1, p + src)[h, :], v(gain)[h, :], lnb[h, w, :], ALU.mult,
                                             ALU.mult).then_inc(sem("ch_qk"), 1)

            def shifted(p, r):
                e, i, n = r // NT, r % NT, p * STEPS + r
                w = (i + 1) * P
                bias = bt[:, bass.ds(p * 2 + e, 1), (3 - i) * P:S].rearrange("p a n -> p (a n)")
                dve.wait_ge(sem("ch_sc"), n + 1)
                dve.scalar_tensor_tensor(csc[:, r % 2, 0:w], ps[:, r % 2, 0:w], SCALE, bias, ALU.mult, ALU.add
                                         ).then_inc(sem("ch_s"), 1)
                dve.wait_ge(sem("ch_s"), n + 3)
                dve.tensor_reduce(cstat[:, r % 2, 0:1], csc[:, r % 2, 0:w], AX_X, ALU.max, negate=True
                                  ).then_inc(sem("ch_m"), 1)

            def divided(p, r):
                n, w = p * STEPS + r, (r % NT + 1) * P
                dve.wait_ge(sem("ch_e"), n + 1)
                dve.reciprocal(cstat[:, r % 2, 2:3], cstat[:, r % 2, 1:2]).then_inc(sem("ch_r"), 1)
                dve.wait_ge(sem("ch_r"), n + 1)
                dve.tensor_scalar(cpr[:, r % 2, 0:w], cpr[:, r % 2, 0:w], cstat[:, r % 2, 2:3], None, ALU.mult
                                  ).then_inc(sem("ch_p"), 1)

            def step(p, r, last):
                if not last or r + 2 < STEPS:
                    shifted(*ahead(p, r, 2))
                if not last or r + 1 < STEPS:
                    divided(*ahead(p, r, 1))
                if not last and r in (NT - 1, NT + 2):
                    normed(p + 1, (r - NT + 1) // 3)

            for e in range(2):
                normed(0, e)
            shifted(0, 0)
            shifted(0, 1)
            divided(0, 0)
            all_steps(dve, CH_PAIRS, step)

            for j in range(KD):
                dve.wait_ge(sem("gn_rs"), j + 1)
                dve.wait_ge(sem("sp_l"), split_base("gn") + j + 1)
                dve.scalar_tensor_tensor(tmp[:, j % 2, :], yT[:, j, :], v("out_norm", j), lnb[:, j % 2, :], ALU.mult,
                                         ALU.mult).then_inc(sem("sp_t"), 1)
            add_to_x("out1")
            norm(1, "ffn_norm", "n1")
            with dve.Fori(0, FF_TILES // 2) as i:
                for q in range(2):
                    if q:
                        dve.wait_ge(sem("w_used"), i * 2 + (FIRST["ffn"] + 4))
                    else:
                        dve.wait_ge(sem("mm_u"), i + 1)
                    dve.wait_ge(sem("ffn_g"), i * 2 + (q + 3))
                    dve.wait_ge(sem("hid_l"), i * 2 + (q + 1))
                    dve.tensor_tensor(hid[:, q, :], sg[:, q, :], ps[:, 2 + q, :], ALU.mult).then_inc(sem("ffn_u"), 1)
            for k in range(KD):
                if k < KD - 1:
                    dve.wait_ge(sem("down_sum"), k + 1)
                else:
                    dve.wait_ge(sem("w_used"), FIRST["in2"] + 2)
                dve.tensor_tensor(xT[:, k, :], xT[:, k, :], ps[:, k, :], ALU.add).then_inc(sem("x_tile"), 1)
            norm(2, "norm1", "n2")

            dve.wait_ge(sem("pos_loaded"), 16)
            two_pi = 2.0 * np.pi
            part1 = 6.28125
            part2 = float((np.array([two_pi - part1], np.float32).view(np.uint32) & np.uint32(0xFFFFF000))
                          .view(np.float32)[0])
            part3 = float(np.float32(two_pi - part1 - part2))
            to_whole = 1.5 * 2.0 ** 23
            limit = 3.1415925
            whole, angle = sqb[:, 0, :], sqb[:, 1, :]
            chain(dve.tensor_copy(angle, pos_i[:, :]))
            chain(dve.tensor_scalar(angle, angle, v("inv"), None, ALU.mult))
            for q, shift in ((0, np.pi / 2), (1, 0.0)):
                a = csin[:, q, :]
                chain(dve.tensor_scalar(whole, angle, 1.0 / two_pi, shift / two_pi, ALU.mult, ALU.add))
                chain(dve.tensor_scalar(whole, whole, to_whole, None, ALU.add))
                chain(dve.tensor_scalar(whole, whole, -to_whole, None, ALU.add))
                chain(dve.scalar_tensor_tensor(a, whole, -part1, angle, ALU.mult, ALU.add))
                chain(dve.scalar_tensor_tensor(a, whole, -part2, a, ALU.mult, ALU.add))
                chain(dve.scalar_tensor_tensor(a, whole, -part3, a, ALU.mult, ALU.add))
                chain(dve.tensor_scalar(a, a, float(shift), limit, ALU.add, ALU.min))
                chain(dve.tensor_scalar(a, a, -limit, None, ALU.max))
            dve.sem_inc(sem("rp_a"), 1)

            with dve.Fori(0, KD // 2) as i:
                dve.wait_ge(sem("ev_in2"), i * 2 + (GATE + 2 + 4))
                steps = TAPS + 1
                for q in range(2):
                    j = i * 2 + q
                    dve.tensor_tensor(zt(z2, j), zt(z2, j), zt(z2, j + GATE), ALU.mult).then_inc(sem(f"cv2_{q}"), 1)
                for back in range(TAPS):
                    for q in range(2):
                        j = i * 2 + q
                        w = vd("conv2", j * TAPS + (TAPS - 1 - back))
                        acc, u = zt(z2, j + GATE), zt(z2, j)
                        dve.wait_ge(sem(f"cv2_{q}"), i * steps + (back + 1))
                        if back == 0:
                            dve.tensor_scalar(acc, u, w, vd("conv2_b", j), ALU.mult, ALU.add
                                              ).then_inc(sem(f"cv2_{q}"), 1)
                        else:
                            dve.scalar_tensor_tensor(acc[:, back:S], u[:, 0:S - back], w, acc[:, back:S],
                                                     ALU.mult, ALU.add).then_inc(sem(f"cv2_{q}"), 1)
                for q in range(2):
                    dve.wait_ge(sem(f"cv2_{q}"), i * steps + steps)
                    dve.sem_inc(sem("cv2_y"), 1)

            dve.wait_ge(sem("ln_m"), 1)
            for j in range(KD):
                dve.tensor_tensor(z2[:, GATE + j, :], z2[:, GATE + j, :], ps[:, 6, :], ALU.subtract
                                  ).then_inc(sem("ln_x"), 1)
            dve.wait_ge(sem("ln_rs"), 1)
            for j in range(KD):
                dve.wait_ge(sem("ln_sq"), j + 1)
                dve.tensor_tensor(z2[:, GATE + j, :], z2[:, GATE + j, :], lnb[:, 1, :], ALU.mult
                                  ).then_inc(sem("ln_n"), 1)

            for n in range(KD):
                tile_done(dve, "co", n // 2, n % 2)
                dve.tensor_tensor(z2[:, GCONV + n, :], z2[:, GCONV + n, :], ps[:, bank_of("co", n), :], ALU.mult
                                  ).then_inc(sem("ev_co"), 1)

            dve.wait_ge(sem("rp_s"), 1)
            dve.wait_ge(sem("rk_mm"), 1)
            chain(dve.tensor_tensor(rq[:, 0, :], z2[:, K2, :], csin[:, 0, :], ALU.mult))
            chain(dve.tensor_tensor(rt[:, 0, :], ps[:, 6, :], csin[:, 1, :], ALU.mult))
            chain(dve.tensor_tensor(rq[:, 0, :], rq[:, 0, :], rt[:, 0, :], ALU.add))
            chain(dve.tensor_scalar(nsink[:, :], v("sinks", 0, 2 * SWA_PAIRS), -1.0, None, ALU.mult))
            for kv in range(2):
                for e in range(2):
                    dve.tensor_copy(kdup[HD * e:HD * e + HD, kv, :], rq[HD * kv:HD * kv + HD, 0, :]
                                    ).then_inc(sem("kd"), 1)
            dve.wait_ge(sem("kd"), 4)
            dve.wait_ge(sem("msk"), 3)
            def shifted(j, r):
                c, n, st = swa_cols(r), j * STEPS + r, sstat[:, r % 2, :]
                sink = nsink[:, bass.ds(j * 2 + 2 * PAIRS_PER_KV * (r // NT), 2)]
                sc2 = ps[:, r % 2, :].rearrange("p (e n) -> p e n", e=2)
                dve.wait_ge(sem("sw_sc"), n + 1)
                dve.scalar_tensor_tensor(ssc[:, r % 2, :, c:], sc2[:, :, c:], SCALE,
                                         msk[:, c:].unsqueeze(1).to_broadcast([P, 2, 2 * P - c]), ALU.mult, ALU.add
                                         ).then_inc(sem("sw_s"), 1)
                dve.wait_ge(sem("sw_s"), n + 3)
                dve.tensor_reduce(st[:, 0:2], ssc[:, r % 2, :, c:], AX_X, ALU.max, negate=True
                                  ).then_inc(sem("sw_x"), 1)
                dve.wait_ge(sem("sw_x"), n + 1)
                dve.tensor_tensor(st[:, 2:4], st[:, 0:2], sink, ALU.min).then_inc(sem("sw_m"), 1)
                dve.wait_ge(sem("sw_m"), n + 1)
                dve.tensor_tensor(st[:, 4:6], st[:, 2:4], sink, ALU.subtract).then_inc(sem("sw_d"), 1)

            def divided(j, r):
                c, n, st = swa_cols(r), j * STEPS + r, sstat[:, r % 2, :]
                p = spr[:, r % 2, :, c:]
                dve.wait_ge(sem("sw_e"), n * 3 + 3)
                dve.tensor_tensor(st[:, 10:12], st[:, 6:8], st[:, 8:10], ALU.add).then_inc(sem("sw_r"), 1)
                dve.wait_ge(sem("sw_r"), n * 2 + 1)
                dve.reciprocal(st[:, 12:14], st[:, 10:12]).then_inc(sem("sw_r"), 1)
                dve.wait_ge(sem("sw_r"), n * 2 + 2)
                dve.tensor_tensor(p, p, st[:, 12:14].unsqueeze(2).to_broadcast([P, 2, 2 * P - c]), ALU.mult
                                  ).then_inc(sem("sw_p"), 1)

            def step(j, r, last):
                if not last or r + 2 < STEPS:
                    shifted(*ahead(j, r, 2))
                if not last or r + 1 < STEPS:
                    divided(*ahead(j, r, 1))

            shifted(0, 0)
            shifted(0, 1)
            divided(0, 0)
            all_steps(dve, PAIRS_PER_KV, step)

            for n in range(KD):
                tile_done(dve, "ao", n // 2, n % 2)
                dve.tensor_tensor(z2[:, GATTN + n, :], z2[:, GATTN + n, :], ps[:, bank_of("ao", n), :], ALU.mult
                                  ).then_inc(sem("ev_ao"), 1)
            dve.wait_ge(sem("w_used"), FIRST["out2"] + 2)
            for n in range(KD):
                dve.wait_ge(sem("ev_ao"), 4 + n + 1)
                dve.wait_ge(sem("sp_l"), split_base("mg") + n + 1)
                dve.tensor_tensor(tmp[:, n % 2, :], z2[:, GATTN + n, :], z2[:, GCONV + n, :], ALU.add
                                  ).then_inc(sem("sp_t"), 1)
            add_to_x("out2")
            norm(3, "norm2", "n3")

            flat = sc[:, :, :].rearrange("p a n -> p (a n)")
            cand = flat.rearrange("p (h c) -> p h c", h=4)
            cand4 = flat.rearrange("p (h i j) -> p h i j", h=4, i=TOPK)
            pairs = top[:, :, :].rearrange("p (h c) k -> p h c k", c=2)
            keys = topf[:, :, :].rearrange("p (h c) k -> p h c k", c=2)
            grid = [P, 4, TOPK, TOPK]

            def unit(t, half, count):
                steps = 0

                def step(ins):
                    nonlocal steps
                    steps += 1
                    ins.then_inc(sem("tk"), 1)

                def settle():
                    pass_by(dve, "tk", count + steps)

                def sixteen(rows, vals, idx, n):
                    for a in range(n):
                        step(dve.max(out=vals[:, a, 0:8], in_=rows[:, a, :]))
                    settle()
                    for a in range(n):
                        step(dve.max_index(idx[:, a, 0:8], vals[:, a, 0:8], rows[:, a, :]))
                    settle()
                    for a in range(n):
                        step(dve.match_replace(out=rows[:, a, :], in_to_replace=vals[:, a, 0:8],
                                               in_values=rows[:, a, :], imm_value=-3.0e38))
                    settle()
                    for a in range(n):
                        step(dve.max(out=vals[:, a, 8:16], in_=rows[:, a, :]))
                    settle()
                    for a in range(n):
                        step(dve.max_index(idx[:, a, 8:16], vals[:, a, 8:16], rows[:, a, :]))
                    settle()

                pass_by(dve, "sc_in", t * 32 + (16 * half + 16))
                sixteen(sc, top, topi, 8)
                step(dve.tensor_copy(topf[:, :, :], topi[:, :, :]))
                step(dve.tensor_tensor(cand4, pairs[:, :, 0, :].unsqueeze(3).to_broadcast(grid),
                                       pairs[:, :, 1, :].unsqueeze(2).to_broadcast(grid), ALU.add))
                settle()
                sixteen(cand, best, bpos, 4)
                where = bpos[:, :, :].rearrange("p h k -> p (h k)")
                step(dve.tensor_scalar(bab[:, 0, :], where, 4, None, ALU.logical_shift_right))
                step(dve.tensor_scalar(bab[:, 1, :], where, TOPK - 1, None, ALU.bitwise_and))
                settle()
                step(dve.tensor_copy(bfl[:, :, :], bab[:, :, :]))
                settle()
                chosen = sel[:, bass.ds(t, 1), :, half * 4 * TOPK:(half + 1) * 4 * TOPK].rearrange(
                    "p t a s -> p (t a) s")
                for c in range(2):
                    at = bfl[:, c, :].rearrange("p (h k) -> p h k", h=4)
                    step(dve.tensor_tensor(cand4, at.unsqueeze(3).to_broadcast(grid),
                                           iota[:, 0:TOPK].unsqueeze(1).unsqueeze(1).to_broadcast(grid),
                                           ALU.is_equal))
                    settle()
                    step(dve.tensor_tensor(cand4, cand4, keys[:, :, c, :].unsqueeze(2).to_broadcast(grid), ALU.mult))
                    settle()
                    step(dve.tensor_reduce(chosen[:, c, :], flat.rearrange("p (s j) -> p s j", j=TOPK), AX_X, ALU.add))
                    settle()
                step(dve.tensor_tensor(chosen[:, 2, :].rearrange("p (h k) -> p h k", h=4), best[:, :, :],
                                       best[:, :, 0:1].to_broadcast([P, 4, TOPK]), ALU.subtract))
                settle()
                dve.sem_inc(sem("tk_unit"), 1)
                return steps

            UNIT_STEPS = 5 * 8 + 2 + 5 * 4 + 3 + 6 + 1
            with dve.Fori(0, NT) as t:
                for half in range(2):
                    n = unit(t, half, t * (2 * UNIT_STEPS) + half * UNIT_STEPS)
                    assert n == UNIT_STEPS
            dve.wait_ge(sem("gt_e"), 1)
            gates = sel[:, :, 2, :].rearrange("p t (h k) -> p t h k", k=TOPK)
            sums = den[:, 0, :].rearrange("p (t h) -> p t h", t=NT)
            rec = den[:, 1, :].rearrange("p (t h) -> p t h", t=NT)
            chain(dve.tensor_reduce(sums, gates, AX_X, ALU.add))
            chain(dve.reciprocal(rec, sums))
            chain(dve.tensor_scalar(rec, rec, GATE_SCALE, None, ALU.mult))
            dve.tensor_tensor(gates, gates, rec.unsqueeze(3).to_broadcast([P, NT, PH, TOPK]), ALU.mult
                              ).then_inc(sem("gt"), 1)

            for grp in range(GROUPS):
                e0, n0 = grp * EG, grp * (S // TB)

                def hot(n, r):
                    def tokens(a, keys):
                        return slot_t[:, a, bass.ds(n * TB, TB)].unsqueeze(1).to_broadcast([P, keys, TB])

                    dve.wait_ge(sem("g_mm"), n + (n0 + 1))
                    dve.tensor_tensor(eq1[:, r, :, :], iota_t[:, e0:e0 + EG, :], tokens(0, EG), ALU.is_equal
                                      ).then_inc(sem("oh1_eq"), 1)
                    dve.tensor_tensor(oh2[:, r, :, :], iota_t[:, :, :], tokens(1, NKEYS), ALU.is_equal
                                      ).then_inc(sem("oh2"), 1)

                def weigh(n, r):
                    dve.wait_ge(sem("g_mm"), n + (n0 + 1 + 4))
                    at = ga[:, :, bass.ds(n * TB, TB)]
                    dve.scalar_tensor_tensor(at, ps[:, r, :].rearrange("p (t e) -> p e t", t=TB), 1.0 / GATE_SCALE, at,
                                             ALU.mult, ALU.mult).then_inc(sem("g_mul"), 1)

                def low_v(e, r):
                    dve.wait_ge(sem("v_hi"), e * 2 + (2 * e0 + 2))
                    dve.tensor_tensor(gal[:, r, :], zt(ga, e), gah[:, r, :].bitcast(F32), ALU.subtract
                                      ).then_inc(sem("ga_lo"), 1)
                    dve.tensor_tensor(el[:, r, :], er[:, r, :], eh[:, r, :].bitcast(F32), ALU.subtract
                                      ).then_inc(sem("v_lo"), 1)

                if grp == 0:
                    dve.wait_ge(sem("slot_t"), 4)
                    dve.tensor_tensor(slot_t[:, 3, :], gate_t, slot_t[:, 2, :], ALU.subtract).then_inc(sem("gate_p"), 1)
                    dve.tensor_copy(iota_t[:, :, :], iota.unsqueeze(2).to_broadcast([P, NKEYS, TB])
                                    ).then_inc(sem("iota_t"), 1)
                    dve.wait_ge(sem("gate_p"), 1)
                    dve.wait_ge(sem("iota_t"), 1)
                dve.wait_ge(sem("a_mm"), e0 + EG + 2)
                dve.wait_ge(sem("a_ev"), e0 + EG + 2)
                hot(0, 0)
                hot(1, 1)
                with dve.Fori(0, S // TB // 4 - 1) as i:
                    for r in range(4):
                        hot(i * 4 + (r + 2), (r + 2) % 4)
                        weigh(i * 4 + r, r)
                n = S // TB
                hot(n - 2, 2)
                weigh(n - 4, 0)
                hot(n - 1, 3)
                for r in range(1, 4):
                    weigh(n - 4 + r, r)
                rolled(dve, EG, 2, low_v)

                def sum_done(c):
                    if c < KD - 1:
                        dve.wait_ge(sem("v_sum"), grp * (KD - 1) + c + 1)
                    else:
                        dve.wait_ge(sem("v_used"), e0 + EG + 2)

                if grp == 0:
                    for c in range(KD):
                        sum_done(c)
                        dve.tensor_copy(ga[:, c, :], ps[:, c, :]).then_inc(sem("e_part"), 1)
                else:
                    dve.wait_ge(sem("x_back"), 32)
                    for c in range(KD):
                        dve.tensor_tensor(xf[:, c, :], xf[:, c, :], pf[:, c, :], ALU.add).then_inc(sem("y_part"), 1)
                    for c in range(KD):
                        sum_done(c)
                        dve.wait_ge(sem("y_part"), c + 1)
                        dve.tensor_tensor(xf[:, c, :], xf[:, c, :], ps[:, c, :], ALU.add).then_inc(sem("y_sum"), 1)
            dve.wait_ge(sem("nm_rs"), 5)
            for k in range(KD):
                dve.scalar_tensor_tensor(pf[:, k, :], xf[:, k, :], v("final", k), fln[:, 1, :], ALU.mult, ALU.mult
                                         ).then_inc(sem("y_t"), 1)


def constants():
    i = np.arange(P)
    same64 = (i[:, None] // HD == i[None, :] // HD).astype(np.float32)
    half = HD // 2
    turn = np.zeros((P, P), np.float32)
    for m in range(P):
        if m % HD < half:
            turn[m + half, m] = -1.0
        else:
            turn[m - half, m] = 1.0
    tables = {
        "ident": np.eye(P, dtype=np.float32),
        "blk64": same64 / HD,
        "mean": np.full((P, P), 1.0 / D, np.float32),
        "negtri": -(i[:, None] >= i[None, :]).astype(np.float32),
        "negone": np.full((P, P), -1.0, np.float32),
        "rot": turn,
        "iota": np.broadcast_to(i.astype(np.float32)[None, :], (P, P)),
    }
    return np.ascontiguousarray(np.stack([tables[n] for n in CST], axis=1).astype(np.float32))


def kernel(**inputs):
    import concourse.bacc as bacc
    from concourse.bass_utils import run_bass_kernel_spmd

    a = {k: np.asarray(x) for k, x in inputs.items()}

    def cols(x):
        return x.reshape(-1, P).T

    half = HD // 2
    inv = 10000.0 ** (-(np.arange(half, dtype=np.float32) * np.float32(2.0) / np.float32(HD)))
    packed = {
        "attn_norm": cols(a["attn_norm_w"][0]), "ffn_norm": cols(a["ffn_norm_w"][0]), "norm1": cols(a["norm1_g_2"][0]),
        "norm2": cols(a["norm2_g_2"][0]), "final": cols(a["final_g_2"]), "out_norm": cols(a["out_norm_w"][0]),
        "qn": np.tile(a["q_norm_w"][0], 2)[:, None], "kn": np.tile(a["k_norm_w"][0], 2)[:, None],
        "conv": a["conv_w"][0].reshape(3, CV_TILES, P).transpose(2, 1, 0).reshape(P, -1),
        "b_in": cols(a["b_in_2"][0]),
        "conv2": a["conv_w_2"][0].reshape(TAPS, KD, P).transpose(2, 1, 0).reshape(P, -1),
        "conv2_b": cols(a["conv_b_2"][0]), "ln_g": cols(a["conv_ln_g_2"][0]), "ln_b": cols(a["conv_ln_b_2"][0]),
        "sinks": np.tile(a["attn_sinks_2"], (P, 1)),
        "inv": np.tile(inv.astype(np.float32), P // half)[:, None],
        "eps": np.full((P, 1), EPS, np.float32), "one": np.ones((P, 1), np.float32),
    }
    vec = np.concatenate([packed[n] for n, _ in VECS], axis=1)
    assert vec.shape == (P, NVEC)
    far = np.clip(S - P + np.arange(P)[:, None] - np.arange(S)[None, :], -P, P) + P

    def by_cols(w):
        return w.reshape(KD, P, -1, 256).transpose(2, 1, 0, 3).reshape(-1, P, 2048)

    gate_up = np.stack([by_cols(a["w_gate"][0]), by_cols(a["w_up"][0])], axis=1).reshape(-1, P, 2048)
    down = a["w_down"][0].reshape(-1, 2, P, D).transpose(0, 2, 1, 3).reshape(-1, P, 2048)
    slots = [by_cols(a["w_in"][0]), by_cols(a["w_out"][0]), gate_up, down, by_cols(a["w_in_2"][0]),
             by_cols(a["w_conv_out_2"][0]), by_cols(a["w_attn_o_2"][0]), by_cols(a["w_out_2"][0]),
             by_cols(a["w_peer_q_2"][0])]
    assert [x.shape[0] for x in slots] == [c for _, c in SLOTS]
    arrays = {
        "x": a["x"][0].reshape(S, KD, P).transpose(2, 1, 0), "cst": constants(), "vec": vec,
        "rel_tiles": a["rel_bias"][0][:, far], "positions": np.tile(a["positions_2"], (P, 1)),
        "w_slots": np.concatenate(slots),
        "sub_keys": a["peer_sub_keys_2"][0].reshape(HC, NKEYS, P).transpose(2, 0, 1),
        "u_tiles": a["peer_u_2"][0].reshape(NKEYS, P, KD, P).transpose(0, 3, 2, 1).reshape(NKEYS, P, D),
        "v_tiles": a["peer_v_2"][0].reshape(NKEYS, P, D),
    }
    arrays = {f"in_{n}": np.ascontiguousarray(x) for n, x in arrays.items()}

    nc = bacc.Bacc("TRN2", target_bir_lowering=False, num_devices=1)
    ins = {n[3:]: nc.dram_tensor(n, x.shape, mybir.dt.from_np(x.dtype), kind="ExternalInput").ap()
           for n, x in arrays.items()}
    out = nc.dram_tensor("out", (P, KD, S), F32, kind="ExternalOutput").ap()
    build(nc, ins, out)
    r = run_bass_kernel_spmd(nc, [arrays], core_ids=[0])
    return r.results[0]["out"].transpose(2, 1, 0).reshape(1, S, D)
```
